# Optimizing a Trainium2 kernel written in Bass

```python
import jax, jax.numpy as jnp
from jax import lax
import numpy as np

D_MODEL = 1024
BATCH = 1
SEQ = 256
DEPTH = 2

N_HEADS = 16
HEAD_DIM = 64
ATTN_DIM = N_HEADS * HEAD_DIM
ROT_DIM = HEAD_DIM // 4
ROPE_THETA = 500000.0
D_FF = 2816
FFN_RESIDUAL_WEIGHT = 0.5
N_A_LAYERS = DEPTH // 2
N_B_LAYERS = DEPTH - N_A_LAYERS
DILATION_PAIRS = ((128, 1), (512, 4), (2048, 16))
MOBA_BLOCK = 256
MOBA_TOPK = 3
MOBA_Q_CHUNK = 32
RMS_EPS = 1e-6


def rmsnorm(x, g):
    xf = x.astype(jnp.float32)
    y = xf * lax.rsqrt(jnp.mean(xf * xf, axis=-1, keepdims=True) + RMS_EPS)
    return (y * g.astype(jnp.float32)).astype(x.dtype)

def swiglu(h, w_gate, w_up, w_down):
    return (jax.nn.silu(h @ w_gate) * (h @ w_up)) @ w_down

def partial_rotary(t, pos):
    half = ROT_DIM // 2
    inv_freq = ROPE_THETA ** (-jnp.arange(half, dtype=jnp.float32) / half)
    ang = pos.astype(jnp.float32)[:, None] * inv_freq[None, :]
    cos, sin = jnp.cos(ang), jnp.sin(ang)
    tf = t.astype(jnp.float32)
    x1, x2 = tf[..., :half], tf[..., half:ROT_DIM]
    out = jnp.concatenate([x1 * cos - x2 * sin, x1 * sin + x2 * cos, tf[..., ROT_DIM:]], axis=-1)
    return out.astype(t.dtype)

def dilated_branch(q, k, v, window, dil):
    B, H, S, Dh = q.shape
    blk = window // dil
    span = blk * dil
    s_pad = -(-S // span) * span
    L = s_pad // dil
    nb = L // blk

    def to_sub(t):
        t = jnp.pad(t, ((0, 0), (0, 0), (0, s_pad - S), (0, 0)))
        t = t.reshape(B, H, L, dil, Dh).transpose(0, 1, 3, 2, 4)
        return t.reshape(B, H, dil, nb, blk, Dh)

    qs, ks, vs = to_sub(q), to_sub(k), to_sub(v)

    def with_prev(t):
        prev = jnp.pad(t, ((0, 0), (0, 0), (0, 0), (1, 0), (0, 0), (0, 0)))[:, :, :, :-1]
        return jnp.concatenate([prev, t], axis=4)

    kk, vv = with_prev(ks), with_prev(vs)
    s = jnp.einsum('bhrnqd,bhrnkd->bhrnqk', qs, kk).astype(jnp.float32) * (HEAD_DIM ** -0.5)
    qi = jnp.arange(blk)[:, None]
    kj = jnp.arange(2 * blk)[None, :]
    diff = blk + qi - kj
    band = (diff >= 0) & (diff <= blk)
    has_prev = (jnp.arange(nb)[:, None, None] > 0) | (kj[None] >= blk)
    mask = band[None] & has_prev
    s = jnp.where(mask, s, -jnp.inf)
    m = jnp.max(s, axis=-1, keepdims=True)
    p = jnp.exp(s - m)
    l = jnp.sum(p, axis=-1, keepdims=True)
    o = jnp.einsum('bhrnqk,bhrnkd->bhrnqd', (p / l).astype(v.dtype), vv)
    lse = m + jnp.log(l)

    def from_sub(t):
        X = t.shape[-1]
        t = t.reshape(B, H, dil, L, X).transpose(0, 1, 3, 2, 4).reshape(B, H, s_pad, X)
        return t[:, :, :S]

    return from_sub(o), from_sub(lse)[..., 0]

def mixer_a(h, w_qkv, w_o, pos):
    B, S, _ = h.shape
    qkv = (h @ w_qkv).reshape(B, S, 3, N_HEADS, HEAD_DIM).transpose(2, 0, 3, 1, 4)
    q, k, v = partial_rotary(qkv[0], pos), partial_rotary(qkv[1], pos), qkv[2]
    outs, lses = [], []
    for window, dil in DILATION_PAIRS:
        o_i, lse_i = dilated_branch(q, k, v, window, dil)
        outs.append(o_i)
        lses.append(lse_i)
    wts = jax.nn.softmax(jnp.stack(lses, axis=0), axis=0)
    o = jnp.sum(wts[..., None] * jnp.stack(outs, axis=0).astype(jnp.float32), axis=0).astype(h.dtype)
    return o.transpose(0, 2, 1, 3).reshape(B, S, ATTN_DIM) @ w_o

def shared_kv(h_stream, kv_norm, kv_w, pos):
    B, S, _ = h_stream.shape
    hn = rmsnorm(h_stream, kv_norm)
    kv = (hn @ kv_w).reshape(B, S, 2, N_HEADS, HEAD_DIM).transpose(2, 0, 3, 1, 4)
    k, v = partial_rotary(kv[0], pos), kv[1]
    s_pad = -(-S // MOBA_BLOCK) * MOBA_BLOCK
    pad = ((0, 0), (0, 0), (0, s_pad - S), (0, 0))
    k_pad, v_pad = jnp.pad(k, pad), jnp.pad(v, pad)
    nb = s_pad // MOBA_BLOCK
    k_mean = jnp.mean(k_pad.reshape(B, N_HEADS, nb, MOBA_BLOCK, HEAD_DIM).astype(jnp.float32), axis=3)
    return k_pad, v_pad, k_mean.astype(k.dtype)

def mixer_b(h, w_q, w_o, k_pad, v_pad, k_mean, pos):
    B, S, _ = h.shape
    q = (h @ w_q).reshape(B, S, N_HEADS, HEAD_DIM).transpose(0, 2, 1, 3)
    q = partial_rotary(q, pos)
    nb = k_mean.shape[2]
    ksel = min(MOBA_TOPK, nb)
    k_blocks = k_pad.reshape(B, N_HEADS, nb, MOBA_BLOCK, HEAD_DIM)
    v_blocks = v_pad.reshape(B, N_HEADS, nb, MOBA_BLOCK, HEAD_DIM)
    n_chunks = S // MOBA_Q_CHUNK
    q_chunks = q.reshape(B, N_HEADS, n_chunks, MOBA_Q_CHUNK, HEAD_DIM).transpose(2, 0, 1, 3, 4)
    gather = jax.vmap(jax.vmap(lambda blocks, idx: blocks[idx]))
    scale = HEAD_DIM ** -0.5

    def chunk_attend(args):
        c, qc = args
        t = c * MOBA_Q_CHUNK + jnp.arange(MOBA_Q_CHUNK)
        own = (c * MOBA_Q_CHUNK) // MOBA_BLOCK
        gate = jnp.einsum('bhqd,bhnd->bhqn', qc, k_mean).astype(jnp.float32)
        gate = jnp.where(jnp.arange(nb) < own, gate, -jnp.inf)
        _, sel = lax.top_k(gate, ksel)
        valid = sel < own
        k_s = gather(k_blocks, sel)
        v_s = gather(v_blocks, sel)
        s_sel = jnp.einsum('bhqd,bhqnkd->bhqnk', qc, k_s).astype(jnp.float32) * scale
        s_sel = jnp.where(valid[..., None], s_sel, -jnp.inf).reshape(B, N_HEADS, MOBA_Q_CHUNK, ksel * MOBA_BLOCK)
        k_o = lax.dynamic_slice_in_dim(k_pad, own * MOBA_BLOCK, MOBA_BLOCK, axis=2)
        v_o = lax.dynamic_slice_in_dim(v_pad, own * MOBA_BLOCK, MOBA_BLOCK, axis=2)
        s_own = jnp.einsum('bhqd,bhkd->bhqk', qc, k_o).astype(jnp.float32) * scale
        causal = (own * MOBA_BLOCK + jnp.arange(MOBA_BLOCK))[None, :] <= t[:, None]
        s_own = jnp.where(causal, s_own, -jnp.inf)
        p = jax.nn.softmax(jnp.concatenate([s_sel, s_own], axis=-1), axis=-1).astype(qc.dtype)
        p_sel = p[..., :ksel * MOBA_BLOCK].reshape(B, N_HEADS, MOBA_Q_CHUNK, ksel, MOBA_BLOCK)
        p_own = p[..., ksel * MOBA_BLOCK:]
        return (jnp.einsum('bhqnk,bhqnkd->bhqd', p_sel, v_s)
                + jnp.einsum('bhqk,bhkd->bhqd', p_own, v_o))

    out = lax.map(chunk_attend, (jnp.arange(n_chunks), q_chunks))
    out = out.transpose(1, 0, 3, 2, 4).reshape(B, S, ATTN_DIM)
    return out @ w_o

def first_inputs(seed: int = 0) -> dict:
    key = jax.random.key(seed)
    ks = jax.random.split(key, 18)
    f32 = jnp.float32

    def w(k, shape, fan_in):
        return jax.random.normal(k, shape, f32) * (fan_in ** -0.5)

    def gain(k, shape):
        return 1.0 + 0.02 * jax.random.normal(k, shape, f32)

    return {
        'x': jax.random.normal(ks[0], (BATCH, SEQ, D_MODEL), f32),
        'ffn1_norm': gain(ks[1], (DEPTH, D_MODEL)),
        'ffn1_w_gate': w(ks[2], (DEPTH, D_MODEL, D_FF), D_MODEL),
        'ffn1_w_up': w(ks[3], (DEPTH, D_MODEL, D_FF), D_MODEL),
        'ffn1_w_down': w(ks[4], (DEPTH, D_FF, D_MODEL), D_FF),
        'mix_norm': gain(ks[5], (DEPTH, D_MODEL)),
        'ffn2_norm': gain(ks[6], (DEPTH, D_MODEL)),
        'ffn2_w_gate': w(ks[7], (DEPTH, D_MODEL, D_FF), D_MODEL),
        'ffn2_w_up': w(ks[8], (DEPTH, D_MODEL, D_FF), D_MODEL),
        'ffn2_w_down': w(ks[9], (DEPTH, D_FF, D_MODEL), D_FF),
        'a_w_qkv': w(ks[10], (N_A_LAYERS, D_MODEL, 3 * ATTN_DIM), D_MODEL),
        'a_w_o': w(ks[11], (N_A_LAYERS, ATTN_DIM, D_MODEL), ATTN_DIM),
        'kv_norm': gain(ks[12], (D_MODEL,)),
        'kv_w': w(ks[13], (D_MODEL, 2 * ATTN_DIM), D_MODEL),
        'b_w_q': w(ks[14], (N_B_LAYERS, D_MODEL, ATTN_DIM), D_MODEL),
        'b_w_o': w(ks[15], (N_B_LAYERS, ATTN_DIM, D_MODEL), ATTN_DIM),
        'final_norm': gain(ks[16], (D_MODEL,)),
    }

def first_block(x, ffn1_norm, ffn1_w_gate, ffn1_w_up, ffn1_w_down, mix_norm,
              ffn2_norm, ffn2_w_gate, ffn2_w_up, ffn2_w_down, a_w_qkv, a_w_o,
              kv_norm, kv_w, b_w_q, b_w_o, final_norm):
    pos = jnp.arange(x.shape[1], dtype=jnp.int32)
    h = x
    shared = None
    for layer in range(DEPTH):
        h = h + FFN_RESIDUAL_WEIGHT * swiglu(rmsnorm(h, ffn1_norm[layer]),
                                             ffn1_w_gate[layer], ffn1_w_up[layer], ffn1_w_down[layer])
        hn = rmsnorm(h, mix_norm[layer])
        if layer < N_A_LAYERS:
            h = h + mixer_a(hn, a_w_qkv[layer], a_w_o[layer], pos)
        else:
            j = layer - N_A_LAYERS
            h = h + mixer_b(hn, b_w_q[j], b_w_o[j], shared[0], shared[1], shared[2], pos)
        h = h + FFN_RESIDUAL_WEIGHT * swiglu(rmsnorm(h, ffn2_norm[layer]),
                                             ffn2_w_gate[layer], ffn2_w_up[layer], ffn2_w_down[layer])
        if layer == N_A_LAYERS - 1:
            shared = shared_kv(h, kv_norm, kv_w, pos)
    return rmsnorm(h, final_norm)


N_HEADS_2 = D_MODEL // HEAD_DIM
N_A = max(1, DEPTH // 2)
N_B = DEPTH - N_A
DECAY_LORA = 64
AAA_LORA = 64
MV_LORA = 32
GATE_LORA = 160
N_GROUPS = 4
EXP_PER_GROUP = 8
N_EXPERTS = N_GROUPS * EXP_PER_GROUP
TOP_K = 2
D_EXPERT = 512
EXPERT_BLOCK = 128
Q_BLOCK = 128
DEEPNORM_ALPHA = (2 * DEPTH) ** 0.25
DEEPNORM_BETA = (8 * DEPTH) ** -0.25
LN_EPS = 1e-5
GN_EPS = 64e-5
QK_EPS = 1e-6


def layer_norm(x, g, b, eps=LN_EPS):
    xf = x.astype(jnp.float32)
    mu = xf.mean(-1, keepdims=True)
    var = jnp.square(xf - mu).mean(-1, keepdims=True)
    return ((xf - mu) * lax.rsqrt(var + eps)).astype(x.dtype) * g + b

def head_rms(t, g, eps=QK_EPS):
    tf = t.astype(jnp.float32)
    return (tf * lax.rsqrt(jnp.mean(tf * tf, -1, keepdims=True) + eps)).astype(t.dtype) * g

def wkv7_scan(r, w, k, v, a, b):
    B, S, H, N = r.shape

    def step(state, inp):
        r_t, w_t, k_t, v_t, a_t, b_t = inp
        sa = jnp.einsum('bhij,bhj->bhi', state, a_t)
        state = (state * w_t[:, :, None, :] + sa[..., None] * b_t[:, :, None, :]
                 + v_t[..., None] * k_t[:, :, None, :])
        return state, jnp.einsum('bhij,bhj->bhi', state, r_t)

    tm = lambda t: jnp.moveaxis(t, 1, 0)
    state0 = jnp.zeros((B, H, N, N), jnp.float32)
    _, y = lax.scan(step, state0, (tm(r), tm(w), tm(k), tm(v), tm(a), tm(b)))
    return jnp.moveaxis(y, 0, 1)

def rwkv7_time_mix(h, v_first, mu, w_rkv, w0, w1, w2, a0, a1, a2, g1, g2,
                   k_k, k_a, r_k, gn_g, gn_b, w_o, v_mix):
    B, S, D = h.shape
    f32 = jnp.float32
    xx = jnp.pad(h, ((0, 0), (1, 0), (0, 0)))[:, :-1] - h
    xr, xw, xk, xv, xa, xg = [h + xx * mu[i] for i in range(6)]
    r, k, v = jnp.einsum('nbsd,nde->nbse', jnp.stack([xr, xk, xv]), w_rkv)
    w_log = -jnp.exp((-jax.nn.softplus(-(w0 + jnp.tanh(xw @ w1) @ w2)) - 0.5).astype(f32))
    if v_mix is None:
        v_first = v
    else:
        v0, v1, v2 = v_mix
        v = v + (v_first - v) * jax.nn.sigmoid(v0 + (xv @ v1) @ v2)
    a = jax.nn.sigmoid(a0 + (xa @ a1) @ a2)
    g = jax.nn.sigmoid(xg @ g1) @ g2
    heads = lambda t: t.reshape(B, S, N_HEADS_2, HEAD_DIM).astype(f32)
    kk = heads(k * k_k)
    kk = kk / jnp.maximum(jnp.sqrt(jnp.sum(kk * kk, -1, keepdims=True)), 1e-12)
    k = k * (1 + (a - 1) * k_a)
    rh, kh, vh, ah = heads(r), heads(k), heads(v), heads(a)
    y = wkv7_scan(rh, jnp.exp(heads(w_log)), kh, vh, -kk, kk * ah)
    ym = y.mean(-1, keepdims=True)
    yv = jnp.square(y - ym).mean(-1, keepdims=True)
    y = ((y - ym) * lax.rsqrt(yv + GN_EPS)).reshape(B, S, D).astype(h.dtype) * gn_g + gn_b
    bonus = (jnp.sum(rh * kh * r_k, -1, keepdims=True) * vh).reshape(B, S, D).astype(h.dtype)
    return ((y + bonus) * g) @ w_o, v_first

def shared_kv_2(x, cs, ada_w, ada_b, w_kvf, b_f, k_norm):
    B, S, D = x.shape
    shift, scale = jnp.split(cs @ ada_w + ada_b, 2, axis=-1)
    hk = x * (1 + scale[:, None]) + shift[:, None]
    kvf = hk @ w_kvf
    k = head_rms(kvf[..., :D].reshape(B, S, N_HEADS_2, HEAD_DIM), k_norm)
    v = kvf[..., D:2 * D].reshape(B, S, N_HEADS_2, HEAD_DIM)
    log_f = jax.nn.log_sigmoid((kvf[..., 2 * D:] + b_f).astype(jnp.float32))
    fcum = jnp.cumsum(log_f, axis=1)
    return (k.transpose(0, 2, 1, 3), v.transpose(0, 2, 1, 3), fcum.transpose(0, 2, 1))

def forgetting_attention(q, k, v, fcum):
    S = q.shape[2]
    scale = HEAD_DIM ** -0.5
    outs = []
    for i in range(S // Q_BLOCK):
        lo, hi = i * Q_BLOCK, (i + 1) * Q_BLOCK
        logits = (jnp.einsum('bhqd,bhkd->bhqk', q[:, :, lo:hi], k[:, :, :hi]).astype(jnp.float32) * scale
                  + (fcum[:, :, lo:hi, None] - fcum[:, :, None, :hi]))
        causal = (lo + jnp.arange(Q_BLOCK))[:, None] >= jnp.arange(hi)[None, :]
        logits = jnp.where(causal, logits, -jnp.inf)
        p = jax.nn.softmax(logits, axis=-1).astype(v.dtype)
        outs.append(jnp.einsum('bhqk,bhkd->bhqd', p, v[:, :, :hi]))
    return jnp.concatenate(outs, axis=2)

def fox_layer(h, kv, w_qg, q_norm, w_o):
    B, S, D = h.shape
    k, v, fcum = kv
    qg = h @ w_qg
    q = head_rms(qg[..., :D].reshape(B, S, N_HEADS_2, HEAD_DIM), q_norm).transpose(0, 2, 1, 3)
    o = forgetting_attention(q, k, v, fcum).transpose(0, 2, 1, 3).reshape(B, S, D)
    return (o * jax.nn.sigmoid(qg[..., D:])) @ w_o

def grouped_experts(xf, expert_idx, gates, w_gate, w_up, w_down):
    T, D = xf.shape
    A = T * TOP_K
    n_blocks = -(-(A + N_EXPERTS * EXPERT_BLOCK) // EXPERT_BLOCK)
    n_slots = n_blocks * EXPERT_BLOCK
    flat_e = expert_idx.reshape(A)
    order = jnp.argsort(flat_e)
    sorted_e = flat_e[order]
    counts = jnp.bincount(flat_e, length=N_EXPERTS)
    padded = (counts + EXPERT_BLOCK - 1) // EXPERT_BLOCK * EXPERT_BLOCK
    pad_end = jnp.cumsum(padded)
    pad_start = pad_end - padded
    start = jnp.cumsum(counts) - counts
    dest_sorted = pad_start[sorted_e] + (jnp.arange(A) - start[sorted_e])
    dest = jnp.zeros((A,), jnp.int32).at[order].set(dest_sorted.astype(jnp.int32))
    slot_tok = jnp.zeros((n_slots,), jnp.int32).at[dest].set(jnp.arange(A, dtype=jnp.int32) // TOP_K)
    block_exp = jnp.minimum(jnp.searchsorted(pad_end, jnp.arange(n_blocks) * EXPERT_BLOCK, side='right'),
                            N_EXPERTS - 1)
    xs = xf[slot_tok].reshape(n_blocks, EXPERT_BLOCK, D)

    def one_block(args):
        xb, e = args
        hb = jax.nn.silu(xb @ w_gate[e]) * (xb @ w_up[e])
        return hb @ w_down[e]

    ys = lax.map(one_block, (xs, block_exp)).reshape(n_slots, D)
    y_assign = ys[dest].reshape(T, TOP_K, D)
    return jnp.einsum('tk,tkd->td', gates, y_assign)

def hier_moe(h, w_grp, b_grp, w_exp, b_exp, w_gate, w_up, w_down):
    B, S, D = h.shape
    T = B * S
    hf = h.reshape(T, D)
    p_grp = jax.nn.softmax((hf @ w_grp).astype(jnp.float32) + b_grp, axis=-1)
    g_sel = jnp.argmax(p_grp, axis=-1)
    p_g = jnp.take_along_axis(p_grp, g_sel[:, None], axis=-1)
    e_logits = ((hf @ w_exp).astype(jnp.float32) + b_exp).reshape(T, N_GROUPS, EXP_PER_GROUP)
    e_logits = jnp.take_along_axis(e_logits, g_sel[:, None, None], axis=1)[:, 0]
    top_p, top_i = lax.top_k(jax.nn.softmax(e_logits, axis=-1), TOP_K)
    gates = (p_g * top_p / jnp.sum(top_p, -1, keepdims=True)).astype(h.dtype)
    expert_idx = (g_sel[:, None] * EXP_PER_GROUP + top_i).astype(jnp.int32)
    return grouped_experts(hf, expert_idx, gates, w_gate, w_up, w_down).reshape(B, S, D)

def second_inputs(seed: int = 0) -> dict:
    key = jax.random.key(seed)
    ks = iter(jax.random.split(key, 64))
    nrm = lambda shape, s: jax.random.normal(next(ks), shape, jnp.float32) * s
    uni = lambda shape, lo, hi: jax.random.uniform(next(ks), shape, jnp.float32, lo, hi)
    D, H, N = D_MODEL, N_HEADS_2, HEAD_DIM
    s_in = D ** -0.5
    beta = DEEPNORM_BETA
    nv = N_A - 1
    return {
        'x': nrm((BATCH, SEQ, D), 1.0),
        'c': nrm((BATCH, D), 1.0),
        'ada_w': nrm((DEPTH, D, 6 * D), 0.1 * s_in),
        'ada_b': nrm((DEPTH, 6 * D), 0.01),
        'ln_g': 1.0 + nrm((DEPTH, 2, D), 0.02),
        'ln_b': nrm((DEPTH, 2, D), 0.02),
        'rw_mu': uni((N_A, 6, D), 0.0, 1.0),
        'rw_rkv': nrm((N_A, 3, D, D), s_in) * jnp.array([1.0, 1.0, beta], jnp.float32)[None, :, None, None],
        'rw_w0': uni((N_A, D), -6.0, -1.0),
        'rw_w1': nrm((N_A, D, DECAY_LORA), s_in),
        'rw_w2': nrm((N_A, DECAY_LORA, D), 0.1 * DECAY_LORA ** -0.5),
        'rw_a0': nrm((N_A, D), 0.1),
        'rw_a1': nrm((N_A, D, AAA_LORA), s_in),
        'rw_a2': nrm((N_A, AAA_LORA, D), 0.1 * AAA_LORA ** -0.5),
        'rw_g1': nrm((N_A, D, GATE_LORA), s_in),
        'rw_g2': nrm((N_A, GATE_LORA, D), GATE_LORA ** -0.5),
        'rw_kk': 0.85 + nrm((N_A, D), 0.02),
        'rw_ka': 1.0 + nrm((N_A, D), 0.02),
        'rw_rk': nrm((N_A, H, N), 0.1),
        'rw_gn_g': 1.0 + nrm((N_A, D), 0.02),
        'rw_gn_b': nrm((N_A, D), 0.02),
        'rw_wo': nrm((N_A, D, D), s_in * beta),
        'rw_v0': 1.0 + nrm((nv, D), 0.1),
        'rw_v1': nrm((nv, D, MV_LORA), s_in),
        'rw_v2': nrm((nv, MV_LORA, D), 0.1 * MV_LORA ** -0.5),
        'kv_ada_w': nrm((D, 2 * D), 0.1 * s_in),
        'kv_ada_b': nrm((2 * D,), 0.01),
        'kv_w': jnp.concatenate([nrm((D, D), s_in), nrm((D, D), s_in * beta), nrm((D, H), s_in)], axis=1),
        'kv_fb': uni((H,), 0.0, 5.0),
        'kv_knorm': 1.0 + nrm((N,), 0.02),
        'fx_wqg': nrm((N_B, D, 2 * D), s_in),
        'fx_qnorm': 1.0 + nrm((N_B, N), 0.02),
        'fx_wo': nrm((N_B, D, D), s_in * beta),
        'moe_wgrp': nrm((DEPTH, D, N_GROUPS), s_in),
        'moe_bgrp': nrm((DEPTH, N_GROUPS), 0.01),
        'moe_wexp': nrm((DEPTH, D, N_EXPERTS), s_in),
        'moe_bexp': nrm((DEPTH, N_EXPERTS), 0.01),
        'moe_wgate': nrm((DEPTH, N_EXPERTS, D, D_EXPERT), s_in),
        'moe_wup': nrm((DEPTH, N_EXPERTS, D, D_EXPERT), s_in),
        'moe_wdown': nrm((DEPTH, N_EXPERTS, D_EXPERT, D), D_EXPERT ** -0.5 * beta),
    }

def second_block(x, c, ada_w, ada_b, ln_g, ln_b, rw_mu, rw_rkv, rw_w0, rw_w1, rw_w2, rw_a0, rw_a1, rw_a2,
              rw_g1, rw_g2, rw_kk, rw_ka, rw_rk, rw_gn_g, rw_gn_b, rw_wo, rw_v0, rw_v1, rw_v2,
              kv_ada_w, kv_ada_b, kv_w, kv_fb, kv_knorm, fx_wqg, fx_qnorm, fx_wo,
              moe_wgrp, moe_bgrp, moe_wexp, moe_bexp, moe_wgate, moe_wup, moe_wdown):
    cs = jax.nn.silu(c)
    kv = None
    v_first = None
    for l in range(DEPTH):
        mod = cs @ ada_w[l] + ada_b[l]
        sh_m, sc_m, gt_m, sh_f, sc_f, gt_f = [m[:, None, :] for m in jnp.split(mod, 6, axis=-1)]
        h = x * (1 + sc_m) + sh_m
        if l < N_A:
            v_mix = None if l == 0 else (rw_v0[l - 1], rw_v1[l - 1], rw_v2[l - 1])
            y, v_first = rwkv7_time_mix(h, v_first, rw_mu[l], rw_rkv[l], rw_w0[l], rw_w1[l], rw_w2[l],
                                        rw_a0[l], rw_a1[l], rw_a2[l], rw_g1[l], rw_g2[l], rw_kk[l],
                                        rw_ka[l], rw_rk[l], rw_gn_g[l], rw_gn_b[l], rw_wo[l], v_mix)
        else:
            j = l - N_A
            y = fox_layer(h, kv, fx_wqg[j], fx_qnorm[j], fx_wo[j])
        x = layer_norm(DEEPNORM_ALPHA * x + (1 + gt_m) * y, ln_g[l, 0], ln_b[l, 0])
        h = x * (1 + sc_f) + sh_f
        y = hier_moe(h, moe_wgrp[l], moe_bgrp[l], moe_wexp[l], moe_bexp[l],
                     moe_wgate[l], moe_wup[l], moe_wdown[l])
        x = layer_norm(DEEPNORM_ALPHA * x + (1 + gt_f) * y, ln_g[l, 1], ln_b[l, 1])
        if l == N_A - 1:
            kv = shared_kv_2(x, cs, kv_ada_w, kv_ada_b, kv_w, kv_fb, kv_knorm)
    return x


def setup_inputs(seed=0):
    out = dict(first_inputs(seed))
    for name, value in second_inputs(seed + 1).items():
        if name != "x":
            out[name + "_2"] = value
    return out


def reference(
    x, ffn1_norm, ffn1_w_gate, ffn1_w_up, ffn1_w_down, mix_norm, ffn2_norm, ffn2_w_gate,
    ffn2_w_up, ffn2_w_down, a_w_qkv, a_w_o, kv_norm, kv_w, b_w_q, b_w_o, final_norm, c_2,
    ada_w_2, ada_b_2, ln_g_2, ln_b_2, rw_mu_2, rw_rkv_2, rw_w0_2, rw_w1_2, rw_w2_2, rw_a0_2,
    rw_a1_2, rw_a2_2, rw_g1_2, rw_g2_2, rw_kk_2, rw_ka_2, rw_rk_2, rw_gn_g_2, rw_gn_b_2,
    rw_wo_2, rw_v0_2, rw_v1_2, rw_v2_2, kv_ada_w_2, kv_ada_b_2, kv_w_2, kv_fb_2, kv_knorm_2,
    fx_wqg_2, fx_qnorm_2, fx_wo_2, moe_wgrp_2, moe_bgrp_2, moe_wexp_2, moe_bexp_2, moe_wgate_2,
    moe_wup_2, moe_wdown_2,
):
    x = first_block(
        x, ffn1_norm, ffn1_w_gate, ffn1_w_up, ffn1_w_down, mix_norm, ffn2_norm, ffn2_w_gate,
        ffn2_w_up, ffn2_w_down, a_w_qkv, a_w_o, kv_norm, kv_w, b_w_q, b_w_o, final_norm,
    )
    return second_block(
        x, c_2, ada_w_2, ada_b_2, ln_g_2, ln_b_2, rw_mu_2, rw_rkv_2, rw_w0_2, rw_w1_2, rw_w2_2,
        rw_a0_2, rw_a1_2, rw_a2_2, rw_g1_2, rw_g2_2, rw_kk_2, rw_ka_2, rw_rk_2, rw_gn_g_2,
        rw_gn_b_2, rw_wo_2, rw_v0_2, rw_v1_2, rw_v2_2, kv_ada_w_2, kv_ada_b_2, kv_w_2, kv_fb_2,
        kv_knorm_2, fx_wqg_2, fx_qnorm_2, fx_wo_2, moe_wgrp_2, moe_bgrp_2, moe_wexp_2,
        moe_bexp_2, moe_wgate_2, moe_wup_2, moe_wdown_2,
    )


_drawn_inputs = setup_inputs


def setup_inputs(seed=0):
    import zlib

    import numpy as np

    out = dict(_drawn_inputs(seed))
    spreads = {}
    factors = {'ffn1_norm': 2.936,
     'mix_norm': 4.013,
     'ffn2_norm': 3.53,
     'kv_norm': 5.969,
     'ada_b_2': 3.335,
     'rw_w1_2': 8.0,
     'rw_w2_2': 8.0,
     'rw_a0_2': 3.789,
     'rw_a1_2': 4.847,
     'rw_a2_2': 4.551,
     'rw_kk_2': 7.821,
     'rw_ka_2': 4.831,
     'rw_gn_g_2': 7.006,
     'rw_gn_b_2': 5.946,
     'kv_ada_w_2': 4.991,
     'kv_ada_b_2': 8.0,
     'kv_knorm_2': 8.0,
     'fx_qnorm_2': 8.0,
     'moe_bgrp_2': 5.873,
     'moe_bexp_2': 8.0}
    for name, (base, spread) in spreads.items():
        noise = np.random.default_rng([zlib.crc32(name.encode()), seed]).standard_normal(out[name].shape)
        drawn = base * np.exp(spread * noise) if base else spread * noise
        out[name] = __import__('jax').numpy.asarray(drawn.astype(out[name].dtype))
    for name, factor in factors.items():
        out[name] = (out[name] * factor).astype(out[name].dtype)
    return out
```

```python
from contextlib import ExitStack, contextmanager

import numpy as np

import concourse.bass as bass
from concourse import mybir

F32 = mybir.dt.float32
I32 = mybir.dt.int32
U32 = mybir.dt.uint32
ALU = mybir.AluOpType
ACT = mybir.ActivationFunctionType
AX = mybir.AxisListType

P = 128
SEQ, D = 256, 1024
TB = SEQ // P
KC = D // P
H, HD = 16, 64
DFF = 2816
SLAB = 256
NSLAB = DFF // SLAB
LAYERS = 2
R = 6
UNIT = 2048
BANK = 512
NEG = -1.0e30
RMS_EPS = 1e-6
LN_EPS = 1e-5
GN_EPS = 64e-5
QK_EPS = 1e-6
ALPHA = float((2 * 2) ** 0.25)
DECAY = float(np.exp(-0.5))

ROT = HD // 4
HALF = ROT // 2
THETA = 500000.0
DILATIONS = ((128, 1), (512, 4), (2048, 16))
CH = 64
SUB = 16
N_GRP, N_PER = 4, 8
N_EXP = N_GRP * N_PER
N_RT = N_GRP + N_EXP
D_EXP = 512
CAP = 64


def shape_constants():
    t = np.arange(SEQ)
    rel = t[:, None] - t[None, :]

    def halves(m):
        return m.reshape(TB, P, -1).transpose(1, 0, 2).reshape(P, -1)

    count = sum(((rel >= 0) & (rel <= w) & (rel % d == 0)).astype(np.float32) for w, d in DILATIONS)
    inv = np.float32(THETA) ** (-np.arange(HALF, dtype=np.float32) / np.float32(HALF))
    ang = t.astype(np.float32)[:, None] * inv[None, :].astype(np.float32)
    p = np.arange(P)
    row, col = p[:, None], p[None, :]
    chunk = row // CH == col // CH
    sub = row // SUB == col // SUB
    aug = p % 64
    c = {
        "ident": (row == col),
        "mask_causal": halves(np.where(rel >= 0, 0.0, NEG)),
        "mask_dilated": halves(np.where(count > 0, 0.0, NEG)),
        "count_dilated": halves(count),
        "cos": halves(np.cos(ang)), "sin": halves(np.sin(ang)),
        "sub_lower": sub & (row > col),
        "sub_upper": sub & (row < col),
        "off_lower": chunk & ~sub & (row > col),
        "chunk_upper": chunk & (row < col),
        "chunk_upto": chunk & (row <= col),
        "decay_upto": -np.exp(-0.5) * (chunk & (row <= col)),
        "decay_of": -np.exp(-0.5) * (row // CH == np.arange(2)[None, :]),
        "upto": halves(t[:, None] <= t[None, :]),
        "aug_sel": np.where(aug[:, None] % 32 == np.arange(H)[None, :], 8.0, 0.0),
        "aug_val": ((aug >= 32) & (aug < 48))[:, None],
        "aug_one": (aug < 16)[:, None],
        "slots": np.broadcast_to(np.arange(CAP)[None, :], (P, CAP)),
        "eight": np.broadcast_to(np.arange(8)[None, :], (P, 8)),
    }
    return {k: np.ascontiguousarray(np.asarray(v, np.float32)) for k, v in c.items()}


CONST = shape_constants()
CONST_AT, _n = {}, 0
for _name, _a in CONST.items():
    CONST_AT[_name] = (_n, _a.shape[1])
    _n += _a.shape[1]
NCONST = _n

GAINS = ["ffn1_0", "ffn1_1", "mix_0", "mix_1", "ffn2_0", "ffn2_1", "kv", "mu0", "mu1", "mu2", "mu3", "mu4", "mu5"]


RK_PE = ["ab", "abt", "k", "ny", "d2", "d2t", "d4", "d4t", "d8", "at", "b", "t16t", "t16", "f", "ft", "f2", "gt", "tt",
         "u0", "w1", "u_0", "z_0", "u_1", "z_1", "yb"]
RK_DVE = ["de", "dtm", "mk", "d2", "dti", "d4t", "d2i", "d8i", "d4ti", "at", "t16t", "f", "f2i", "fti", "tt", "w1",
          "u_0", "z_0", "u_1", "z_1", "yb"]
RK_ACT = ["ny", "d2t", "d4", "b", "t16", "ft", "gt", "u0"]


class Cursor:

    def __init__(self):
        self.pos, self.lots, self.i, self.per = 0, [0] * R, None, 0

    def take(self, dmas=1):
        slot = self.pos % R
        self.lots[slot] += 16 * dmas
        self.pos += 1
        if self.i is None:
            return slot, self.lots[slot], self.pos
        return slot, self.i * (16 * self.per // R) + self.lots[slot], self.i * self.per + self.pos

    @contextmanager
    def loop(self, eng, n, per):
        assert per % R == 0
        with eng.Fori(0, n) as i:
            self.i, self.per = i, per
            yield i
        self.i = None
        self.pos += (n - 1) * per
        self.lots = [x + (n - 1) * 16 * (per // R) for x in self.lots]


PROJ = [("qkv_a", 6, "act"), ("wo_a", 2, "dve"), ("kv_b", 4, "act"), ("q_b", 2, "act"), ("wo_b", 2, "dve"),
        ("mod_0", 4, "dve"), ("rwkv_r", 2, "act"), ("rwkv_k", 2, "act"), ("rwkv_v", 2, "act"),
        ("lora_w", 2, "dve"), ("lora_a", 2, "dve"), ("lora_g", 2, "act"),
        ("gate_m0", 2, "dve"), ("wo_r", 2, "dve"),
        ("mod_f0", 4, "dve"), ("gate_f0", 2, "dve"),
        ("mod_kv", 4, "dve"), ("kv_f", 4, "act"), ("forget", 1, "dve"),
        ("mod_1", 4, "dve"), ("qg_f", 4, "act"), ("gate_m1", 2, "dve"), ("wo_f", 2, "dve"),
        ("mod_f1", 4, "dve"), ("gate_f1", 2, "dve")]
PROJ_AT, PROJ_TAKES, PROJ_DONE, _b = {}, [], [], 0
_taken, _sums = {"act": 0, "dve": 0}, 0
for _name, _k, _eng in PROJ:
    PROJ_AT[_name] = _b
    _b += _k
    _halves = 1 if _name.startswith(("mod_", "gate_")) else TB
    for _ in range(_k):
        PROJ_DONE.append(_sums)
        _sums += _halves
        _taken[_eng] += _halves
        PROJ_TAKES.append((_eng, _taken[_eng]))

TRANS = ["ffn0", "mix_a", "q_a", "k_a", "ffn1", "kv", "k_b", "ffn2", "mix_b", "q_b", "ffn3",
         "mix_r", "y_r", "moe0", "kv_f", "k_f", "mix_f", "q_f", "g_f", "moe1"]
ROWS = ["final_norm", "sh_m0", "sc_m0", "w0", "a0", "k_k", "k_a", "r_k", "gn_g", "gn_b", "gt_m0", "ln_g0", "ln_b0",
        "sh_f0", "sc_f0", "gt_f0", "ln_g1", "ln_b1", "sh_kv", "sc_kv", "sh_m1", "sc_m1", "gt_m1", "ln_g2", "ln_b2",
        "sh_f1", "sc_f1", "gt_f1", "ln_g3", "ln_b3"]
NROW = 6
PAIRS = N_EXP // 2
PROJ_N = {n: k for n, k, _ in PROJ}
TRANS_AT = {n: i for i, n in enumerate(TRANS)}


def build(nc, A, out):
    ctx = ExitStack()
    with ctx:
        def sb(name, shape, dt=F32):
            return ctx.enter_context(nc.sbuf_tensor(name, shape, dt))

        def sem(name):
            return ctx.enter_context(nc.semaphore(name))

        ring = sb("ring", [P, R, UNIT])
        X = sb("X", [P, TB, D])
        xt = sb("xt", [P, KC, SEQ])
        const = sb("const", [P, NCONST])
        gains = sb("gains", [P, len(GAINS) * KC])
        B = [sb(f"B{i}", [P, TB, D]) for i in range(10)]
        small = sb("small", [P, 512])

        def cst(name, *shape):
            a, n = CONST_AT[name]
            v = const[:, a:a + n]
            if len(shape) == 2:
                v = v.rearrange("p (a b) -> p a b", a=shape[0])
            return v

        def gain(name, k):
            i = GAINS.index(name) * KC + k
            return gains[:, i:i + 1]

        ident = cst("ident")
        bank = [ctx.enter_context(nc.psum_tensor(f"bank{i}", [P, BANK], F32)) for i in range(8)]

        Xn = B[0]
        Q, K, V = B[1], B[2], B[3]
        QT = B[4][:].rearrange("p a (b c) -> p (a b) c", c=SEQ)
        KT = B[5][:].rearrange("p a (b c) -> p (a b) c", c=SEQ)
        OT = B[6][:].rearrange("p a (b c) -> p (a b) c", c=SEQ)
        work = B[7]
        ff_silu_t = [work[:, 0, 256 * i:256 * (i + 1)] for i in range(2)]
        ff_h_t = [work[:, 1, 256 * i:256 * (i + 1)] for i in range(4)]
        PR = [work[:, 0, 512 * i:512 * (i + 1)] for i in range(2)] + [work[:, 1, 0:512]]
        PT = [work[:, 1, 512:512 + 384], B[8][:, 0, 0:384]]

        def row_source(name):
            mods = ("sh_m", "sc_m", "gt_m", "sh_f", "sc_f", "gt_f")
            if name[:4] in mods:
                i = mods.index(name[:4])
                return A["ada_b_2"][int(name[4]), i * D:(i + 1) * D]
            if name[:4] in ("ln_g", "ln_b"):
                n = int(name[4])
                return A[name[:4] + "_2"][n // 2, n % 2, :]
            return {"final_norm": lambda: A["final_norm"], "w0": lambda: A["rw_w0_2"][0], "a0": lambda: A["rw_a0_2"][0],
                    "k_k": lambda: A["rw_kk_2"][0], "k_a": lambda: A["rw_ka_2"][0],
                    "r_k": lambda: A["rw_rk_2"][0].rearrange("h n -> (h n)"),
                    "gn_g": lambda: A["rw_gn_g_2"][0], "gn_b": lambda: A["rw_gn_b_2"][0],
                    "sh_kv": lambda: A["kv_ada_b_2"][0:D], "sc_kv": lambda: A["kv_ada_b_2"][D:2 * D]}[name]()

        rR, rK, rV, rG, rA, rS, rKK = B[1], B[2], B[3], B[4], B[5], B[6], B[0]
        def fm(b):
            return b[:].rearrange("p a (b c) -> p (a b) c", c=SEQ)
        xxT, xi = fm(B[7]), [fm(B[8]), fm(B[9])]
        rE = [B[7], B[8], B[9]]
        AR = fm(B[6]).rearrange("p r (x t) -> p r x t", x=2)
        BK = fm(B[7]).rearrange("p r (x t) -> p r x t", x=2)
        wkx = sb("wkx", [P, 7 * BANK])
        _tiles = [B[i][:, h, j * BANK:(j + 1) * BANK] for i in (8, 9) for h in range(TB) for j in range(2)] + \
                 [xt[:, 2 * i:2 * i + 2, :].rearrange("p a b -> p (a b)") for i in range(4)] + \
                 [wkx[:, BANK * i:BANK * (i + 1)] for i in range(7)]
        rk_t = [_tiles[0:9], _tiles[9:18]]
        rk_n = [_tiles[18][:, 0:256], _tiles[18][:, 256:512]]
        Z = sb("Z", [P, KC, HD])
        pct = sb("pct", [P, KC, 4])
        lo = sb("lo", [P, 1024])

        def tiny(i, n):
            return small_s[:, i:i + n]

        small_s = sb("small_s", [P, 256])
        cs = tiny(100, KC)
        hs_sum, hs_root, hs_inv, bonus = [tiny(112 + 32 * i, 32) for i in range(4)]
        rms_m, rms_r, rms_i = [[tiny(6 * i + 2 * j, 2) for i in range(2)] for j in range(3)]
        at_max, at_bias, at_sum, at_inv = [[tiny(16 + 8 * i + 2 * j, 2) for i in range(3)] for j in range(4)]
        bc = [sb(f"bc{i}", [P, D])[:] for i in range(NROW)]
        csb = sb("csb", [P, KC, P])

        Yacc = B[1]
        XeT = B[2][:, 0, :].rearrange("p (k s) -> p k s", k=KC)
        ye = B[2][:, 1, :]
        m_h, m_sg = B[3][:, 0, 0:BANK], B[3][:, 0, BANK:2 * BANK]
        m_hT = B[3][:, 1, 0:BANK]
        m_pack = B[3][:, 1, BANK:BANK + 256].rearrange("p (t s) -> p t s", t=TB)
        m_gate = B[3][:, 1, BANK + 256:2 * BANK].rearrange("p (t s) -> p t s", t=TB)
        m_gT = B[5][:, 0, 0:SEQ]
        _r, _at = B[4][:, 0, :], [0]

        def rt(n, *shape):
            v = _r[:, _at[0]:_at[0] + n]
            _at[0] += n
            return v.rearrange("p (a b) -> p a b", a=shape[0]) if shape else v

        rt_w, rt_b, rt_l = rt(KC * N_RT, KC), rt(N_RT), rt(TB * N_RT, TB)
        rt_g8, rt_gm, rt_ohg, rt_ex = rt(16, TB), rt(16, TB), rt(16, TB), rt(8, TB)
        rt_es, rt_em, rt_ge, rt_se, rt_t = rt(16, TB), rt(16, TB), rt(16, TB), rt(16, TB), rt(16, TB)
        rt_if, rt_sum, rt_nm, rt_e2, rt_w1 = rt(16, TB), rt(4), rt(4), rt(4), rt(4)
        rt_gate, rt_sel, rt_rank = rt(2 * N_EXP, TB), rt(2 * N_EXP, TB), rt(2 * N_EXP, TB)
        rt_cnt = rt(2)
        ov_flag = [sb(f"ov_flag{l}", [P, 1], I32) for l in range(LAYERS)]
        ov_h = m_h, m_sg
        ov_hT = m_hT, B[2][:, 0, 0:BANK]
        rt_idx = ctx.enter_context(nc.sbuf_tensor("rt_idx", [P, 16], U32))[:].rearrange("p (t n) -> p t n", t=TB)
        fQ, fK, fV, fG, fGT = B[1], B[2], B[3], B[0], fm(B[9])
        fx = B[8]
        aug_f, aug_r = fx[:, 1, 0:SEQ], fx[:, 1, SEQ:2 * SEQ]
        aug_tiles = [fx[:, 1, 512 + SEQ * i:512 + SEQ * (i + 1)] for i in range(2)]
        fx_ls = fx[:, 0, 512:736].rearrange("p (t n) -> p t n", t=TB)
        fx_w = fx[:, 0, 736:864].rearrange("p (k n) -> p k n", k=KC)
        fx_b, fx_kn, fx_qn = fx[:, 0, 864:880], fx[:, 0, 880:944], fx[:, 0, 944:1008]
        fx_z = [small[:, 32 * i:32 * (i + 1)].rearrange("p (t n) -> p t n", t=TB) for i in range(4)]

        def aug_l(h):
            return aug_tiles[h % 2]

        tr_source = {"y_r": B[1], "k_f": fK, "q_f": fQ, "g_f": fG, "q_a": Q, "k_a": K, "k_b": K, "q_b": Q}
        for name in TRANS:
            tr_source.setdefault(name, Xn)

        w_landed = [sem(f"w_landed{i}") for i in range(R)]
        w_free = sem("w_free")
        in_landed = sem("in_landed")
        row_landed = [sem(f"row_landed{i}") for i in range(NROW)]
        row_free = [sem(f"row_free{i}") for i in range(NROW)]
        cs_set = sem("cs_set")
        dve_chain = sem("dve_chain")
        act_chain = sem("act_chain")
        rms_ms = sem("rms_ms")
        rms_root = sem("rms_root")
        tr_src = sem("tr_src")
        tr_pe = sem("tr_pe")
        tr_act = sem("tr_act")
        tr_dve = sem("tr_dve")
        pj_pe = sem("pj_pe")
        pj_act = sem("pj_act")
        pj_dve = sem("pj_dve")
        ff_gu = sem("ff_gu")
        ff_silu = sem("ff_silu")
        ff_h = sem("ff_h")
        ff_down = sem("ff_down")
        ff_out = sem("ff_out")
        at_qk = sem("at_qk")
        at_s = sem("at_s")
        at_sm = sem("at_sm")
        at_nb = sem("at_nb")
        at_e = sem("at_e")
        at_p = sem("at_p")
        at_t = sem("at_t")
        at_pt = sem("at_pt")
        at_pv = sem("at_pv")
        at_o = sem("at_o")
        xi_set = sem("xi_set")
        lo_pe = sem("lo_pe")
        lo_act = sem("lo_act")
        rk_z = sem("rk_z")
        rk_f = sem("rk_f")
        rk_c = sem("rk_c")
        rk_in = sem("rk_in")
        wt_pe = sem("wt_pe")
        wt_act = sem("wt_act")
        wt_dve = sem("wt_dve")
        rk_pe = [sem(f"rk_pe{i}") for i in range(2)]
        rk_dve = [sem(f"rk_dve{i}") for i in range(2)]
        rk_act = [sem(f"rk_act{i}") for i in range(2)]
        rt_landed = sem("rt_landed")
        rt_pe = sem("rt_pe")
        rt_dve = sem("rt_dve")
        rt_act = sem("rt_act")
        mo_sel = sem("mo_sel")
        mo_g = sem("mo_g")
        mo_x = sem("mo_x")
        mo_xa = sem("mo_xa")
        mo_xd = sem("mo_xd")
        mo_gt = sem("mo_gt")
        mo_gte = sem("mo_gte")
        mo_gu = sem("mo_gu")
        mo_silu = sem("mo_silu")
        mo_h = sem("mo_h")
        mo_ht = sem("mo_ht")
        mo_hte = sem("mo_hte")
        mo_y = sem("mo_y")
        mo_ye = sem("mo_ye")
        mo_s = sem("mo_s")
        mo_acc = sem("mo_acc")
        ov_known = sem("ov_known")
        ov_step = [sem(f"ov_step{l}") for l in range(LAYERS)]
        ov_landed = [sem(f"ov_landed{l}") for l in range(LAYERS)]
        ov_gu = [sem(f"ov_gu{l}") for l in range(LAYERS)]
        ov_silu = [sem(f"ov_silu{l}") for l in range(LAYERS)]
        ov_act = [sem(f"ov_act{l}") for l in range(LAYERS)]
        ov_t = [sem(f"ov_t{l}") for l in range(LAYERS)]
        ov_te = [sem(f"ov_te{l}") for l in range(LAYERS)]
        ov_y = [sem(f"ov_y{l}") for l in range(LAYERS)]
        ov_acc = [sem(f"ov_acc{l}") for l in range(LAYERS)]
        fx_landed = sem("fx_landed")
        fx_z1 = sem("fx_z1")
        fx_act = sem("fx_act")
        fx_pe = sem("fx_pe")
        fx_aug = sem("fx_aug")
        x_final = sem("x_final")
        done = sem("done")
        block = ctx.enter_context(nc.Block())

        def pair_of(b):
            return b[:, :].rearrange("p (k t) -> p k t", k=2)

        def rk_wait(eng, who, g, name):
            s, names = {"pe": (rk_pe, RK_PE), "dve": (rk_dve, RK_DVE), "act": (rk_act, RK_ACT)}[who]
            eng.wait_ge(s[g % 2], (g // 2) * len(names) + names.index(name) + 1)

        def rk_heads(g):
            return [(2 * par + pp, par, pp, 2 * (g % 4) + pp, 2 * (2 * (g % 4) + pp) + par)
                    for par in range(2) for pp in range(2)]

        def rk_cols(buf, g, par):
            v = buf[:].rearrange("p t (r q d) -> p t r q d", q=2, d=HD)
            return v[:, g // 4, 2 * (g % 4):2 * (g % 4) + 2, par, :]

        class Chain:

            def __init__(self, eng, s):
                self.eng, self.s, self.n = eng, s, 0

            def link(self, ins):
                self.n += 1
                ins.then_inc(self.s, 1)
                self.eng.wait_ge(self.s, self.n)

        def overflowed(eng, l):
            eng.wait_ge(ov_known, l + 1)
            return eng.If(eng.value_load(ov_flag[l][0:1, 0:1], min_val=0, max_val=1) == 1)

        def wait_taken(eng, b):
            who, n = PROJ_TAKES[b]
            eng.wait_ge(pj_act if who == "act" else pj_dve, n)

        @block.sync
        def _(sp):
            cur = Cursor()
            sp.dma_start(const[:], A["const"]).then_inc(in_landed, 16)
            sp.dma_start(gains[:], A["gains"]).then_inc(in_landed, 16)
            sp.dma_start(cs, A["c"]).then_inc(in_landed, 16)
            sp.dma_start(X[:], A["x"].rearrange("(h p) d -> p h d", p=P)).then_inc(in_landed, 16)

            def load(*parts):
                slot, _, pos = cur.take(len(parts))
                sp.wait_ge(w_free, pos)
                for c0, src in parts:
                    n = int(np.prod(src.shape[1:]))
                    dst = ring[0:src.shape[0], slot, c0:c0 + n]
                    if len(src.shape) == 3:
                        dst = dst.rearrange("p (a b) -> p a b", a=src.shape[1])
                    sp.dma_start(dst, src).then_inc(w_landed[slot], 16)

            def panels(w, nblk, c0=0):
                v = w.rearrange("(k p) n -> p k n", p=P)
                for j in range(nblk):
                    for u in range(2):
                        load((0, v[:, 4 * u:4 * u + 4, c0 + j * BANK:c0 + (j + 1) * BANK]))

            def ffn(wg, wu, wd):
                g = wg.rearrange("(k p) (s n) -> s p k n", p=P, n=SLAB)
                u = wu.rearrange("(k p) (s n) -> s p k n", p=P, n=SLAB)
                d = wd.rearrange("(s c p) n -> s p c n", p=P, c=SLAB // P)
                load((0, g[0]))
                load((0, u[0]))
                with cur.loop(sp, (NSLAB - 1) // 2, 6) as i:
                    for j in range(2):
                        load((0, g[i * 2 + (1 + j)]))
                        load((0, u[i * 2 + (1 + j)]))
                        load((0, d[i * 2 + j]))
                load((0, d[NSLAB - 1]))

            def ffn_n(n):
                ffn(*[A[f"ffn{1 + n % 2}_w_{x}"][n // 2] for x in ("gate", "up", "down")])

            def finish():
                sp.wait_ge(x_final, 1)
                sp.dma_start(out.rearrange("(h p) d -> p h d", p=P), X[:]).then_inc(done, 16)
                sp.wait_ge(done, 16)

            ffn_n(0)
            panels(A["a_w_qkv"][0], 6)
            panels(A["a_w_o"][0], 2)
            ffn_n(1)
            panels(A["kv_w"], 4)
            ffn_n(2)
            panels(A["b_w_q"][0], 2)
            panels(A["b_w_o"][0], 2)
            ffn_n(3)
            panels(A["ada_w_2"][0], 4)
            for i in range(3):
                panels(A["rw_rkv_2"][0, i], 2)
            load((0, A["rw_w1_2"][0].rearrange("(k p) n -> p k n", p=P)),
                 (512, A["rw_a1_2"][0].rearrange("(k p) n -> p k n", p=P)), (1024, A["rw_w2_2"][0]))
            load((0, A["rw_g1_2"][0].rearrange("(k p) n -> p k n", p=P)))
            load((0, A["rw_a2_2"][0]), (1024, A["rw_g2_2"][0][0:P]))
            load((0, A["rw_g2_2"][0][P:P + 32]))
            panels(A["ada_w_2"][0][:, 2 * D:3 * D], 2)
            panels(A["rw_wo_2"][0], 2)

            def moe(l):
                g = A["moe_wgate_2"][l].rearrange("(i e) (u k p) n -> i e u p k n", e=2, u=2, p=P)
                u = A["moe_wup_2"][l].rearrange("(i e) (u k p) n -> i e u p k n", e=2, u=2, p=P)
                d = A["moe_wdown_2"][l].rearrange("(i e) (u c p) n -> i e u p c n", e=2, u=2, p=P)
                with cur.loop(sp, PAIRS, 12) as i:
                    for w in (g, u, d):
                        for half in range(2):
                            for e in range(2):
                                load((0, w[i, e, half]))
                w = [x.rearrange("i e u p k n -> (i e) p u k n") for x in (g, u, d)]
                with overflowed(sp, l):
                    with sp.Fori(0, N_EXP) as i:
                        sp.wait_ge(ov_step[l], i + 1)
                        for j in range(3):
                            for half in range(2):
                                dst = ring[:, 2 * j + half, :]
                                src = w[j][i, :, half]
                                sp.dma_start(dst.rearrange("p (k n) -> p k n", k=src.shape[1]), src)\
                                    .then_inc(ov_landed[l], 16)
                    sp.wait_ge(ov_step[l], N_EXP + 1)

            panels(A["ada_w_2"][0][:, 3 * D:6 * D], 6)
            moe(0)
            panels(A["kv_ada_w_2"], 4)
            panels(A["kv_w_2"], 4)
            panels(A["ada_w_2"][1], 4)
            panels(A["fx_wqg_2"][0], 4)
            panels(A["ada_w_2"][1][:, 2 * D:3 * D], 2)
            panels(A["fx_wo_2"][0], 2)
            panels(A["ada_w_2"][1][:, 3 * D:6 * D], 6)
            moe(1)
            finish()

        @block.tensor
        def _(pe):
            cur = Cursor()
            owed = [0]
            pe.sem_inc(w_free, R)

            def unit():
                slot, landed, _ = cur.take()
                pe.wait_ge(w_landed[slot], landed)
                return slot

            def mm(out, lhsT, rhs, start=True, stop=True, signal=None, transpose=False, tile=None):
                if transpose:
                    ins = pe.transpose(out, lhsT, rhs)
                else:
                    ins = pe.matmul(out, lhsT, rhs, start=start, stop=stop, skip_group_check=True)
                if signal is not None:
                    ins.then_inc(signal, 1)
                elif owed[0]:
                    ins.then_inc(w_free, owed[0])
                    owed[0] = 0

            def transposes(name):
                n = TRANS_AT[name]
                src = tr_source[name]
                pe.wait_ge(tr_src, n + 1)
                for b in range(4):
                    if n:
                        pe.wait_ge(tr_act if b < 2 else tr_dve, 2 * (n - 1) + b % 2 + 1)
                    for k in (2 * b, 2 * b + 1):
                        for h in range(TB):
                            c = (k % 2) * SEQ + h * P
                            mm(bank[4 + b][:, c:c + P], src[:, h, k * P:(k + 1) * P], ident, transpose=True,
                               signal=tr_pe if k % 2 and h else None)

            def transposed(name):
                pe.wait_ge(tr_act, 2 * TRANS_AT[name] + 2)
                pe.wait_ge(tr_dve, 2 * TRANS_AT[name] + 2)

            def project(name, lhs, halves=TB):
                first = PROJ_AT[name]
                for b in range(first, first + PROJ_N[name]):
                    if b >= 2:
                        wait_taken(pe, b - 2)
                    for u in range(2):
                        s = unit()
                        w = ring[:, s, :].rearrange("p (k n) -> p k n", k=4)
                        for h in range(halves):
                            for k in range(4):
                                kk = 4 * u + k
                                mm(bank[2 * (b % 2) + h][:, :], lhs(kk, h), w[:, k, :], kk == 0, kk == KC - 1,
                                   signal=None if k < 3 or (u == 0 and h < halves - 1) else pj_pe if u else w_free)
                    owed[0] += 1

            def tokens_of(buf):
                return lambda k, h: buf[:, k, h * P:(h + 1) * P]

            def gate_up(q0, i=None):
                sg, su = unit(), unit()
                wg = ring[:, sg, :].rearrange("p (k n) -> p k n", k=KC)
                wu = ring[:, su, :].rearrange("p (k n) -> p k n", k=KC)
                for c in range(2):
                    q = q0 + c
                    if q >= 4:
                        pe.wait_ge(ff_h, q - 3 if i is None else i * 4 + (q - 3))
                    for w, o in ((wg, 0), (wu, SEQ)):
                        for k in range(KC):
                            sig = None
                            if k == KC - 1:
                                sig = ff_gu if w is wu else w_free if c else None
                            mm(bank[4 + q % 4][:, o:o + SEQ], w[:, k, c * P:(c + 1) * P], xt[:, k, :],
                               k == 0, k == KC - 1, signal=sig)
                owed[0] += 1

            def down(q0, i=None, first=False, last=False):
                s = unit()
                w = ring[:, s, :].rearrange("p (c n) -> p c n", c=2)
                for c in range(2):
                    q = q0 + c
                    pe.wait_ge(ff_h, q + 1 if i is None else i * 4 + (q + 1))
                    for h in range(TB):
                        for e in range(2):
                            mm(bank[2 * h + e][:, :], ff_h_t[q % 4][:, h * P:(h + 1) * P],
                               w[:, c, e * BANK:(e + 1) * BANK], first and c == 0, last and c == 1,
                               signal=(ff_down if last else w_free) if c and h and e else None)
                if last:
                    owed[0] += 1

            def ffn(n):
                transposes(f"ffn{n}")
                transposed(f"ffn{n}")
                q = 2 * NSLAB * n
                gate_up(q)
                for j in range(2):
                    gate_up(q + 2 + 2 * j)
                    down(q + 2 * j, first=j == 0)
                with cur.loop(pe, (NSLAB - 3) // 2, 6) as i:
                    for j in range(2):
                        gate_up(q + 6 + 2 * j, i)
                        down(q + 4 + 2 * j, i)
                down(q + 2 * (NSLAB - 1), last=True)

            def attention(n, Q_, K_, V_, bias=False):
                g = H * n
                for i in range(H + 3):
                    if i < H:
                        h = i
                        p0, pr = HD * (h % 2), h // 2
                        if g + h >= 4:
                            pe.wait_ge(at_sm, g + h - 3)
                        if bias:
                            pe.wait_ge(fx_aug, h + 1)
                        for t in range(TB):
                            n_s = P * (t + 1)
                            o = bank[h % 4][:, SEQ * t:SEQ * t + n_s]
                            mm(o, Q_[p0:p0 + HD, pr, t * P:(t + 1) * P], K_[p0:p0 + HD, pr, 0:n_s],
                               True, not bias, signal=at_s if t and not bias else None)
                            if bias:
                                mm(o, aug_l(h)[p0:p0 + 48, t * P:(t + 1) * P], aug_r[p0:p0 + 48, 0:n_s],
                                   False, True, signal=at_s if t else None)
                    if 2 <= i < H + 2:
                        h = i - 2
                        pe.wait_ge(at_p, g + h + 1)
                        if g + h >= 2:
                            pe.wait_ge(at_pt, g + h - 1)
                        for j, (t, s) in enumerate(((0, 0), (1, 0), (1, 1))):
                            mm(bank[4 + h % 2][:, j * P:(j + 1) * P], PR[h % 3][:, t * SEQ + s * P:t * SEQ + s * P + P],
                               ident, transpose=True, signal=at_t if j == 2 else None)
                    if i >= 3:
                        h = i - 3
                        pe.wait_ge(at_pt, g + h + 1)
                        if (g + h) // 2 >= 2 and h % 2 == 0:
                            pe.wait_ge(at_o, (g + h) // 2 - 1)
                        o = bank[6 + (h // 2) % 2][HD * (h % 2):HD * (h % 2) + HD, 0:SEQ]
                        mm(o, V_[:, 0, h * HD:(h + 1) * HD], PT[h % 2][:, 0:SEQ], True, False)
                        mm(o[:, P:SEQ], V_[:, 1, h * HD:(h + 1) * HD], PT[h % 2][:, SEQ:SEQ + P], False, True,
                           signal=at_pv)

            def attended(n):
                pe.wait_ge(at_o, H // 2 * (n + 1))

            def gather(n, i, half):
                for k in range(4 * half, 4 * half + 4):
                    for t in range(TB):
                        mm(bank[4 + half][:, (k % 4) * P:(k % 4 + 1) * P], Xn[:, t, k * P:(k + 1) * P], m_pack[:, t, :],
                           t == 0, t == TB - 1, signal=mo_x if k % 4 == 3 and t else None)

            def scatter():
                for t in range(TB):
                    for e in range(2):
                        mm(bank[4 + 2 * t + e][:, :], m_gT[:, t * P:(t + 1) * P], ye[:, e * BANK:(e + 1) * BANK],
                           signal=mo_s)

            def pair(n, i=None, first=False, last=False):
                def at(per, c):
                    return per * n + c if i is None else i * per + (per * n + c)

                pe.wait_ge(mo_xa, at(1, 1))
                pe.wait_ge(mo_xd, at(1, 1))
                for x in range(2):
                    for half in range(2):
                        s = [unit(), unit()]
                        for k in range(4):
                            for e in range(2):
                                w = ring[:, s[e], :].rearrange("p (k n) -> p k n", k=4)
                                kk = 4 * half + k
                                sig = None
                                if k == 3:
                                    sig = mo_gu if half and e else w_free
                                mm(bank[x][64 * e:64 * e + 64, :], XeT[:, kk, 64 * e:64 * e + 64], w[:, k, :],
                                   kk == 0, kk == KC - 1, signal=sig)
                    owed[0] += 1
                if not first:
                    pe.wait_ge(mo_ye, at(2, 0))
                    pe.wait_ge(mo_gte, at(1, 0))
                    scatter()
                if not last:
                    if not first:
                        pe.wait_ge(mo_acc, at(4, -3))
                    pe.wait_ge(mo_sel, at(1, 2))
                    gather(n, i, 0)
                if not first:
                    pe.wait_ge(mo_acc, at(4, -1))
                pe.wait_ge(mo_h, at(1, 1))
                for c in range(4):
                    mm(bank[6][:, c * P:(c + 1) * P], m_h[:, c * P:(c + 1) * P], ident, transpose=True,
                       signal=mo_ht if c == 3 else None)
                if not last:
                    gather(n, i, 1)
                if not first:
                    pe.wait_ge(mo_acc, at(4, 0))
                pe.wait_ge(mo_g, at(1, 1))
                for t in range(TB):
                    mm(bank[7][:, t * P:(t + 1) * P], m_gate[:, t, :], ident, transpose=True,
                       signal=mo_gt if t else None)
                pe.wait_ge(mo_hte, at(1, 1))
                for half in range(2):
                    s = [unit(), unit()]
                    for c in range(2):
                        for j in range(2):
                            for e in range(2):
                                w = ring[:, s[e], :].rearrange("p (c n) -> p c n", c=2)
                                cc = 2 * half + c
                                sig = None
                                if c and j:
                                    sig = mo_y if half and e else w_free
                                mm(bank[2 + j][64 * e:64 * e + 64, :],
                                   m_hT[:, cc * P + 64 * e:cc * P + 64 * e + 64], w[:, c, j * BANK:(j + 1) * BANK],
                                   cc == 0, cc == 3, signal=sig)
                owed[0] += 1

            def unpacked(l, i):
                pe.wait_ge(ov_step[l], i + 1)
                pe.wait_ge(ov_landed[l], i * 96 + 96)
                for t in range(TB):
                    for x in range(2):
                        for kk in range(KC):
                            w = ring[:, 2 * x + kk // 4, :].rearrange("p (k n) -> p k n", k=4)
                            ins = pe.matmul(bank[2 * t + x][:, :], xt[:, kk, t * P:(t + 1) * P], w[:, kk % 4, :],
                                            start=kk == 0, stop=kk == KC - 1, skip_group_check=True)
                    ins.then_inc(ov_gu[l], 1)
                for t in range(TB):
                    pe.wait_ge(ov_act[l], i * 2 + (t + 1))
                    for c in range(4):
                        ins = pe.transpose(bank[4 + t][:, c * P:(c + 1) * P], ov_h[t][:, c * P:(c + 1) * P], ident)
                    ins.then_inc(ov_t[l], 1)
                for t in range(TB):
                    pe.wait_ge(ov_te[l], i * 2 + (t + 1))
                    if t:
                        pe.wait_ge(ov_acc[l], i * 2 + 1)
                    for j in range(2):
                        for c in range(4):
                            w = ring[:, 4 + c // 2, :].rearrange("p (c n) -> p c n", c=2)
                            ins = pe.matmul(bank[6 + j][:, :], ov_hT[t][:, c * P:(c + 1) * P],
                                            w[:, c % 2, j * BANK:(j + 1) * BANK], start=c == 0, stop=c == 3,
                                            skip_group_check=True)
                    ins.then_inc(ov_y[l], 1)

            def moe(l):
                transposes(f"moe{l}")
                transposed(f"moe{l}")
                wait_taken(pe, PROJ_AT[f"gate_f{l}"] + 1)
                pe.wait_ge(rt_landed, 48 * (l + 1))
                for t in range(TB):
                    for k in range(KC):
                        mm(bank[t][:, 0:N_RT], xt[:, k, t * P:(t + 1) * P], rt_w[:, k, :], k == 0, k == KC - 1,
                           signal=rt_pe if t and k == KC - 1 else None)
                pe.wait_ge(rt_dve, 3 * l + 3)
                up = cst("upto", TB, SEQ)
                mm(bank[2][:, 0:N_EXP], up[:, 0, 0:P], rt_sel[:, 0, :])
                mm(bank[2][:, N_EXP:2 * N_EXP], up[:, 0, P:SEQ], rt_sel[:, 0, :], True, False)
                mm(bank[2][:, N_EXP:2 * N_EXP], up[:, 1, P:SEQ], rt_sel[:, 1, :], False, True)
                mm(bank[2][0:1, 2 * N_EXP:3 * N_EXP], up[:, 0, SEQ - 1:SEQ], rt_sel[:, 0, :], True, False)
                mm(bank[2][0:1, 2 * N_EXP:3 * N_EXP], up[:, 1, SEQ - 1:SEQ], rt_sel[:, 1, :], False, True, signal=rt_pe)
                n = PAIRS * l
                pe.wait_ge(mo_sel, n + 1)
                gather(n, None, 0)
                gather(n, None, 1)
                pair(n, first=True)
                with cur.loop(pe, PAIRS - 2, 12) as i:
                    pair(n + 1, i)
                pair(n + PAIRS - 1, last=True)
                pe.wait_ge(mo_ye, 2 * (n + PAIRS))
                pe.wait_ge(mo_gte, n + PAIRS)
                scatter()
                with overflowed(pe, l):
                    with pe.Fori(0, N_EXP) as i:
                        unpacked(l, i)

            def low_rank():
                s1, landed, _ = cur.take(3)
                pe.wait_ge(w_landed[s1], landed)
                sg1, landed, _ = cur.take()
                pe.wait_ge(w_landed[sg1], landed)
                s3, landed, _ = cur.take(2)
                pe.wait_ge(w_landed[s3], landed)
                s4 = unit()
                w1 = ring[:, s1, 0:512].rearrange("p (k n) -> p k n", k=KC)
                a1 = ring[:, s1, 512:1024].rearrange("p (k n) -> p k n", k=KC)
                g1 = ring[:, sg1, 0:1280].rearrange("p (k n) -> p k n", k=KC)

                def hidden(n, o, w):
                    for k in range(KC):
                        mm(o, w(k), xi[n % 2][:, k, :], k == 0, k == KC - 1, signal=lo_pe if k == KC - 1 else None)

                def expand(name, parts):
                    for j in range(2):
                        b = PROJ_AT[name] + j
                        wait_taken(pe, b - 2)
                        for h in range(TB):
                            for n, (x, w) in enumerate(parts):
                                mm(bank[2 * (b % 2) + h][:, :], x[:, h * P:(h + 1) * P],
                                   w[:, j * BANK:(j + 1) * BANK], n == 0, n == len(parts) - 1,
                                   signal=pj_pe if n == len(parts) - 1 else None)

                pe.wait_ge(xi_set, 4)
                hidden(3, bank[4][0:64, 0:SEQ], lambda k: w1[:, k, :])
                pe.wait_ge(xi_set, 5)
                hidden(4, bank[5][0:64, 0:SEQ], lambda k: a1[:, k, :])
                pe.wait_ge(lo_act, 1)
                expand("lora_w", [(lo[0:64, 0:SEQ], ring[0:64, s1, 1024:2048])])
                owed[0] += 1
                pe.wait_ge(xi_set, 6)
                hidden(5, bank[6][:, 0:SEQ], lambda k: g1[:, k, 0:P])
                hidden(5, bank[7][0:32, 0:SEQ], lambda k: g1[:, k, P:P + 32])
                owed[0] += 1
                pe.wait_ge(lo_act, 2)
                expand("lora_a", [(lo[0:64, SEQ:2 * SEQ], ring[0:64, s3, 0:1024])])
                pe.wait_ge(lo_act, 4)
                expand("lora_g", [(lo[:, 2 * SEQ:3 * SEQ], ring[:, s3, 1024:2048]),
                                  (lo[0:32, 3 * SEQ:4 * SEQ], ring[0:32, s4, 0:1024])])
                owed[0] += 2

            def rk_transposes(t):
                if t == 0:
                    pe.wait_ge(rk_in, 1)
                    pe.wait_ge(rk_f, 14)
                else:
                    for g in (2, 3):
                        rk_wait(pe, "dve", g, "yb")
                        rk_wait(pe, "act", g, "u0")
                for x, (s0, s1) in enumerate(((rKK, rR), (rA, rK))):
                    for b in range(4):
                        for r in (2 * b, 2 * b + 1):
                            for y, src in enumerate((s0, s1)):
                                c = (r % 2) * SEQ + y * P
                                mm(bank[4 * x + b][:, c:c + P], src[:, t, r * P:(r + 1) * P], ident, transpose=True,
                                   signal=wt_pe if r % 2 and y else None)
                pe.wait_ge(wt_act, 4 * t + 4)
                pe.wait_ge(wt_dve, 4 * t + 4)

            def rk_bank(g, x):
                return bank[4 * (g % 2) + x]

            def four(g, x, lhs, rhs, sig):
                for i in range(4):
                    c = slice(i * P, (i + 1) * P)
                    mm(rk_bank(g, x)[:, c], rk_t[g % 2][lhs][:, c], rk_t[g % 2][rhs][:, c],
                       signal=rk_pe[g % 2] if i == 3 else None)

            def need(g, dve=None, act=None):
                if dve:
                    rk_wait(pe, "dve", g, dve)
                if act:
                    rk_wait(pe, "act", g, act)

            def s_ab(g):
                if g >= 2 and g != 4 and g != 5:
                    need(g - 2, "yb", "u0")
                for i, par, pp, r, h in rk_heads(g):
                    q = slice(HD * par, HD * par + HD)
                    mm(rk_bank(g, par)[:, pp * P:(pp + 1) * P], AR[q, r, 0, :], BK[q, r, 0, :],
                       signal=rk_pe[g % 2] if i == 3 else None)
                for i, par, pp, r, h in rk_heads(g):
                    q = slice(HD * par, HD * par + HD)
                    mm(rk_bank(g, 2 + par)[:, pp * SEQ:(pp + 1) * SEQ], BK[q, r, 0, :],
                       AR[q, r, :, :].rearrange("p x t -> p (x t)"), signal=rk_pe[g % 2] if i == 3 else None)

            def s_k(g):
                need(g, dve="de")
                for i, par, pp, r, h in rk_heads(g):
                    q = slice(HD * par, HD * par + HD)
                    mm(rk_bank(g, par)[:, pp * SEQ:(pp + 1) * SEQ], BK[q, r, 1, :],
                       AR[q, r, :, :].rearrange("p x t -> p (x t)"), signal=rk_pe[g % 2] if i == 3 else None)

            def s_ny(g):
                need(g, dve="mk")
                for x, tile in enumerate((5, 6)):
                    for i, par, pp, r, h in rk_heads(g):
                        mm(rk_bank(g, 2)[:, x * SEQ + i * HD:x * SEQ + (i + 1) * HD],
                           rk_t[g % 2][tile][:, i * P:(i + 1) * P], rV[:, g // 4, h * HD:(h + 1) * HD],
                           signal=rk_pe[g % 2] if x and i == 3 else None)

            def s_d2(g):
                four(g, 0, 1, 0, True)
                four(g, 1, 0, 1, True)

            def s_d4(g):
                need(g, "d2", "d2t")
                four(g, 0, 4, 3, True)
                four(g, 1, 3, 4, True)

            def s_d8(g):
                need(g, "d4t", "d4")
                four(g, 3, 6, 5, True)

            def s_at(g):
                need(g, "d2i", "ny")
                four(g, 0, 3, 1, True)
                need(g, "d4ti")
                four(g, 1, 6, 7, True)

            def s_t16(g):
                need(g, "at", "b")
                four(g, 2, 4, 0, True)
                four(g, 3, 0, 4, True)

            def s_f(g):
                need(g, "t16t", "t16")
                four(g, 0, 5, 2, True)
                four(g, 1, 2, 5, True)

            def s_f2(g):
                need(g, "f", "ft")
                four(g, 2, 3, 1, True)

            def s_gt(g):
                need(g, "fti")
                four(g, 0, 0, 3, True)

            def s_tt(g):
                need(g, act="gt")
                four(g, 1, 7, 4, True)

            def s_uw(g):
                need(g, "tt", "ny")
                tt = rk_t[g % 2][2]
                for i, par, pp, r, h in rk_heads(g):
                    mm(rk_bank(g, 2)[:, i * HD:(i + 1) * HD], tt[:, i * P:(i + 1) * P],
                       rk_n[g % 2][:, i * HD:(i + 1) * HD], signal=rk_pe[g % 2] if i == 3 else None)
                for i, par, pp, r, h in rk_heads(g):
                    mm(rk_bank(g, 3)[HD * par:HD * par + HD, pp * P:(pp + 1) * P],
                       rKK[:, g // 4, h * HD:(h + 1) * HD], tt[:, i * P:(i + 1) * P],
                       signal=rk_pe[g % 2] if i == 3 else None)

            def s_u(c):
                def step(g):
                    need(g, "z_0" if c else "w1", "u0")
                    if g >= 4 and c == 0:
                        need(g - 4, "z_1")
                    t = slice(CH * c, CH * c + CH)
                    for par in range(2):
                        for x in range(2):
                            for pp in range(2):
                                r, q = 2 * (g % 4) + pp, slice(HD * par, HD * par + HD)
                                lhs = AR[q, r, 1, t] if x else rk_t[g % 2][6][q, SEQ + pp * P + CH * c:SEQ + pp * P + CH * c + CH]
                                mm(rk_bank(g, par)[t, x * P + pp * HD:x * P + (pp + 1) * HD], lhs, Z[q, r, :],
                                   signal=rk_pe[g % 2] if par and x and pp else None)
                return step

            def s_z(c):
                def step(g):
                    need(g, f"u_{c}")
                    t = slice(CH * c, CH * c + CH)
                    for i, par, pp, r, h in rk_heads(g):
                        o = rk_bank(g, 2)[HD * par:HD * par + HD, pp * HD:(pp + 1) * HD]
                        hc = slice(h * HD, (h + 1) * HD)
                        mm(o, rA[t, g // 4, hc], rk_t[g % 2][5][t, i * HD:(i + 1) * HD], True, False)
                        mm(o, rK[t, g // 4, hc], rV[t, g // 4, hc], False, True,
                           signal=rk_pe[g % 2] if i == 3 else None)
                return step

            def s_yb(g):
                for i, par, pp, r, h in rk_heads(g):
                    mm(rk_bank(g, 3)[:, i * HD:(i + 1) * HD], rk_t[g % 2][8][:, i * P:(i + 1) * P],
                       rk_t[g % 2][5][:, i * HD:(i + 1) * HD], signal=rk_pe[g % 2] if i == 3 else None)

            rk_steps = [s_ab, s_k, s_ny, s_d2, s_d4, s_d8, s_at, s_t16, s_f, s_f2, s_gt, s_tt, s_uw,
                        s_u(0), s_z(0), s_u(1), s_z(1), s_yb]

            pe.wait_ge(in_landed, 64)
            ffn(0)
            transposes("mix_a")
            transposed("mix_a")
            project("qkv_a", tokens_of(xt))
            transposes("q_a")
            transposes("k_a")
            transposed("k_a")
            wait_taken(pe, PROJ_AT["qkv_a"] + 5)
            attention(0, QT, KT, V)
            attended(0)
            project("wo_a", tokens_of(OT))
            ffn(1)
            transposes("kv")
            transposed("kv")
            project("kv_b", tokens_of(xt))
            transposes("k_b")
            ffn(2)
            transposes("mix_b")
            transposed("mix_b")
            project("q_b", tokens_of(xt))
            transposes("q_b")
            transposed("q_b")
            attention(1, QT, KT, V)
            attended(1)
            project("wo_b", tokens_of(OT))
            ffn(3)
            pe.wait_ge(cs_set, 2)
            pe.wait_ge(ff_out, 4)
            project("mod_0", lambda k, h: csb[:, k, :], 1)
            transposes("mix_r")
            transposed("mix_r")
            for n, name in enumerate(("rwkv_r", "rwkv_k", "rwkv_v")):
                pe.wait_ge(xi_set, n + 1)
                project(name, tokens_of(xi[n % 2]))
            low_rank()
            pe.wait_ge(rk_f, 1)
            wait_taken(pe, PROJ_AT["lora_g"] + 1)
            for h in range(TB):
                for j in range(2):
                    mm(bank[2 * h + j][:, :], cst("decay_upto"), rS[:, h, j * BANK:(j + 1) * BANK],
                       signal=rk_c if h and j else None)
            for h in range(TB):
                for k in range(KC):
                    mm(bank[4][:, 4 * k + 2 * h:4 * k + 2 * h + 2], rS[:, h, k * P:(k + 1) * P], cst("decay_of"),
                       signal=rk_c if h and k == KC - 1 else None)
            for duo in range(4):
                if duo % 2 == 0:
                    rk_transposes(duo // 2)
                for step in rk_steps:
                    for g in (2 * duo, 2 * duo + 1):
                        step(g)
            for g in (6, 7):
                rk_wait(pe, "dve", g, "yb")
            project("gate_m0", lambda k, h: csb[:, k, :], 1)
            transposes("y_r")
            transposed("y_r")
            project("wo_r", tokens_of(xt))
            project("mod_f0", lambda k, h: csb[:, k, :], 1)
            project("gate_f0", lambda k, h: csb[:, k, :], 1)
            moe(0)
            pe.wait_ge(mo_acc, 4 * PAIRS)
            project("mod_kv", lambda k, h: csb[:, k, :], 1)
            transposes("kv_f")
            transposed("kv_f")
            project("kv_f", tokens_of(xt))
            b = PROJ_AT["forget"]
            wait_taken(pe, b - 2)
            pe.wait_ge(fx_landed, 64)
            for h in range(TB):
                for k in range(KC):
                    mm(bank[2 * (b % 2) + h][:, 0:H], xt[:, k, h * P:(h + 1) * P], fx_w[:, k, :], k == 0, k == KC - 1,
                       signal=pj_pe if k == KC - 1 else None)
            pe.wait_ge(fx_z1, 2)
            transposes("k_f")
            mm(bank[2][0:112, 0:SEQ], fx_ls[:, 0, :], cst("upto", TB, SEQ)[:, 0, :], True, False)
            mm(bank[2][0:112, 0:SEQ], fx_ls[:, 1, :], cst("upto", TB, SEQ)[:, 1, :], False, True, signal=fx_pe)
            pe.wait_ge(fx_z1, 3)
            project("mod_1", lambda k, h: csb[:, k, :], 1)
            transposes("mix_f")
            transposed("mix_f")
            project("qg_f", tokens_of(xt))
            transposes("q_f")
            transposes("g_f")
            transposed("g_f")
            attention(2, QT, KT, fV, bias=True)
            attended(2)
            project("gate_m1", lambda k, h: csb[:, k, :], 1)
            project("wo_f", tokens_of(OT))
            project("mod_f1", lambda k, h: csb[:, k, :], 1)
            project("gate_f1", lambda k, h: csb[:, k, :], 1)
            moe(1)

        @block.scalar
        def _(act):
            def transposes(name, dst, gain_name=None):
                n = TRANS_AT[name]
                for b in range(2):
                    act.wait_ge(tr_pe, 4 * n + b + 1)
                    if gain_name:
                        for k in (2 * b, 2 * b + 1):
                            ins = act.activation(dst[:, k, :], bank[4 + b][:, (k % 2) * SEQ:(k % 2 + 1) * SEQ],
                                                 ACT.Copy, scale=gain(gain_name, k))
                    else:
                        ins = act.activation(dst[:, 2 * b:2 * b + 2, :], pair_of(bank[4 + b]), ACT.Copy)
                    ins.then_inc(tr_act, 1)

            def root(n):
                act.wait_ge(rms_ms, n + 1)
                act.activation(rms_r[n % 2], rms_m[n % 2], ACT.Sqrt).then_inc(rms_root, 1)

            def take(name, dst):
                first = PROJ_AT[name]
                for j in range(PROJ_N[name]):
                    for h in range(TB):
                        act.wait_ge(pj_pe, PROJ_DONE[first + j] + h + 1)
                        act.activation(dst(j, h), bank[2 * ((first + j) % 2) + h][:, :], ACT.Copy).then_inc(pj_act, 1)

            def columns(*bufs):
                return lambda j, h: bufs[j // 2][:, h, (j % 2) * BANK:(j % 2 + 1) * BANK]

            def silu(q, i=None):
                for c in range(2):
                    n = q + c
                    act.wait_ge(ff_gu, n + 1 if i is None else i * 4 + (n + 1))
                    if n >= 2:
                        act.wait_ge(ff_h, n - 1 if i is None else i * 4 + (n - 1))
                    act.activation(ff_silu_t[n % 2], bank[4 + n % 4][:, 0:SEQ], ACT.Silu).then_inc(ff_silu, 1)

            def ffn(n):
                q = 2 * NSLAB * n
                silu(q)
                with act.Fori(0, (NSLAB - 1) // 2) as i:
                    silu(q + 2, i)
                    silu(q + 4, i)

            def attention(n, take_out=True):
                g = H * n
                for i in range(H + 4):
                    if i < H:
                        h = i
                        act.wait_ge(at_nb, g + h + 1)
                        for t in range(TB):
                            v = PR[h % 3][:, t * SEQ:t * SEQ + P * (t + 1)]
                            act.activation(v, v, ACT.Exp, bias=at_bias[h % 3][:, t:t + 1], scale=HD ** -0.5,
                                           accum_out=at_sum[h % 3][:, t:t + 1]).then_inc(at_e, 1)
                    if 2 <= i < H + 2:
                        h = i - 2
                        act.wait_ge(at_t, g + h + 1)
                        if h >= 2:
                            act.wait_ge(at_pv, g + h - 1)
                        act.activation(PT[h % 2], bank[4 + h % 2][:, 0:3 * P], ACT.Copy).then_inc(at_pt, 1)
                    if take_out and i >= 4 and i % 2 == 1:
                        r = (i - 4) // 2
                        act.wait_ge(at_pv, g + 2 * r + 2)
                        act.activation(OT[:, r, :], bank[6 + r % 2][:, 0:SEQ], ACT.Copy).then_inc(at_o, 1)

            def moe(l):
                transposes(f"moe{l}", xt)
                for n in range(2):
                    act.wait_ge(rt_dve, 3 * l + n + 1)
                    for t in range(TB):
                        if n == 0:
                            ins = act.activation(rt_ex[:, t, :], rt_l[:, t, 0:N_GRP], ACT.Exp, bias=rt_nm[:, t:t + 1],
                                                 accum_out=rt_sum[:, t:t + 1])
                        else:
                            ins = act.activation(rt_e2[:, t:t + 1], rt_em[:, t, 1:2], ACT.Exp,
                                                 bias=rt_nm[:, 2 + t:3 + t])
                    ins.then_inc(rt_act, 1)

                def pair(n, i=None, last=False):
                    def at(per, c):
                        return per * n + c if i is None else i * per + (per * n + c)

                    act.wait_ge(mo_gu, at(2, 1))
                    act.activation(m_sg, bank[0][:, :], ACT.Silu).then_inc(mo_silu, 1)
                    if not last:
                        act.wait_ge(mo_x, at(2, 3))
                        act.activation(XeT[:, 0:4, :].rearrange("p k s -> p (k s)"), bank[4][:, :], ACT.Copy)\
                           .then_inc(mo_xa, 1)
                    act.wait_ge(mo_ht, at(1, 1))
                    act.activation(m_hT, bank[6][:, :], ACT.Copy).then_inc(mo_hte, 1)
                    act.wait_ge(mo_gt, at(1, 1))
                    act.activation(m_gT, bank[7][:, 0:SEQ], ACT.Copy).then_inc(mo_gte, 1)
                    act.wait_ge(mo_y, at(1, 1))
                    for j in range(2):
                        act.activation(ye[:, j * BANK:(j + 1) * BANK], bank[2 + j][:, :], ACT.Copy).then_inc(mo_ye, 1)

                n = PAIRS * l
                act.wait_ge(mo_x, 2 * n + 1)
                act.activation(XeT[:, 0:4, :].rearrange("p k s -> p (k s)"), bank[4][:, :], ACT.Copy).then_inc(mo_xa, 1)
                pair(n)
                with act.Fori(0, PAIRS - 2) as i:
                    pair(n + 1, i)
                pair(n + PAIRS - 1, last=True)
                with overflowed(act, l):
                    act.wait_ge(ov_step[l], 1)
                    with act.Fori(0, N_EXP) as i:
                        for t in range(TB):
                            act.wait_ge(ov_gu[l], i * 2 + (t + 1))
                            act.activation(ov_h[t], bank[2 * t][:, :], ACT.Silu).then_inc(ov_silu[l], 1)
                        for t in range(TB):
                            act.wait_ge(ov_t[l], i * 2 + (t + 1))
                            act.activation(ov_hT[t], bank[4 + t][:, :], ACT.Copy).then_inc(ov_te[l], 1)

            act.wait_ge(in_landed, 64)
            act.activation(cs, cs, ACT.Silu).then_inc(cs_set, 1)
            root(0)
            transposes("ffn0", xt, "ffn1_0")
            ffn(0)
            root(1)
            transposes("mix_a", xt, "mix_0")
            take("qkv_a", columns(Q, K, V))
            transposes("q_a", QT)
            transposes("k_a", KT)
            attention(0)
            root(2)
            transposes("ffn1", xt, "ffn2_0")
            ffn(1)
            root(3)
            transposes("kv", xt, "kv")
            take("kv_b", columns(K, V))
            transposes("k_b", KT)
            root(4)
            transposes("ffn2", xt, "ffn1_1")
            ffn(2)
            root(5)
            transposes("mix_b", xt, "mix_1")
            take("q_b", columns(Q))
            transposes("q_b", QT)
            attention(1)
            root(6)
            transposes("ffn3", xt, "ffn2_1")
            ffn(3)
            root(7)
            transposes("mix_r", xt)
            take("rwkv_r", columns(rR))
            take("rwkv_k", columns(rK))
            take("rwkv_v", columns(rV))
            for n, (o, i, f) in enumerate(((lo[0:64, 0:SEQ], bank[4][0:64, 0:SEQ], ACT.Tanh),
                                           (lo[0:64, SEQ:2 * SEQ], bank[5][0:64, 0:SEQ], ACT.Copy),
                                           (lo[:, 2 * SEQ:3 * SEQ], bank[6][:, 0:SEQ], ACT.Sigmoid),
                                           (lo[0:32, 3 * SEQ:4 * SEQ], bank[7][0:32, 0:SEQ], ACT.Sigmoid))):
                act.wait_ge(lo_pe, n + 1)
                act.activation(o, i, f).then_inc(lo_act, 1)
            act.wait_ge(rk_z, 1)
            act.activation(rS[:], rS[:], ACT.Sigmoid).then_inc(rk_f, 1)
            act.wait_ge(rk_z, 2)
            act.activation(rA[:], rA[:], ACT.Sigmoid).then_inc(rk_f, 1)
            take("lora_g", columns(rG))
            act.wait_ge(rk_z, 3)
            act.activation(hs_root, hs_sum, ACT.Sqrt).then_inc(rk_f, 1)
            act.wait_ge(rk_c, 2)
            act.activation(pct[:].rearrange("p k c -> p (k c)"), bank[4][:, 0:32], ACT.Exp).then_inc(rk_f, 1)
            for n, sc in enumerate((1.0, -1.0)):
                for h in range(TB):
                    for j in range(2):
                        act.activation(rE[n][:, h, j * BANK:(j + 1) * BANK], bank[2 * h + j][:, :], ACT.Exp,
                                       scale=sc).then_inc(rk_f, 1)
            act.wait_ge(rk_z, 4)
            for h in range(TB):
                act.activation(rE[2][:, h, :], rE[2][:, h, :], ACT.Exp).then_inc(rk_f, 1)

            def rk_copy(g, name, dst, x, cols=slice(0, BANK), on=None):
                rk_wait(act, "pe", g, on or name)
                return act.activation(dst, bank[4 * (g % 2) + x][:, cols], ACT.Copy)

            def rk_step(name, tile, x):
                def step(g):
                    rk_copy(g, name, rk_t[g % 2][tile], x).then_inc(rk_act[g % 2], 1)
                return step

            def rk_ny(g):
                rk_wait(act, "pe", g, "ny")
                act.activation(rk_n[g % 2], bank[4 * (g % 2) + 2][:, 0:SEQ], ACT.Copy)
                for par in range(2):
                    v = bank[4 * (g % 2) + 2][:, SEQ + 2 * HD * par:SEQ + 2 * HD * (par + 1)]
                    ins = act.activation(rk_cols(rR, g, par), v.rearrange("p (a d) -> p a d", a=2), ACT.Copy)
                ins.then_inc(rk_act[g % 2], 1)

            def rk_u0(g):
                rk_wait(act, "pe", g, "u0")
                act.activation(rk_t[g % 2][6][:, 0:SEQ], bank[4 * (g % 2) + 2][:, 0:SEQ], ACT.Copy)\
                   .then_inc(rk_act[g % 2], 1)

            for duo in range(4):
                if duo % 2 == 0:
                    for b in range(4):
                        act.wait_ge(wt_pe, 8 * (duo // 2) + b + 1)
                        act.activation(AR[:, 2 * b:2 * b + 2, :, :].rearrange("p r x t -> p (r x t)"), bank[b][:, :],
                                       ACT.Copy).then_inc(wt_act, 1)
                for step in (rk_ny, rk_step("d2t", 4, 1), rk_step("d4", 5, 0), rk_step("b", 4, 1),
                             rk_step("t16", 7, 3), rk_step("ft", 3, 1), rk_step("gt", 4, 0), rk_u0):
                    for g in (2 * duo, 2 * duo + 1):
                        step(g)
            act.wait_ge(rk_z, 5)
            act.activation(hs_root, hs_sum, ACT.Sqrt).then_inc(rk_f, 1)
            transposes("y_r", xt)
            root(8)
            moe(0)
            root(9)
            transposes("kv_f", xt)
            take("kv_f", columns(fK, fV))
            act.wait_ge(fx_z1, 1)
            act.activation(fx_z[1], fx_z[1], ACT.Exp, scale=-1.0).then_inc(fx_act, 1)
            act.wait_ge(fx_act, 1)
            act.activation(fx_z[1], fx_z[1], ACT.Ln, bias=1.0).then_inc(fx_act, 1)
            act.wait_ge(rk_z, 6)
            act.activation(hs_root, hs_sum, ACT.Sqrt).then_inc(rk_f, 1)
            transposes("k_f", KT)
            transposes("mix_f", xt)
            take("qg_f", columns(fQ, fG))
            act.wait_ge(pj_act, PROJ_TAKES[PROJ_AT["qg_f"] + 3][1])
            act.activation(fG[:], fG[:], ACT.Sigmoid).then_inc(fx_act, 1)
            act.wait_ge(rk_z, 7)
            act.activation(hs_root, hs_sum, ACT.Sqrt).then_inc(rk_f, 1)
            transposes("q_f", QT)
            transposes("g_f", fGT)
            attention(2, take_out=False)
            root(10)
            moe(1)
            root(11)

        @block.vector
        def _(dve):
            ch = Chain(dve, dve_chain)
            link = ch.link

            def row(name):
                n = ROWS.index(name)
                dve.wait_ge(row_landed[n % NROW], 16 * (n // NROW + 1))
                return bc[n % NROW]

            def row_done(ins, name):
                n = ROWS.index(name)
                ins.then_inc(row_free[n % NROW], 1)
                dve.wait_ge(row_free[n % NROW], n // NROW + 1)

            def modulation(proj, tile, j0, one=0.0):
                for j in range(2):
                    b = PROJ_AT[proj] + j0 + j
                    dve.wait_ge(pj_pe, PROJ_DONE[b] + 1)
                    t = tile[:, j * BANK:(j + 1) * BANK]
                    dve.scalar_tensor_tensor(out=t, in0=bank[2 * (b % 2)][:, :], scalar=one, in1=t,
                                             op0=ALU.add, op1=ALU.add).then_inc(pj_dve, 1)
                wait_taken(dve, b)

            def modulate(tag, proj):
                sh, sc = row("sh_" + tag), row("sc_" + tag)
                modulation(proj, sh, 0)
                modulation(proj, sc, 2, 1.0)
                for h in range(TB):
                    ins = dve.tensor_tensor(Xn[:, h, :], X[:, h, :], sc, ALU.mult)
                row_done(ins, "sc_" + tag)
                for h in range(TB):
                    ins = dve.tensor_tensor(Xn[:, h, :], Xn[:, h, :], sh, ALU.add)
                row_done(ins, "sh_" + tag)
                dve.engine_nop().then_inc(tr_src, 1)

            def layer_norm(n, tag, Y_):
                gt = row("gt_" + tag)
                for h in range(TB):
                    ins = dve.tensor_tensor(Y_[:, h, :], Y_[:, h, :], gt, ALU.mult)
                row_done(ins, "gt_" + tag)
                for h in range(TB):
                    ins = dve.scalar_tensor_tensor(out=X[:, h, :], in0=X[:, h, :], scalar=ALPHA, in1=Y_[:, h, :],
                                                   op0=ALU.mult, op1=ALU.add)
                link(ins)
                st = tiny(64, 24).rearrange("p (h j s) -> p h j s", h=TB, j=2)
                mv = tiny(88, 4).rearrange("p (h s) -> p h s", h=TB)
                for h in range(TB):
                    for j in range(2):
                        ins = dve.bn_stats(st[:, h, j, :], X[:, h, j * BANK:(j + 1) * BANK])
                link(ins)
                for h in range(TB):
                    ins = dve.bn_aggr(mv[:, h, :], st[:, h, :, :].rearrange("p j s -> p (j s)"))
                link(ins)
                k = 8 + n
                dve.tensor_scalar(rms_m[k % 2], mv[:, :, 1], LN_EPS, None, ALU.add).then_inc(rms_ms, 1)
                dve.wait_ge(rms_root, k + 1)
                link(dve.reciprocal(rms_i[k % 2], rms_r[k % 2]))
                for h in range(TB):
                    ins = dve.tensor_scalar(X[:, h, :], X[:, h, :], mv[:, h, 0:1], rms_i[k % 2][:, h:h + 1],
                                            ALU.subtract, ALU.mult)
                link(ins)
                g, b = row(f"ln_g{n}"), row(f"ln_b{n}")
                for h in range(TB):
                    ins = dve.tensor_tensor(X[:, h, :], X[:, h, :], g, ALU.mult)
                row_done(ins, f"ln_g{n}")
                for h in range(TB):
                    ins = dve.tensor_tensor(X[:, h, :], X[:, h, :], b, ALU.add)
                row_done(ins, f"ln_b{n}")

            def mean_square(n, src=X):
                for h in range(TB):
                    ins = dve.tensor_tensor_reduce(Xn[:, h, :], src[:, h, :], src[:, h, :], 1.0, 0.0, ALU.mult,
                                                   ALU.add, rms_m[n % 2][:, h:h + 1])
                link(ins)
                dve.tensor_scalar(rms_m[n % 2], rms_m[n % 2], 1.0 / D, RMS_EPS, ALU.mult, ALU.add).then_inc(rms_ms, 1)
                dve.wait_ge(rms_root, n + 1)
                link(dve.reciprocal(rms_i[n % 2], rms_r[n % 2]))

            def normalise(n, name):
                mean_square(n)
                for h in range(TB):
                    ins = dve.tensor_scalar(Xn[:, h, :], X[:, h, :], rms_i[n % 2][:, h:h + 1], None, ALU.mult)
                ins.then_inc(tr_src, 1)

            def transposes(name, dst, gain_name=None):
                n = TRANS_AT[name]
                for b in (2, 3):
                    dve.wait_ge(tr_pe, 4 * n + b + 1)
                    if gain_name:
                        for k in (2 * b, 2 * b + 1):
                            ins = dve.tensor_scalar(dst[:, k, :], bank[4 + b][:, (k % 2) * SEQ:(k % 2 + 1) * SEQ],
                                                    gain(gain_name, k), None, ALU.mult)
                    else:
                        ins = dve.tensor_copy(dst[:, 2 * b:2 * b + 2, :], pair_of(bank[4 + b]))
                    ins.then_inc(tr_dve, 1)

            def hidden(q, i=None):
                for c in range(2):
                    n = q + c
                    dve.wait_ge(ff_silu, n + 1 if i is None else i * 4 + (n + 1))
                    dve.tensor_tensor(ff_h_t[n % 4], ff_silu_t[n % 2], bank[4 + n % 4][:, SEQ:2 * SEQ],
                                      ALU.mult).then_inc(ff_h, 1)

            def ffn(n):
                q = 2 * NSLAB * n
                hidden(q)
                with dve.Fori(0, (NSLAB - 1) // 2) as i:
                    hidden(q + 2, i)
                    hidden(q + 4, i)
                dve.wait_ge(ff_down, n + 1)
                for h in range(TB):
                    for e in range(2):
                        x = X[:, h, e * BANK:(e + 1) * BANK]
                        ins = dve.scalar_tensor_tensor(out=x, in0=bank[2 * h + e][:, :], scalar=0.5, in1=x,
                                                       op0=ALU.mult, op1=ALU.add)
                ins.then_inc(ff_out, 1)
                dve.wait_ge(ff_out, n + 1)

            def add_projection(name):
                first = PROJ_AT[name]
                for j in range(2):
                    for h in range(TB):
                        dve.wait_ge(pj_pe, PROJ_DONE[first + j] + h + 1)
                        x = X[:, h, j * BANK:(j + 1) * BANK]
                        ins = dve.tensor_tensor(x, bank[2 * ((first + j) % 2) + h][:, :], x, ALU.add)
                        ins.then_inc(pj_dve, 1)
                dve.wait_ge(pj_dve, PROJ_TAKES[first + 1][1])

            def rotate(buf, name):
                v = buf[:].rearrange("p t (h d) -> p t h d", d=HD)
                for h in range(TB):
                    x1, x2 = v[:, h, :, 0:HALF], v[:, h, :, HALF:ROT]
                    c = cst("cos", TB, HALF)[:, h, :].unsqueeze(1).to_broadcast([P, H, HALF])
                    s = cst("sin", TB, HALF)[:, h, :].unsqueeze(1).to_broadcast([P, H, HALF])
                    t = [small[:, 128 * j:128 * (j + 1)].rearrange("p (h d) -> p h d", h=H) for j in range(4)]
                    dve.tensor_tensor(t[0], x1, c, ALU.mult)
                    dve.tensor_tensor(t[1], x2, s, ALU.mult)
                    dve.tensor_tensor(t[2], x1, s, ALU.mult)
                    link(dve.tensor_tensor(t[3], x2, c, ALU.mult))
                    dve.tensor_tensor(x1, t[0], t[1], ALU.subtract)
                    ins = dve.tensor_tensor(x2, t[2], t[3], ALU.add)
                    if h == 0:
                        link(ins)
                ins.then_inc(tr_src, 1)
                dve.wait_ge(tr_src, TRANS_AT[name] + 1)

            def attention(n, mask, count=None, bias=False):
                g = H * n

                def gate_terms(h):
                    dve.tensor_scalar(aug_l(h)[0:112], aug_f[0:112], cst("aug_sel")[0:112, h:h + 1], None, ALU.mult)\
                       .then_inc(fx_aug, 1)

                if bias:
                    gate_terms(0)
                    gate_terms(1)
                for i in range(H + (4 if bias else 1)):
                    if i < H:
                        h = i
                        dve.wait_ge(at_s, g + h + 1)
                        if bias and h + 2 < H:
                            gate_terms(h + 2)
                        if h >= 3:
                            dve.wait_ge(at_t, g + h - 2)
                        for t in range(TB):
                            w = P * (t + 1)
                            ins = dve.tensor_tensor_reduce(PR[h % 3][:, t * SEQ:t * SEQ + w],
                                                           bank[h % 4][:, t * SEQ:t * SEQ + w],
                                                           mask[:, t, 0:w], 1.0, NEG, ALU.add, ALU.max,
                                                           at_max[h % 3][:, t:t + 1])
                        ins.then_inc(at_sm, 1)
                        dve.wait_ge(at_sm, g + h + 1)
                        dve.tensor_scalar(at_bias[h % 3], at_max[h % 3], -HD ** -0.5, None, ALU.mult).then_inc(at_nb, 1)
                    if 1 <= i <= H:
                        h = i - 1
                        dve.wait_ge(at_e, 2 * (g + h) + 2)
                        if count is not None:
                            for t in range(TB):
                                v = PR[h % 3][:, t * SEQ:t * SEQ + P * (t + 1)]
                                ins = dve.tensor_tensor_reduce(v, v, count[:, t, 0:P * (t + 1)], 1.0, 0.0, ALU.mult,
                                                               ALU.add, at_sum[h % 3][:, t:t + 1])
                            link(ins)
                        link(dve.reciprocal(at_inv[h % 3], at_sum[h % 3]))
                        for t in range(TB):
                            v = PR[h % 3][:, t * SEQ:t * SEQ + P * (t + 1)]
                            ins = dve.tensor_scalar(v, v, at_inv[h % 3][:, t:t + 1], None, ALU.mult)
                        ins.then_inc(at_p, 1)
                    if bias and i >= 4 and i % 2 == 1:
                        r = (i - 4) // 2
                        dve.wait_ge(at_pv, g + 2 * r + 2)
                        dve.tensor_tensor(OT[:, r, :], bank[6 + r % 2][:, 0:SEQ], fGT[:, r, :], ALU.mult)\
                           .then_inc(at_o, 1)

            def heads(buf, h):
                return buf[:, h, :].rearrange("p (h d) -> p h d", d=HD)

            def head_sums(src, h):
                return dve.tensor_reduce(hs_sum[:, h * H:(h + 1) * H], heads(src, h), AX.X, ALU.add)

            def per_head(t, h):
                return t[:, h * H:(h + 1) * H].unsqueeze(2).to_broadcast([P, H, HD])

            def take(name, dst):
                first = PROJ_AT[name]
                for j in range(PROJ_N[name]):
                    for h in range(TB):
                        dve.wait_ge(pj_pe, PROJ_DONE[first + j] + h + 1)
                        dve.tensor_copy(dst(j, h), bank[2 * ((first + j) % 2) + h][:, :]).then_inc(pj_dve, 1)
                wait_taken(dve, first + PROJ_N[name] - 1)

            def columns(*bufs):
                return lambda j, h: bufs[j // 2][:, h, (j % 2) * BANK:(j % 2 + 1) * BANK]

            def head_norm(buf, g, n):
                for h in range(TB):
                    ins = dve.tensor_tensor(B[9][:, h, :], buf[:, h, :], buf[:, h, :], ALU.mult)
                link(ins)
                head_sums(B[9], 0)
                link(head_sums(B[9], 1))
                dve.tensor_scalar(hs_sum, hs_sum, 1.0 / HD, QK_EPS, ALU.mult, ALU.add).then_inc(rk_z, 1)
                dve.wait_ge(rk_f, n)
                link(dve.reciprocal(hs_inv, hs_root))
                for h in range(TB):
                    ins = dve.tensor_tensor(heads(buf, h), heads(buf, h), per_head(hs_inv, h), ALU.mult)
                link(ins)
                for h in range(TB):
                    ins = dve.tensor_tensor(heads(buf, h), heads(buf, h),
                                            g.unsqueeze(1).to_broadcast([P, H, HD]), ALU.mult)
                ins.then_inc(tr_src, 1)

            def route(l):
                def both(f):
                    f(0)
                    link(f(1))

                dve.wait_ge(rt_landed, 48 * (l + 1))
                dve.wait_ge(rt_pe, 2 * l + 1)
                dve.memset(rt_g8, NEG)
                both(lambda t: dve.tensor_tensor(rt_l[:, t, :], bank[t][:, 0:N_RT], rt_b, ALU.add))
                link(dve.tensor_copy(rt_g8[:, :, 0:N_GRP], rt_l[:, :, 0:N_GRP]))
                both(lambda t: dve.max(rt_gm[:, t, :], rt_g8[:, t, :]))
                dve.tensor_scalar(rt_nm[:, 0:2], rt_gm[:, :, 0], -1.0, None, ALU.mult).then_inc(rt_dve, 1)
                both(lambda t: dve.max_index(rt_idx[:, t, :], rt_gm[:, t, :], rt_g8[:, t, :]))
                link(dve.tensor_copy(rt_if, rt_idx))
                both(lambda t: dve.tensor_scalar(rt_ohg[:, t, :], cst("eight"), rt_if[:, t, 0:1], None, ALU.is_equal))
                both(lambda t: dve.tensor_scalar(rt_es[:, t, :], rt_l[:, t, N_GRP:N_GRP + N_PER], rt_ohg[:, t, 0:1],
                                                 None, ALU.mult))
                for g in range(1, N_GRP):
                    a = N_GRP + N_PER * g
                    both(lambda t: dve.scalar_tensor_tensor(out=rt_es[:, t, :], in0=rt_l[:, t, a:a + N_PER],
                                                            scalar=rt_ohg[:, t, g:g + 1], in1=rt_es[:, t, :],
                                                            op0=ALU.mult, op1=ALU.add))
                both(lambda t: dve.max(rt_em[:, t, :], rt_es[:, t, :]))
                dve.tensor_scalar(rt_nm[:, 2:4], rt_em[:, :, 0], -1.0, None, ALU.mult).then_inc(rt_dve, 1)
                both(lambda t: dve.max_index(rt_idx[:, t, :], rt_em[:, t, :], rt_es[:, t, :]))
                link(dve.tensor_copy(rt_if, rt_idx))
                both(lambda t: dve.tensor_scalar(rt_se[:, t, :], cst("eight"), rt_if[:, t, 0:1], None, ALU.is_equal))
                both(lambda t: dve.tensor_scalar(rt_t[:, t, :], cst("eight"), rt_if[:, t, 1:2], None, ALU.is_equal))
                link(dve.tensor_tensor(rt_se, rt_se, rt_t, ALU.add))
                for t in range(TB):
                    ins = dve.tensor_tensor(rt_sel[:, t, :].rearrange("p (g e) -> p g e", g=N_GRP),
                                            rt_ohg[:, t, 0:N_GRP].unsqueeze(2).to_broadcast([P, N_GRP, N_PER]),
                                            rt_se[:, t, :].unsqueeze(1).to_broadcast([P, N_GRP, N_PER]), ALU.mult)
                ins.then_inc(rt_dve, 1)
                dve.wait_ge(rt_act, 2 * l + 2)
                link(dve.tensor_scalar(rt_w1[:, 0:2], rt_e2[:, 0:2], 1.0, None, ALU.add))
                link(dve.tensor_tensor(rt_w1[:, 0:2], rt_w1[:, 0:2], rt_sum[:, 0:2], ALU.mult))
                link(dve.reciprocal(rt_w1[:, 0:2], rt_w1[:, 0:2]))
                link(dve.tensor_tensor(rt_w1[:, 2:4], rt_w1[:, 0:2], rt_e2[:, 0:2], ALU.mult))
                both(lambda t: dve.tensor_scalar(rt_ge[:, t, :], cst("eight"), rt_if[:, t, 0:1], rt_w1[:, t:t + 1],
                                                 ALU.is_equal, ALU.mult))
                both(lambda t: dve.tensor_scalar(rt_t[:, t, :], cst("eight"), rt_if[:, t, 1:2], rt_w1[:, 2 + t:3 + t],
                                                 ALU.is_equal, ALU.mult))
                link(dve.tensor_tensor(rt_ge, rt_ge, rt_t, ALU.add))
                both(lambda t: dve.tensor_tensor(rt_gate[:, t, :].rearrange("p (g e) -> p g e", g=N_GRP),
                                                 rt_ohg[:, t, 0:N_GRP].unsqueeze(2).to_broadcast([P, N_GRP, N_PER]),
                                                 rt_ge[:, t, :].unsqueeze(1).to_broadcast([P, N_GRP, N_PER]), ALU.mult))
                dve.wait_ge(rt_pe, 2 * l + 2)
                both(lambda t: dve.tensor_tensor(rt_rank[:, t, :], bank[2][:, t * N_EXP:(t + 1) * N_EXP],
                                                 rt_sel[:, t, :], ALU.mult))
                dve.tensor_reduce(rt_cnt[0:1, 0:1], bank[2][0:1, 2 * N_EXP:3 * N_EXP], AX.X, ALU.max)
                link(dve.tensor_scalar(rt_rank, rt_rank, -1.0, None, ALU.add))
                dve.tensor_scalar(ov_flag[l][0:1, :], rt_cnt[0:1, 0:1], CAP + 0.5, None, ALU.is_gt).then_inc(ov_known, 1)

            def moe(l):
                modulate(f"f{l}", f"mod_f{l}")
                modulation(f"gate_f{l}", row(f"gt_f{l}"), 0, 1.0)
                transposes(f"moe{l}", xt)
                route(l)
                link(dve.memset(Yacc[:], 0.0))

                def matrix(dst, t, e, first, gates):
                    r = rt_rank[:, t, bass.ds(first + e, 1)]
                    g = rt_gate[:, t, bass.ds(first + e, 1)] if gates else None
                    return dve.tensor_scalar(dst[:, t, 64 * e:64 * e + 64], cst("slots"), r, g, ALU.is_equal,
                                             ALU.mult if gates else ALU.bypass)

                def pack(p):
                    for t in range(TB):
                        for e in range(2):
                            ins = matrix(m_pack, t, e, p * 2, False)
                    ins.then_inc(mo_sel, 1)

                def take_packed(v):
                    dve.wait_ge(mo_x, v)
                    dve.tensor_copy(XeT[:, 4:8, :].rearrange("p k s -> p (k s)"), bank[5][:, :]).then_inc(mo_xd, 1)

                def add_blocks(wait):
                    for t in range(TB):
                        for e in range(2):
                            dve.wait_ge(mo_s, wait(2 * t + e + 1))
                            y = Yacc[:, t, e * BANK:(e + 1) * BANK]
                            dve.tensor_tensor(y, bank[4 + 2 * t + e][:, :], y, ALU.add).then_inc(mo_acc, 1)

                def pair(n, p, i=None, first=False, last=False):
                    def at(per, c):
                        return per * n + c if i is None else i * per + (per * n + c)

                    if not last:
                        dve.wait_ge(mo_x, at(2, 2))
                        pack(p + 1)
                    if not first:
                        dve.wait_ge(mo_gt, at(1, 0))
                    for t in range(TB):
                        for e in range(2):
                            ins = matrix(m_gate, t, e, p * 2, True)
                    ins.then_inc(mo_g, 1)
                    dve.wait_ge(mo_silu, at(1, 1))
                    dve.wait_ge(mo_gu, at(2, 2))
                    dve.tensor_tensor(m_h, m_sg, bank[1][:, :], ALU.mult).then_inc(mo_h, 1)
                    if not first:
                        if i is not None or n % PAIRS > 1:
                            dve.wait_ge(mo_acc, at(4, -4))
                        add_blocks(lambda c: at(4, c - 4))
                    if not last:
                        take_packed(at(2, 4))

                n = PAIRS * l
                pack(0)
                take_packed(2 * n + 2)
                pair(n, 0, first=True)
                with dve.Fori(0, PAIRS - 2) as i:
                    pair(n + 1, i + 1, i)
                pair(n + PAIRS - 1, PAIRS - 1, last=True)
                dve.wait_ge(mo_acc, 4 * (n + PAIRS - 1))
                add_blocks(lambda c: 4 * (n + PAIRS - 1) + c)
                dve.wait_ge(mo_acc, 4 * (n + PAIRS))
                with overflowed(dve, l):
                    dve.scalar_tensor_tensor(out=rt_gate, in0=rt_rank, scalar=CAP - 0.5, in1=rt_gate,
                                             op0=ALU.is_gt, op1=ALU.mult).then_inc(ov_step[l], 1)
                    dve.wait_ge(ov_step[l], 1)
                    with dve.Fori(0, N_EXP) as i:
                        for t in range(TB):
                            dve.wait_ge(ov_silu[l], i * 2 + (t + 1))
                            dve.tensor_tensor(ov_h[t], ov_h[t], bank[2 * t + 1][:, :], ALU.mult).then_inc(ov_act[l], 1)
                        for t in range(TB):
                            dve.wait_ge(ov_y[l], i * 2 + (t + 1))
                            for j in range(2):
                                y = Yacc[:, t, j * BANK:(j + 1) * BANK]
                                ins = dve.scalar_tensor_tensor(out=y, in0=bank[6 + j][:, :],
                                                               scalar=rt_gate[:, t, bass.ds(i, 1)], in1=y,
                                                               op0=ALU.mult, op1=ALU.add)
                            ins.then_inc(ov_acc[l], 1)
                            dve.wait_ge(ov_acc[l], i * 2 + (t + 1))
                        dve.sem_inc(ov_step[l], 1)
                    dve.wait_ge(ov_step[l], N_EXP + 1)

            dve.wait_ge(in_landed, 64)
            dve.wait_ge(cs_set, 1)
            dve.tensor_copy(csb[:], cs.unsqueeze(2).to_broadcast([P, KC, P])).then_inc(cs_set, 1)
            normalise(0, "ffn0")
            transposes("ffn0", xt, "ffn1_0")
            ffn(0)
            normalise(1, "mix_a")
            transposes("mix_a", xt, "mix_0")
            wait_taken(dve, PROJ_AT["qkv_a"] + 1)
            rotate(Q, "q_a")
            wait_taken(dve, PROJ_AT["qkv_a"] + 3)
            rotate(K, "k_a")
            transposes("q_a", QT)
            transposes("k_a", KT)
            attention(0, cst("mask_dilated", TB, SEQ), cst("count_dilated", TB, SEQ))
            add_projection("wo_a")
            normalise(2, "ffn1")
            transposes("ffn1", xt, "ffn2_0")
            ffn(1)
            normalise(3, "kv")
            transposes("kv", xt, "kv")
            wait_taken(dve, PROJ_AT["kv_b"] + 1)
            rotate(K, "k_b")
            transposes("k_b", KT)
            normalise(4, "ffn2")
            transposes("ffn2", xt, "ffn1_1")
            ffn(2)
            normalise(5, "mix_b")
            transposes("mix_b", xt, "mix_1")
            wait_taken(dve, PROJ_AT["q_b"] + 1)
            rotate(Q, "q_b")
            transposes("q_b", QT)
            attention(1, cst("mask_causal", TB, SEQ))
            add_projection("wo_b")
            normalise(6, "ffn3")
            transposes("ffn3", xt, "ffn2_1")
            ffn(3)
            mean_square(7)
            g = row("final_norm")
            for h in range(TB):
                ins = dve.scalar_tensor_tensor(out=X[:, h, :], in0=X[:, h, :], scalar=rms_i[1][:, h:h + 1],
                                               in1=g, op0=ALU.mult, op1=ALU.mult)
            row_done(ins, "final_norm")
            modulate("m0", "mod_0")
            transposes("mix_r", xt)
            dve.wait_ge(tr_act, 2 * TRANS_AT["mix_r"] + 2)
            dve.wait_ge(tr_dve, 2 * TRANS_AT["mix_r"] + 2)
            dve.tensor_tensor(xxT[:, :, 1:SEQ], xt[:, :, 0:SEQ - 1], xt[:, :, 1:SEQ], ALU.subtract)
            link(dve.tensor_scalar(xxT[:, :, 0:1], xt[:, :, 0:1], -1.0, None, ALU.mult))
            for n, m in enumerate((0, 2, 3, 1, 4, 5)):
                if 2 <= n < 5:
                    dve.wait_ge(pj_pe, PROJ_DONE[PROJ_AT[("rwkv_k", "rwkv_v", "lora_w")[n - 2]]])
                if n == 5:
                    dve.wait_ge(lo_pe, 1)
                for k in range(KC):
                    ins = dve.scalar_tensor_tensor(out=xi[n % 2][:, k, :], in0=xxT[:, k, :], scalar=gain(f"mu{m}", k),
                                                   in1=xt[:, k, :], op0=ALU.mult, op1=ALU.add)
                ins.then_inc(xi_set, 1)

            def add_row(proj, dst, name):
                w = row(name)
                for j in range(2):
                    b = PROJ_AT[proj] + j
                    for h in range(TB):
                        dve.wait_ge(pj_pe, PROJ_DONE[b] + h + 1)
                        c = slice(j * BANK, (j + 1) * BANK)
                        ins = dve.tensor_tensor(dst[:, h, c], bank[2 * (b % 2) + h][:, :], w[:, c], ALU.add)
                        ins.then_inc(pj_dve, 1)
                wait_taken(dve, PROJ_AT[proj] + 1)

            add_row("lora_w", rS, "w0")
            dve.engine_nop().then_inc(row_free[ROWS.index("w0") % NROW], 1)
            dve.engine_nop().then_inc(rk_z, 1)
            add_row("lora_a", rA, "a0")
            dve.engine_nop().then_inc(row_free[ROWS.index("a0") % NROW], 1)
            dve.engine_nop().then_inc(rk_z, 1)

            wait_taken(dve, PROJ_AT["rwkv_v"] + 1)
            w = row("k_k")
            for h in range(TB):
                ins = dve.tensor_tensor(rKK[:, h, :], rK[:, h, :], w, ALU.mult)
            row_done(ins, "k_k")
            wait_lo = PROJ_TAKES[PROJ_AT["lora_a"] + 1][1]
            for h in range(TB):
                if h == 0:
                    dve.wait_ge(lo_pe, 4)
                ins = dve.tensor_tensor(B[9][:, h, :], rKK[:, h, :], rKK[:, h, :], ALU.mult)
            link(ins)
            head_sums(B[9], 0)
            head_sums(B[9], 1).then_inc(rk_z, 1)
            dve.wait_ge(rk_f, 3)
            link(dve.tensor_scalar(hs_root, hs_root, 1e-12, None, ALU.max))
            link(dve.reciprocal(hs_inv, hs_root))
            for h in range(TB):
                ins = dve.tensor_tensor(heads(rKK, h), heads(rKK, h), per_head(hs_inv, h), ALU.mult)
            link(ins)
            w = row("k_a")
            for h in range(TB):
                ins = dve.scalar_tensor_tensor(out=B[9][:, h, :], in0=rA[:, h, :], scalar=-1.0, in1=w,
                                               op0=ALU.add, op1=ALU.mult)
            row_done(ins, "k_a")
            for h in range(TB):
                ins = dve.scalar_tensor_tensor(out=rK[:, h, :], in0=B[9][:, h, :], scalar=1.0, in1=rK[:, h, :],
                                               op0=ALU.add, op1=ALU.mult)
            link(ins)
            for h in range(TB):
                ins = dve.tensor_tensor(B[9][:, h, :], rR[:, h, :], rK[:, h, :], ALU.mult)
            link(ins)
            w = row("r_k")
            for h in range(TB):
                ins = dve.tensor_tensor(B[9][:, h, :], B[9][:, h, :], w, ALU.mult)
            row_done(ins, "r_k")
            for h in range(TB):
                ins = dve.tensor_reduce(bonus[:, h * H:(h + 1) * H], heads(B[9], h), AX.X, ALU.add)
            link(ins)
            for h in range(TB):
                ins = dve.tensor_tensor(rA[:, h, :], rA[:, h, :], rKK[:, h, :], ALU.mult)
            link(ins)
            dve.wait_ge(rk_f, 12)
            for h in range(TB):
                for j in range(2):
                    c = slice(j * BANK, (j + 1) * BANK)
                    ins = dve.scalar_tensor_tensor(out=B[9][:, h, c], in0=rS[:, h, c], scalar=DECAY,
                                                   in1=bank[2 * h + j][:, :], op0=ALU.mult, op1=ALU.add)
            ins.then_inc(rk_z, 1)
            for h in range(TB):
                dve.tensor_tensor(rR[:, h, :], rR[:, h, :], rE[0][:, h, :], ALU.mult)
                dve.tensor_tensor(rK[:, h, :], rK[:, h, :], rE[1][:, h, :], ALU.mult)
                dve.tensor_tensor(rA[:, h, :], rA[:, h, :], rE[1][:, h, :], ALU.mult)
            dve.wait_ge(rk_f, 14)
            for h in range(TB):
                dve.scalar_tensor_tensor(out=rKK[:, h, :], in0=rKK[:, h, :], scalar=-1.0, in1=rE[2][:, h, :],
                                         op0=ALU.mult, op1=ALU.mult)
            dve.memset(Z[:], 0.0).then_inc(rk_in, 1)

            def rkb(g, x):
                return bank[4 * (g % 2) + x]

            def sig(ins, g):
                ins.then_inc(rk_dve[g % 2], 1)

            def masked(g, tile, src, mask, x0):
                for par in range(2):
                    v = src(rkb(g, x0 + par))
                    ins = dve.tensor_tensor(rk_t[g % 2][tile][:, par * SEQ:(par + 1) * SEQ]
                                            .rearrange("p (a s) -> p a s", a=2), v,
                                            cst(mask).unsqueeze(1).to_broadcast([P, 2, P]), ALU.mult)
                return ins

            def low(b):
                return b[:, 0:SEQ].rearrange("p (a s) -> p a s", a=2)

            def side(x):
                return lambda b: b[:, :].rearrange("p (a x s) -> p a x s", a=2, x=2)[:, :, x, :]

            def v_de(g):
                rk_wait(dve, "pe", g, "ab")
                masked(g, 0, low, "sub_lower", 0)
                sig(masked(g, 2, low, "off_lower", 0), g)

            def v_dtm(g):
                rk_wait(dve, "pe", g, "abt")
                masked(g, 1, side(0), "sub_upper", 2)
                sig(masked(g, 8, side(1), "chunk_upto", 2), g)

            def v_mk(g):
                rk_wait(dve, "pe", g, "k")
                masked(g, 5, side(0), "chunk_upper", 0)
                sig(masked(g, 6, side(1), "chunk_upto", 0), g)

            def v_copy(name, tile, x):
                def step(g):
                    rk_wait(dve, "pe", g, name)
                    sig(dve.tensor_copy(rk_t[g % 2][tile], rkb(g, x)[:, :]), g)
                return step

            def plus_one(g, dst, src):
                sig(dve.tensor_tensor(dst.rearrange("p (a s) -> p a s", a=4), src.rearrange("p (a s) -> p a s", a=4),
                                      ident.unsqueeze(1).to_broadcast([P, 4, P]), ALU.add), g)

            def v_one(tile, pe_name, own):
                def step(g):
                    rk_wait(dve, "pe", g, pe_name)
                    if own:
                        rk_wait(dve, "dve", g, own)
                    else:
                        rk_wait(dve, "act", g, "ft")
                    plus_one(g, rk_t[g % 2][tile], rk_t[g % 2][tile])
                return step

            def v_from(name, tile, x):
                def step(g):
                    rk_wait(dve, "pe", g, name)
                    plus_one(g, rk_t[g % 2][tile], rkb(g, x)[:, :])
                return step

            def v_w1(g):
                rk_wait(dve, "pe", g, "w1")
                sig(dve.tensor_copy(rk_t[g % 2][6][:, SEQ:2 * SEQ], rkb(g, 3)[:, 0:SEQ]), g)

            def v_u(c):
                def step(g):
                    rk_wait(dve, "pe", g, f"u_{c}")
                    rk_wait(dve, "act", g, "u0")
                    t = slice(CH * c, CH * c + CH)
                    for par in range(2):
                        cc = slice(2 * HD * par, 2 * HD * (par + 1))
                        dve.tensor_tensor(rk_t[g % 2][5][t, cc], rkb(g, par)[t, 0:P], rk_t[g % 2][6][t, cc], ALU.add)
                        y = rk_cols(rR, g, par)[t]
                        ins = dve.tensor_tensor(y, rkb(g, par)[t, P:2 * P].rearrange("p (a d) -> p a d", a=2), y, ALU.add)
                    sig(ins, g)
                return step

            def v_z(c):
                def step(g):
                    rk_wait(dve, "pe", g, f"z_{c}")
                    r = slice(2 * (g % 4), 2 * (g % 4) + 2)
                    z = Z[:, r, :]
                    link(dve.tensor_tensor(z, rkb(g, 2)[:, 0:P].rearrange("p (a d) -> p a d", a=2), z, ALU.add))
                    n = 2 * (g // 4) + c
                    sig(dve.tensor_tensor(z, z, pct[:, r, n:n + 1].to_broadcast([P, 2, HD]), ALU.mult), g)
                return step

            def v_yb(g):
                rk_wait(dve, "pe", g, "yb")
                rk_wait(dve, "dve", g, "u_1")
                for par in range(2):
                    y = rk_cols(rR, g, par)
                    v = rkb(g, 3)[:, 2 * HD * par:2 * HD * (par + 1)].rearrange("p (a d) -> p a d", a=2)
                    ins = dve.tensor_tensor(y, v, y, ALU.add)
                sig(ins, g)

            for duo in range(4):
                if duo % 2 == 0:
                    for b in range(4):
                        dve.wait_ge(wt_pe, 8 * (duo // 2) + 4 + b + 1)
                        dve.tensor_copy(BK[:, 2 * b:2 * b + 2, :, :].rearrange("p r x t -> p (r x t)"),
                                        bank[4 + b][:, :]).then_inc(wt_dve, 1)
                for step in (v_de, v_dtm, v_mk, v_copy("d2", 3, 0), v_one(1, "d2t", "dtm"), v_copy("d4t", 6, 1),
                             v_one(3, "d4t", "d2"), v_from("d8", 7, 3), v_one(6, "d8", "d4t"), v_copy("at", 0, 0),
                             v_copy("t16t", 5, 2), v_copy("f", 1, 0), v_from("f2", 0, 2), v_one(3, "f2", None),
                             v_copy("tt", 2, 1), v_w1, v_u(0), v_z(0), v_u(1), v_z(1), v_yb):
                    for g in (2 * duo, 2 * duo + 1):
                        step(g)
            for g in (6, 7):
                rk_wait(dve, "dve", g, "yb")
            head_sums(rR, 0)
            link(head_sums(rR, 1))
            link(dve.tensor_scalar(hs_sum, hs_sum, 1.0 / HD, None, ALU.mult))
            for h in range(TB):
                ins = dve.tensor_tensor(heads(rR, h), heads(rR, h), per_head(hs_sum, h), ALU.subtract)
            link(ins)
            for h in range(TB):
                ins = dve.tensor_tensor(rS[:, h, :], rR[:, h, :], rR[:, h, :], ALU.mult)
            link(ins)
            head_sums(rS, 0)
            link(head_sums(rS, 1))
            dve.tensor_scalar(hs_sum, hs_sum, 1.0 / HD, GN_EPS, ALU.mult, ALU.add).then_inc(rk_z, 1)
            dve.wait_ge(rk_f, 15)
            link(dve.reciprocal(hs_inv, hs_root))
            for h in range(TB):
                ins = dve.tensor_tensor(heads(rR, h), heads(rR, h), per_head(hs_inv, h), ALU.mult)
                dve.tensor_tensor(heads(rV, h), heads(rV, h), per_head(bonus, h), ALU.mult)
            link(dve.memset(tiny(250, 1), 0.0))
            w = row("gn_g")
            for h in range(TB):
                ins = dve.tensor_tensor(rR[:, h, :], rR[:, h, :], w, ALU.mult)
            row_done(ins, "gn_g")
            w = row("gn_b")
            for h in range(TB):
                ins = dve.tensor_tensor(rR[:, h, :], rR[:, h, :], w, ALU.add)
            row_done(ins, "gn_b")
            for h in range(TB):
                ins = dve.tensor_tensor(rR[:, h, :], rR[:, h, :], rV[:, h, :], ALU.add)
            link(ins)
            for h in range(TB):
                ins = dve.tensor_tensor(rR[:, h, :], rR[:, h, :], rG[:, h, :], ALU.mult)
            ins.then_inc(tr_src, 1)
            gt = row("gt_m0")
            modulation("gate_m0", gt, 0, 1.0)
            transposes("y_r", xt)

            take("wo_r", columns(B[1]))
            layer_norm(0, "m0", B[1])
            gt = row("gt_f0")
            moe(0)
            layer_norm(1, "f0", Yacc)
            modulate("kv", "mod_kv")
            transposes("kv_f", xt)
            dve.wait_ge(fx_landed, 64)
            b = PROJ_AT["forget"]
            for h in range(TB):
                dve.wait_ge(pj_pe, PROJ_DONE[b] + h + 1)
                dve.tensor_tensor(fx_z[0][:, h, :], bank[2 * (b % 2) + h][:, 0:H], fx_b, ALU.add).then_inc(pj_dve, 1)
            wait_taken(dve, b)
            link(dve.tensor_scalar(fx_z[1], fx_z[0], -1.0, None, ALU.mult))
            dve.tensor_tensor(fx_z[1], fx_z[0], fx_z[1], ALU.max).then_inc(fx_z1, 1)
            link(dve.memset(fx_ls, 0.0))
            dve.wait_ge(fx_act, 2)
            for x in range(4):
                n = 16 if x == 3 else 32
                ins = dve.scalar_tensor_tensor(out=fx_ls[:, :, 32 * x:32 * x + 16], in0=fx_z[0], scalar=0.0, in1=fx_z[1],
                                               op0=ALU.min, op1=ALU.subtract)
            ins.then_inc(fx_z1, 1)
            wait_taken(dve, PROJ_AT["kv_f"] + 1)
            head_norm(fK, fx_kn, 16)
            dve.wait_ge(fx_pe, 1)
            f = bank[2][0:112, 0:SEQ]
            dve.tensor_scalar(aug_f[0:112], f, cst("aug_val")[0:112], cst("aug_one")[0:112], ALU.mult, ALU.add)
            link(dve.tensor_scalar(aug_r[0:112], f, cst("aug_one")[0:112], -1.0, ALU.mult, ALU.mult))
            dve.tensor_scalar(aug_r[0:112], aug_r[0:112], cst("aug_val")[0:112], None, ALU.add).then_inc(fx_z1, 1)
            transposes("k_f", KT)
            modulate("m1", "mod_1")
            transposes("mix_f", xt)
            wait_taken(dve, PROJ_AT["qg_f"] + 1)
            head_norm(fQ, fx_qn, 17)
            dve.wait_ge(fx_act, 3)
            dve.engine_nop().then_inc(tr_src, 1)
            transposes("q_f", QT)
            transposes("g_f", fGT)
            dve.wait_ge(fx_z1, 3)
            attention(2, cst("mask_causal", TB, SEQ), bias=True)
            gt = row("gt_m1")
            modulation("gate_m1", gt, 0, 1.0)
            take("wo_f", columns(B[1]))
            layer_norm(2, "m1", B[1])
            moe(1)
            layer_norm(3, "f1", Yacc)
            dve.engine_nop().then_inc(x_final, 1)

        @block.gpsimd
        def _(pool):
            for n, name in enumerate(ROWS):
                if n >= NROW:
                    pool.wait_ge(row_free[n % NROW], n // NROW)
                pool.dma_start(bc[n % NROW], row_source(name).partition_broadcast(P)).then_inc(row_landed[n % NROW], 16)
                if name in ("ln_b0", "ln_b2"):
                    l = 0 if name == "ln_b0" else 1
                    pool.wait_ge(row_free[n % NROW], n // NROW + 1)
                    pool.dma_start(rt_w[:, :, 0:N_GRP], A["moe_wgrp_2"][l].rearrange("(k p) n -> p k n", p=P))\
                        .then_inc(rt_landed, 16)
                    pool.dma_start(rt_w[:, :, N_GRP:N_RT], A["moe_wexp_2"][l].rearrange("(k p) n -> p k n", p=P))\
                        .then_inc(rt_landed, 16)
                    pool.dma_start(rt_b, A["rt_bias"][l].partition_broadcast(P)).then_inc(rt_landed, 16)
                if name == "ln_b1":
                    pool.wait_ge(row_free[n % NROW], n // NROW + 1)
                    pool.dma_start(fx_w, A["kv_w_2"][:, 2 * D:2 * D + H].rearrange("(k p) n -> p k n", p=P))\
                        .then_inc(fx_landed, 16)
                    for dst, src in ((fx_b, A["kv_fb_2"]), (fx_kn, A["kv_knorm_2"]), (fx_qn, A["fx_qnorm_2"][0])):
                        pool.dma_start(dst, src.partition_broadcast(P)).then_inc(fx_landed, 16)


_BIG = ["x", "ffn1_w_gate", "ffn1_w_up", "ffn1_w_down", "ffn2_w_gate", "ffn2_w_up", "ffn2_w_down", "a_w_qkv",
        "a_w_o", "kv_w", "b_w_q", "b_w_o", "final_norm"]


_BIG2 = ["ada_w_2", "ada_b_2", "ln_g_2", "ln_b_2", "rw_rkv_2", "rw_w0_2", "rw_w1_2", "rw_w2_2", "rw_a0_2", "rw_a1_2",
         "rw_a2_2", "rw_g1_2", "rw_g2_2", "rw_kk_2", "rw_ka_2", "rw_rk_2", "rw_gn_g_2", "rw_gn_b_2", "rw_wo_2",
         "kv_ada_w_2", "kv_ada_b_2", "kv_w_2", "kv_fb_2", "kv_knorm_2", "fx_wqg_2", "fx_qnorm_2", "fx_wo_2",
         "moe_wgrp_2", "moe_wexp_2", "moe_wgate_2", "moe_wup_2", "moe_wdown_2"]


def kernel(**inputs):
    from concourse import bacc
    from concourse.bass_utils import run_bass_kernel_spmd

    arrays = {n: np.ascontiguousarray(inputs[n]) for n in _BIG}
    arrays["x"] = arrays["x"].reshape(SEQ, D)
    for n in _BIG2:
        arrays[n] = np.ascontiguousarray(inputs[n])
    arrays["rt_bias"] = np.ascontiguousarray(
        np.concatenate([inputs["moe_bgrp_2"], inputs["moe_bexp_2"]], axis=1))
    arrays["c"] = np.ascontiguousarray(inputs["c_2"].reshape(KC, P).T)
    arrays["const"] = np.concatenate(list(CONST.values()), axis=1)

    def columns(v):
        return np.asarray(v).reshape(KC, P).T

    arrays["gains"] = np.ascontiguousarray(np.concatenate(
        [columns(inputs["ffn1_norm"][0]), columns(inputs["ffn1_norm"][1]), columns(inputs["mix_norm"][0]),
         columns(inputs["mix_norm"][1]), columns(inputs["ffn2_norm"][0]), columns(inputs["ffn2_norm"][1]),
         columns(inputs["kv_norm"])] + [columns(inputs["rw_mu_2"][0, i]) for i in range(6)], axis=1))
    nc = bacc.Bacc("TRN2", target_bir_lowering=False, num_devices=1)
    aps = {n: nc.dram_tensor(f"in_{n}", a.shape, F32, kind="ExternalInput").ap() for n, a in arrays.items()}
    out = nc.dram_tensor("out", (SEQ, D), F32, kind="ExternalOutput").ap()
    build(nc, aps, out)
    r = run_bass_kernel_spmd(nc, [{f"in_{n}": a for n, a in arrays.items()}], core_ids=[0])
    return r.results[0]["out"].reshape(1, SEQ, D)
```

```python
from contextlib import ExitStack, contextmanager

import numpy as np

import concourse.bass as bass
from concourse import mybir

F32 = mybir.dt.float32
F32R = mybir.dt.float32r
I32 = mybir.dt.int32
U32 = mybir.dt.uint32
ALU = mybir.AluOpType
ACT = mybir.ActivationFunctionType
AX = mybir.AxisListType

P = 128
SEQ, D = 256, 1024
TB = SEQ // P
KC = D // P
H, HD = 16, 64
DFF = 2816
SLAB = 256
NSLAB = DFF // SLAB
LAYERS = 2
R = 6
UNIT = 2048
BANK = 512
NEG = -1.0e30
RMS_EPS = 1e-6
LN_EPS = 1e-5
GN_EPS = 64e-5
QK_EPS = 1e-6
ALPHA = float((2 * 2) ** 0.25)
DECAY = float(np.exp(-0.5))

ROT = HD // 4
HALF = ROT // 2
THETA = 500000.0
DILATIONS = ((128, 1), (512, 4), (2048, 16))
CH = 64
SUB = 16
N_GRP, N_PER = 4, 8
N_EXP = N_GRP * N_PER
N_RT = N_GRP + N_EXP
D_EXP = 512
CAP = 64


def shape_constants():
    t = np.arange(SEQ)
    rel = t[:, None] - t[None, :]

    def halves(m):
        return m.reshape(TB, P, -1).transpose(1, 0, 2).reshape(P, -1)

    count = sum(((rel >= 0) & (rel <= w) & (rel % d == 0)).astype(np.float32) for w, d in DILATIONS)
    inv = np.float32(THETA) ** (-np.arange(HALF, dtype=np.float32) / np.float32(HALF))
    ang = t.astype(np.float32)[:, None] * inv[None, :].astype(np.float32)
    p = np.arange(P)
    row, col = p[:, None], p[None, :]
    chunk = row // CH == col // CH
    sub = row // SUB == col // SUB
    aug = p % 64
    c = {
        "ident": (row == col),
        "mask_causal": halves(np.where(rel >= 0, 0.0, NEG)),
        "mask_dilated": halves(np.where(count > 0, 0.0, NEG)),
        "count_dilated": halves(count),
        "cos": halves(np.cos(ang)), "sin": halves(np.sin(ang)),
        "sub_lower": sub & (row > col),
        "sub_upper": sub & (row < col),
        "off_lower": chunk & ~sub & (row > col),
        "chunk_upper": chunk & (row < col),
        "chunk_upto": chunk & (row <= col),
        "decay_upto": -np.exp(-0.5) * (chunk & (row <= col)),
        "decay_of": -np.exp(-0.5) * (row // CH == np.arange(2)[None, :]),
        "upto": halves(t[:, None] <= t[None, :]),
        "aug_sel": np.where(aug[:, None] % 32 == np.arange(H)[None, :], 8.0, 0.0),
        "aug_val": ((aug >= 32) & (aug < 48))[:, None],
        "aug_one": (aug < 16)[:, None],
        "slots": np.broadcast_to(np.arange(CAP)[None, :], (P, CAP)),
        "minus_half": np.full((P, 1), -0.5),
        "eight": np.broadcast_to(np.arange(8)[None, :], (P, 8)),
    }
    return {k: np.ascontiguousarray(np.asarray(v, np.float32)) for k, v in c.items()}


CONST = shape_constants()
CONST_AT, _n = {}, 0
for _name, _a in CONST.items():
    CONST_AT[_name] = (_n, _a.shape[1])
    _n += _a.shape[1]
NCONST = _n

GAINS = ["ffn1_0", "ffn1_1", "mix_0", "mix_1", "ffn2_0", "ffn2_1", "kv", "mu0", "mu1", "mu2", "mu3", "mu4", "mu5"]


RK_PE = ["ab", "abt", "k", "ny", "d2", "d2t", "d4", "d4t", "d8", "at", "b", "t16t", "t16", "f", "ft", "f2", "gt", "tt",
         "u0", "w1", "u_0", "z_0", "u_1", "z_1", "yb"]
RK_DVE = ["de", "dtm", "mk", "d2", "dti", "d4t", "d2i", "d8i", "d4ti", "at", "t16t", "f", "f2i", "fti", "tt", "w1",
          "u_0", "z_0", "u_1", "z_1", "yb"]
RK_ACT = ["ny", "d2t", "d4", "b", "t16", "ft", "gt", "u0"]


class Cursor:

    def __init__(self):
        self.pos, self.lots, self.i, self.per = 0, [0] * R, None, 0

    def take(self, dmas=1):
        slot = self.pos % R
        self.lots[slot] += 16 * dmas
        self.pos += 1
        if self.i is None:
            return slot, self.lots[slot], self.pos
        return slot, self.i * (16 * self.per // R) + self.lots[slot], self.i * self.per + self.pos

    def skip_second_trunk(self):
        for dmas in [1] * 12 + [3, 1, 2, 1] + [1] * (4 + 12 * PAIRS):
            self.take(dmas)

    @contextmanager
    def loop(self, eng, n, per):
        assert per % R == 0
        with eng.Fori(0, n) as i:
            self.i, self.per = i, per
            yield i
        self.i = None
        self.pos += (n - 1) * per
        self.lots = [x + (n - 1) * 16 * (per // R) for x in self.lots]


def f32(ap):
    return ap.bitcast(F32)


SPLIT = [("ffn0", 3 * NSLAB), ("qkv_a", 12), ("ffn1", 3 * NSLAB), ("kv_b", 8), ("ffn2", 3 * NSLAB), ("q_b", 4),
         ("ffn3", 3 * NSLAB), ("kv_f", 8), ("qg_f", 8)]
SPLIT_AT = {n: sum(k for _, k in SPLIT[:i]) for i, (n, _) in enumerate(SPLIT)}
SPLIT_NO = {n: i for i, (n, _) in enumerate(SPLIT)}


def gate_unit(s):
    return 3 * s - 1 if s else 0


def down_unit(s):
    return 3 * s + 4 if s < NSLAB - 1 else 3 * s + 2


PROJ = [("qkv_a", 6, "act"), ("wo_a", 2, "dve"), ("kv_b", 4, "act"), ("q_b", 2, "act"), ("wo_b", 2, "dve"),
        ("rwkv_r", 2, "act"), ("rwkv_k", 2, "act"), ("rwkv_v", 2, "act"),
        ("lora_w", 2, "dve"), ("lora_a", 2, "dve"),
        ("wo_r", 2, "dve"), ("kv_f", 4, "act"), ("forget", 1, "dve"), ("qg_f", 4, "act"), ("wo_f", 2, "dve")]
PROJ_AT, PROJ_TAKES, PROJ_DONE, _b = {}, [], [], 0
_taken, _sums = {"act": 0, "dve": 0}, 0
for _name, _k, _eng in PROJ:
    PROJ_AT[_name] = _b
    _b += _k
    for _ in range(_k):
        PROJ_DONE.append(_sums)
        _sums += TB
        _taken[_eng] += TB
        PROJ_TAKES.append((_eng, _taken[_eng]))

TRANS = ["ffn0", "mix_a", "q_a", "k_a", "ffn1", "kv", "k_b", "ffn2", "mix_b", "q_b", "ffn3",
         "mix_r", "y_r", "moe0", "kv_f", "mix_f", "k_f", "q_f", "g_f", "moe1"]
ROWS = ["final_norm", "sh_m0", "sc_m0", "w0", "a0", "k_k", "k_a", "r_k", "gn_g", "gn_b", "gt_m0", "ln_g0", "ln_b0",
        "sh_f0", "sc_f0", "gt_f0", "ln_g1", "ln_b1", "sh_kv", "sc_kv", "sh_m1", "sc_m1", "gt_m1", "ln_g2", "ln_b2",
        "sh_f1", "sc_f1", "gt_f1", "ln_g3", "ln_b3"]
NROW = 6
PAIRS = N_EXP // 2
PROJ_N = {n: k for n, k, _ in PROJ}
TRANS_AT = {n: i for i, n in enumerate(TRANS)}
MODS = ["mix_a", "q_a", "ffn1", "kv", "mix_b", "ffn3", "mix_r"]
MODW = 2048
NORMED = ["ffn0", "mix_a", "ffn1", "kv", "ffn2", "mix_b", "ffn3"]
MOD_ROWS = {n: D * i for i, n in enumerate(["sh_m0", "sc_m0", "gt_m0", "sh_f0", "sc_f0", "gt_f0", "sh_kv", "sc_kv",
                                            "sh_m1", "sc_m1", "gt_m1", "sh_f1", "sc_f1", "gt_f1"])}


def build(nc, A, out):
    ctx = ExitStack()
    with ctx:
        place = {}

        def sb(name, shape, dt=F32):
            t = ctx.enter_context(nc.sbuf_tensor(name, shape, dt))
            place[name] = nc.sbuf_base - 4 * int(np.prod(shape[1:]))
            return t

        def twin(name, shape):
            return nc.alloc_sbuf_tensor_at(name + "_r", shape, F32R, offset=place[name])

        def sem(name):
            return ctx.enter_context(nc.semaphore(name))

        ring = sb("ring", [P, R, UNIT])
        X = sb("X", [P, TB, D])
        xt = sb("xt", [P, KC, SEQ])
        const = sb("const", [P, NCONST])
        gains = sb("gains", [P, len(GAINS) * KC])
        B = [sb(f"B{i}", [P, TB, D]) for i in range(10)]
        small = sb("small", [P, 512])

        def cst(name, *shape):
            a, n = CONST_AT[name]
            v = const[:, a:a + n]
            if len(shape) == 2:
                v = v.rearrange("p (a b) -> p a b", a=shape[0])
            return v

        def gain(name, k):
            i = GAINS.index(name) * KC + k
            return gains[:, i:i + 1]

        ident = cst("ident")
        bank = [ctx.enter_context(nc.psum_tensor(f"bank{i}", [P, BANK], F32)) for i in range(8)]

        Xn = B[0]
        Q, K, V = B[1], B[2], B[3]
        QT = B[4][:].rearrange("p a (b c) -> p (a b) c", c=SEQ)
        KT = B[5][:].rearrange("p a (b c) -> p (a b) c", c=SEQ)
        OT = B[6][:].rearrange("p a (b c) -> p (a b) c", c=SEQ)
        work = B[7]
        ff_silu_t = [work[:, 0, 256 * i:256 * (i + 1)] for i in range(2)]
        PR = [work[:, 0, 512 * i:512 * (i + 1)] for i in range(2)] + [work[:, 1, 0:512]]
        PT = [work[:, 1, 512:512 + 384], B[8][:, 0, 0:384]]

        def row_source(name):
            if name in MOD_ROWS:
                return mods.rearrange("r n -> (r n)")[MOD_ROWS[name]:MOD_ROWS[name] + D]
            if name[:4] in ("ln_g", "ln_b"):
                n = int(name[4])
                return A[name[:4] + "_2"][n // 2, n % 2, :]
            return {"final_norm": lambda: A["final_norm"], "w0": lambda: A["rw_w0_2"][0], "a0": lambda: A["rw_a0_2"][0],
                    "k_k": lambda: A["rw_kk_2"][0], "k_a": lambda: A["rw_ka_2"][0],
                    "r_k": lambda: A["rw_rk_2"][0].rearrange("h n -> (h n)"),
                    "gn_g": lambda: A["rw_gn_g_2"][0], "gn_b": lambda: A["rw_gn_b_2"][0]}[name]()

        rR, rK, rV, rG, rA, rS, rKK = B[1], B[2], B[3], B[4], B[5], B[6], B[0]
        def fm(b):
            return b[:].rearrange("p a (b c) -> p (a b) c", c=SEQ)
        xxT, xi = fm(B[7]), [fm(B[8]), fm(B[9])]
        rE = [B[7], B[8], B[9]]
        AR = fm(B[6]).rearrange("p r (x t) -> p r x t", x=2)
        BK = fm(B[7]).rearrange("p r (x t) -> p r x t", x=2)
        wkx = sb("wkx", [P, 7 * BANK])
        _tiles = [B[i][:, h, j * BANK:(j + 1) * BANK] for i in (8, 9) for h in range(TB) for j in range(2)] + \
                 [xt[:, 2 * i:2 * i + 2, :].rearrange("p a b -> p (a b)") for i in range(4)] + \
                 [wkx[:, BANK * i:BANK * (i + 1)] for i in range(7)]
        rk_t = [_tiles[0:9], _tiles[9:18]]
        rk_n = [_tiles[18][:, 0:256], _tiles[18][:, 256:512]]
        Z = sb("Z", [P, KC, HD])
        pct = sb("pct", [P, KC, 4])
        lo = sb("lo", [P, 1024])

        def tiny(i, n):
            return small_s[:, i:i + n]

        small_s = sb("small_s", [P, 256])
        cs = tiny(100, KC)
        hs_sum, hs_root, hs_inv, bonus = [tiny(112 + 32 * i, 32) for i in range(4)]
        rms_m, rms_r, rms_i = [[tiny(6 * i + 2 * j, 2) for i in range(2)] for j in range(3)]
        at_max, at_bias, at_sum, at_inv = [[tiny(16 + 8 * i + 2 * j, 2) for i in range(3)] for j in range(4)]
        rows = sb("rows", [P, NROW, D])
        bc = [rows[:, i, :] for i in range(NROW)]
        Br = {i: twin(f"B{i}", [P, UNIT]) for i in (0, 1, 2, 4, 6, 7, 8)}
        ring_r, xt_r = twin("ring", [P, R, UNIT]), twin("xt", [P, KC, SEQ])
        lo_r, wkx_r = twin("lo", [P, 1024]), twin("wkx", [P, 7 * BANK])

        def hi_gate(s):
            return Br[(1, 0)[s % 2]][:]

        def hi_up(s):
            return Br[(2, 4)[s % 2]][:]

        def hi_down(s):
            return Br[6][:] if s < NSLAB - 1 else hi_up(s + 1)

        def hi_proj(u):
            return Br[(6, 4)[u]][:]

        def x_lo(k):
            t, k0 = (lo_r, 0) if k < 4 else (Br[7][:, 2 * SEQ:4 * SEQ], 4) if k < 6 else (wkx_r[:, 3 * D:3 * D + 2 * SEQ], 6)
            return t[:, (k - k0) * SEQ:(k - k0 + 1) * SEQ]

        ff_h_t = [Br[7][:, D + SEQ * i:D + SEQ * (i + 1)] for i in range(4)]
        ff_lo_t = [Br[8][:, SEQ * i:SEQ * (i + 1)] for i in range(4)]

        mod_acc = [B[9][:].rearrange("p a b -> p (a b)"), rows[:, 4:6, :].rearrange("p a b -> p (a b)")]
        mod_w = [wkx[:, D * i:D * (i + 1)] for i in range(3)] + [B[8][:, 1, :]]
        mix_t = sb("mix_t", [P, D])
        gn_t = [mix_t[:, 0:BANK], mix_t[:, BANK:D]]
        mod_sum, mod_bias = mix_t[:, 0:BANK], mix_t[:, BANK:D]
        mods = nc.dram_tensor("mod_rows", (len(MODS), MODW), F32, kind="Internal").ap()

        Yacc = B[1]
        XeT = B[2][:, 0, :].rearrange("p (k s) -> p k s", k=KC)
        ye = B[2][:, 1, :]
        m_h, m_sg = B[3][:, 0, 0:BANK], B[3][:, 0, BANK:2 * BANK]
        m_hT = B[3][:, 1, 0:BANK]
        m_pack = B[3][:, 1, BANK:BANK + 256].rearrange("p (t s) -> p t s", t=TB)
        m_gate = B[3][:, 1, BANK + 256:2 * BANK].rearrange("p (t s) -> p t s", t=TB)
        m_gT = B[5][:, 0, 0:SEQ]
        _r, _at = B[4][:, 0, :], [0]

        def rt(n, *shape):
            v = _r[:, _at[0]:_at[0] + n]
            _at[0] += n
            return v.rearrange("p (a b) -> p a b", a=shape[0]) if shape else v

        rt_w, rt_b, rt_l = rt(KC * N_RT, KC), rt(N_RT), rt(TB * N_RT, TB)
        rt_g8, rt_gm, rt_ohg, rt_ex = rt(16, TB), rt(16, TB), rt(16, TB), rt(8, TB)
        rt_es, rt_em, rt_ge, rt_se, rt_t = rt(16, TB), rt(16, TB), rt(16, TB), rt(16, TB), rt(16, TB)
        rt_if, rt_sum, rt_nm, rt_e2, rt_w1 = rt(16, TB), rt(4), rt(4), rt(4), rt(4)
        rt_gate, rt_sel, rt_rank = rt(2 * N_EXP, TB), rt(2 * N_EXP, TB), rt(2 * N_EXP, TB)
        rt_cnt = rt(2)
        ov_flag = [sb(f"ov_flag{l}", [P, 1], I32) for l in range(LAYERS)]
        ov_h = m_h, m_sg
        ov_hT = m_hT, B[2][:, 0, 0:BANK]
        rt_idx = ctx.enter_context(nc.sbuf_tensor("rt_idx", [P, 16], U32))[:].rearrange("p (t n) -> p t n", t=TB)
        fQ, fK, fV, fG, fGT = B[1], B[2], B[3], B[0], fm(B[9])
        fx = B[8]
        aug_f, aug_r = fx[:, 1, 0:SEQ], fx[:, 1, SEQ:2 * SEQ]
        aug_tiles = [fx[:, 1, 512 + SEQ * i:512 + SEQ * (i + 1)] for i in range(2)]
        fx_ls = fx[:, 0, 512:736].rearrange("p (t n) -> p t n", t=TB)
        fx_w = fx[:, 0, 736:864].rearrange("p (k n) -> p k n", k=KC)
        fx_b, fx_kn, fx_qn = fx[:, 0, 864:880], fx[:, 0, 880:944], fx[:, 0, 944:1008]
        fx_z = [small[:, 32 * i:32 * (i + 1)].rearrange("p (t n) -> p t n", t=TB) for i in range(4)]

        def aug_l(h):
            return aug_tiles[h % 2]

        tr_source = {"y_r": B[1], "k_f": fK, "q_f": fQ, "g_f": fG, "q_a": Q, "k_a": K, "k_b": K, "q_b": Q}
        for name in TRANS:
            tr_source.setdefault(name, Xn)

        w_landed = [sem(f"w_landed{i}") for i in range(R)]
        w_free = sem("w_free")
        in_landed = sem("in_landed")
        const_landed = sem("const_landed")
        x_landed = [sem(f"x_landed{h}") for h in range(TB)]
        nm_inv = sem("nm_inv")
        nm_act = sem("nm_act")
        row_landed = [sem(f"row_landed{i}") for i in range(NROW)]
        row_free = [sem(f"row_free{i}") for i in range(NROW)]
        cs_set = sem("cs_set")
        mod_chain = sem("mod_chain")
        mod_seen = sem("mod_seen")
        mod_b = sem("mod_b")
        mod_landed = [sem(f"mod_landed{i}") for i in range(4)]
        mod_done = sem("mod_done")
        mod_pe = sem("mod_pe")
        mod_take = sem("mod_take")
        mod_out = [sem(f"mod_out{i}") for i in range(2)]
        dve_chain = sem("dve_chain")
        act_chain = sem("act_chain")
        rms_ms = sem("rms_ms")
        rms_root = sem("rms_root")
        tr_src = sem("tr_src")
        tr_pe = sem("tr_pe")
        tr_act = sem("tr_act")
        tr_dve = sem("tr_dve")
        pj_pe = sem("pj_pe")
        pj_act = sem("pj_act")
        pj_dve = sem("pj_dve")
        sp_hi = sem("sp_hi")
        sp_lo = sem("sp_lo")
        xs_lo = sem("xs_lo")
        ff_m = sem("ff_m")
        ff_hi = sem("ff_hi")
        ff_gu = sem("ff_gu")
        ff_silu = sem("ff_silu")
        ff_h = sem("ff_h")
        ff_down = sem("ff_down")
        ff_out = sem("ff_out")
        at_qk = sem("at_qk")
        at_s = sem("at_s")
        at_sm = sem("at_sm")
        at_nb = sem("at_nb")
        at_e = sem("at_e")
        at_p = sem("at_p")
        at_t = sem("at_t")
        at_pt = sem("at_pt")
        at_pv = sem("at_pv")
        at_o = sem("at_o")
        xi_set = sem("xi_set")
        lo_pe = sem("lo_pe")
        lo_act = sem("lo_act")
        rk_z = sem("rk_z")
        rk_f = sem("rk_f")
        lg_pe = sem("lg_pe")
        lg_act = sem("lg_act")
        rk_c = sem("rk_c")
        rk_in = sem("rk_in")
        gn_chain = sem("gn_chain")
        gn_var = sem("gn_var")
        gn_root = sem("gn_root")
        gn_done = sem("gn_done")
        wt_pe = sem("wt_pe")
        wt_act = sem("wt_act")
        wt_dve = sem("wt_dve")
        rk_pe = [sem(f"rk_pe{i}") for i in range(2)]
        rk_dve = [sem(f"rk_dve{i}") for i in range(2)]
        rk_act = [sem(f"rk_act{i}") for i in range(2)]
        rt_landed = sem("rt_landed")
        rt_pe = sem("rt_pe")
        rt_dve = sem("rt_dve")
        rt_act = sem("rt_act")
        mo_sel = sem("mo_sel")
        mo_g = sem("mo_g")
        mo_x = sem("mo_x")
        mo_xa = sem("mo_xa")
        mo_xd = sem("mo_xd")
        mo_gt = sem("mo_gt")
        mo_gte = sem("mo_gte")
        mo_gu = sem("mo_gu")
        mo_silu = sem("mo_silu")
        mo_h = sem("mo_h")
        mo_ht = sem("mo_ht")
        mo_hte = sem("mo_hte")
        mo_y = sem("mo_y")
        mo_ye = sem("mo_ye")
        mo_s = sem("mo_s")
        mo_acc = sem("mo_acc")
        ov_known = sem("ov_known")
        ov_step = [sem(f"ov_step{l}") for l in range(LAYERS)]
        ov_landed = [sem(f"ov_landed{l}") for l in range(LAYERS)]
        ov_gu = [sem(f"ov_gu{l}") for l in range(LAYERS)]
        ov_silu = [sem(f"ov_silu{l}") for l in range(LAYERS)]
        ov_act = [sem(f"ov_act{l}") for l in range(LAYERS)]
        ov_t = [sem(f"ov_t{l}") for l in range(LAYERS)]
        ov_te = [sem(f"ov_te{l}") for l in range(LAYERS)]
        ov_y = [sem(f"ov_y{l}") for l in range(LAYERS)]
        ov_acc = [sem(f"ov_acc{l}") for l in range(LAYERS)]
        fx_landed = sem("fx_landed")
        fx_z1 = sem("fx_z1")
        fx_act = sem("fx_act")
        fx_pe = sem("fx_pe")
        fx_aug = sem("fx_aug")
        m0_mixed = sem("m0_mixed")
        row_mixed = sem("row_mixed")
        mix_chain = sem("mix_chain")
        x_final = sem("x_final")
        done = sem("done")
        block = ctx.enter_context(nc.Block())

        def pair_of(b):
            return b[:, :].rearrange("p (k t) -> p k t", k=2)

        def rk_wait(eng, who, g, name):
            s, names = {"pe": (rk_pe, RK_PE), "dve": (rk_dve, RK_DVE), "act": (rk_act, RK_ACT)}[who]
            eng.wait_ge(s[g % 2], (g // 2) * len(names) + names.index(name) + 1)

        def rk_heads(g):
            return [(2 * par + pp, par, pp, 2 * (g % 4) + pp, 2 * (2 * (g % 4) + pp) + par)
                    for par in range(2) for pp in range(2)]

        def quarter(q):
            return q // 2, slice(BANK * (q % 2), BANK * (q % 2 + 1)), H * (q // 2) + 8 * (q % 2)

        def eight(v):
            return v.rearrange("p (h d) -> p h d", d=HD)

        def spread(t, n):
            return t[:, n:n + 8].unsqueeze(2).to_broadcast([P, 8, HD])

        def rk_cols(buf, g, par):
            v = buf[:].rearrange("p t (r q d) -> p t r q d", q=2, d=HD)
            return v[:, g // 4, 2 * (g % 4):2 * (g % 4) + 2, par, :]

        class Chain:

            def __init__(self, eng, s):
                self.eng, self.s, self.n = eng, s, 0

            def link(self, ins):
                self.n += 1
                ins.then_inc(self.s, 1)
                self.eng.wait_ge(self.s, self.n)

        def overflowed(eng, l):
            eng.wait_ge(ov_known, l + 1)
            return eng.If(eng.value_load(ov_flag[l][0:1, 0:1], min_val=0, max_val=1) == 1)

        def wait_taken(eng, b):
            who, n = PROJ_TAKES[b]
            eng.wait_ge(pj_act if who == "act" else pj_dve, n)

        @block.sync
        def _(sp):
            cur = Cursor()
            for h in range(TB):
                sp.dma_start(X[:, h, :], A["x"].rearrange("(h p) d -> h p d", p=P)[h]).then_inc(x_landed[h], 16)
            sp.dma_start(const[:, 0:P], A["const"][:, 0:P]).then_inc(in_landed, 16)
            sp.dma_start(gains[:], A["gains"]).then_inc(in_landed, 16)
            sp.dma_start(cs, A["c"]).then_inc(in_landed, 16)

            def load(*parts):
                slot, _, pos = cur.take(len(parts))
                sp.wait_ge(w_free, pos)
                for c0, src in parts:
                    n = int(np.prod(src.shape[1:]))
                    dst = ring[0:src.shape[0], slot, c0:c0 + n]
                    if len(src.shape) == 3:
                        dst = dst.rearrange("p (a b) -> p a b", a=src.shape[1])
                    sp.dma_start(dst, src).then_inc(w_landed[slot], 16)

            def panels(w, nblk, c0=0):
                v = w.rearrange("(k p) n -> p k n", p=P)
                for j in range(nblk):
                    for u in range(2):
                        load((0, v[:, 4 * u:4 * u + 4, c0 + j * BANK:c0 + (j + 1) * BANK]))

            def ffn(wg, wu, wd):
                g = wg.rearrange("(k p) (s n) -> s p k n", p=P, n=SLAB)
                u = wu.rearrange("(k p) (s n) -> s p k n", p=P, n=SLAB)
                d = wd.rearrange("(s c p) n -> s p c n", p=P, c=SLAB // P)
                load((0, g[0]))
                load((0, u[0]))
                if cur.pos == 2:
                    sp.dma_start(const[:, P:], A["const"][:, P:]).then_inc(const_landed, 16)
                with cur.loop(sp, (NSLAB - 1) // 2, 6) as i:
                    for j in range(2):
                        load((0, g[i * 2 + (1 + j)]))
                        load((0, u[i * 2 + (1 + j)]))
                        load((0, d[i * 2 + j]))
                load((0, d[NSLAB - 1]))

            def ffn_n(n):
                ffn(*[A[f"ffn{1 + n % 2}_w_{x}"][n // 2] for x in ("gate", "up", "down")])

            def finish():
                sp.wait_ge(x_final, 1)
                sp.dma_start(out.rearrange("(h p) d -> p h d", p=P), X[:]).then_inc(done, 16)
                sp.wait_ge(done, 16)

            ffn_n(0)
            panels(A["a_w_qkv"][0], 6)
            panels(A["a_w_o"][0], 2)
            ffn_n(1)
            panels(A["kv_w"], 4)
            ffn_n(2)
            panels(A["b_w_q"][0], 2)
            panels(A["b_w_o"][0], 2)
            ffn_n(3)
            for i in range(3):
                panels(A["rw_rkv_2"][0, i], 2)
            load((0, A["rw_w1_2"][0].rearrange("(k p) n -> p k n", p=P)),
                 (512, A["rw_a1_2"][0].rearrange("(k p) n -> p k n", p=P)), (1024, A["rw_w2_2"][0]))
            load((0, A["rw_g1_2"][0].rearrange("(k p) n -> p k n", p=P)))
            load((0, A["rw_a2_2"][0]), (1024, A["rw_g2_2"][0][0:P]))
            load((0, A["rw_g2_2"][0][P:P + 32]))
            panels(A["rw_wo_2"][0], 2)

            def moe(l):
                g = A["moe_wgate_2"][l].rearrange("(i e) (u k p) n -> i e u p k n", e=2, u=2, p=P)
                u = A["moe_wup_2"][l].rearrange("(i e) (u k p) n -> i e u p k n", e=2, u=2, p=P)
                d = A["moe_wdown_2"][l].rearrange("(i e) (u c p) n -> i e u p c n", e=2, u=2, p=P)
                with cur.loop(sp, PAIRS, 12) as i:
                    for w in (g, u, d):
                        for half in range(2):
                            for e in range(2):
                                load((0, w[i, e, half]))
                w = [x.rearrange("i e u p k n -> (i e) p u k n") for x in (g, u, d)]
                with overflowed(sp, l):
                    with sp.Fori(0, N_EXP) as i:
                        sp.wait_ge(ov_step[l], i + 1)
                        for j in range(3):
                            for half in range(2):
                                dst = ring[:, 2 * j + half, :]
                                src = w[j][i, :, half]
                                sp.dma_start(dst.rearrange("p (k n) -> p k n", k=src.shape[1]), src)\
                                    .then_inc(ov_landed[l], 16)
                    sp.wait_ge(ov_step[l], N_EXP + 1)

            moe(0)
            panels(A["kv_w_2"], 4)
            panels(A["fx_wqg_2"][0], 4)
            panels(A["fx_wo_2"][0], 2)
            moe(1)
            finish()

        @block.tensor
        def _(pe):
            cur = Cursor()
            owed = [0]
            pe.sem_inc(w_free, R)

            def unit():
                slot, landed, _ = cur.take()
                pe.wait_ge(w_landed[slot], landed)
                return slot

            def mm(out, lhsT, rhs, start=True, stop=True, signal=None, transpose=False, tile=None):
                if transpose:
                    ins = pe.transpose(out, lhsT, rhs)
                else:
                    ins = pe.matmul(out, lhsT, rhs, start=start, stop=stop, skip_group_check=True)
                if signal is not None:
                    ins.then_inc(signal, 1)
                elif owed[0]:
                    ins.then_inc(w_free, owed[0])
                    owed[0] = 0

            def mod_sums(r):
                pe.wait_ge(mod_done, r + 1)
                if r:
                    n = TRANS_AT[MODS[r]]
                    pe.wait_ge(tr_act, 2 * n)
                    pe.wait_ge(tr_dve, 2 * n)
                for b in range(4):
                    mm(bank[4 + b][0:1, :], cst("upto", TB, SEQ)[:, 0, SEQ - 1:SEQ], mod_acc[r % 2][:, b * BANK:(b + 1) * BANK],
                       signal=mod_pe)

            def transposes(name):
                n = TRANS_AT[name]
                src = tr_source[name]
                if name in MODS:
                    mod_sums(MODS.index(name))
                if name in NORMED:
                    pe.wait_ge(nm_act, NORMED.index(name) + 1)
                pe.wait_ge(tr_src, n + 1)
                for b in range(4):
                    if name in MODS:
                        pe.wait_ge(mod_take, 4 * MODS.index(name) + b + 1)
                    elif n:
                        pe.wait_ge(tr_act if b < 2 else tr_dve, 2 * (n - 1) + b % 2 + 1)
                    for k in (2 * b, 2 * b + 1):
                        for h in range(TB):
                            c = (k % 2) * SEQ + h * P
                            mm(bank[4 + b][:, c:c + P], src[:, h, k * P:(k + 1) * P], ident, transpose=True,
                               signal=tr_pe if k % 2 and h else None)

            def transposed(name):
                pe.wait_ge(tr_act, 2 * TRANS_AT[name] + 2)
                pe.wait_ge(tr_dve, 2 * TRANS_AT[name] + 2)

            def project(name, lhs, halves=TB):
                first = PROJ_AT[name]
                for b in range(first, first + PROJ_N[name]):
                    if b >= 2:
                        wait_taken(pe, b - 2)
                    for u in range(2):
                        s = unit()
                        w = ring[:, s, :].rearrange("p (k n) -> p k n", k=4)
                        for h in range(halves):
                            for k in range(4):
                                kk = 4 * u + k
                                mm(bank[2 * (b % 2) + h][:, :], lhs(kk, h), w[:, k, :], kk == 0, kk == KC - 1,
                                   signal=None if k < 3 or (u == 0 and h < halves - 1) else pj_pe if u else w_free)
                    owed[0] += 1

            def project_split(name):
                first = PROJ_AT[name]
                for b in range(first, first + PROJ_N[name]):
                    if b >= 2:
                        wait_taken(pe, b - 2)
                    for u in range(2):
                        s = unit()
                        if b == first:
                            pe.wait_ge(xs_lo, 2 * SPLIT_NO[name] + u + 1)
                        pe.wait_ge(sp_lo, SPLIT_AT[name] + 2 * (b - first) + u + 1)
                        hi, w = [v.rearrange("p (k n) -> p k n", k=4) for v in (hi_proj(u), ring_r[:, s, :])]
                        for h in range(TB):
                            t = slice(h * P, (h + 1) * P)
                            for k in range(4):
                                kk, o = 4 * u + k, bank[2 * (b % 2) + h][:, :]
                                mm(o, xt_r[:, kk, t], hi[:, k, :], kk == 0, False)
                                mm(o, xt_r[:, kk, t], w[:, k, :], False, False)
                                mm(o, x_lo(kk)[:, t], hi[:, k, :], False, kk == KC - 1,
                                   signal=None if k < 3 or (u == 0 and h == 0) else pj_pe if u else w_free)
                    owed[0] += 1

            def tokens_of(buf):
                return lambda k, h: buf[:, k, h * P:(h + 1) * P]

            def split(n, x, i):
                x += SPLIT_AT[f"ffn{n}"] + 1
                pe.wait_ge(sp_lo, x if i is None else i * 6 + x)

            def three(out, whi, wlo, xhi, xlo, start, stop, signal=None):
                mm(out, whi, xhi, start, False)
                mm(out, whi, xlo, False, False)
                mm(out, wlo, xhi, False, stop, signal=signal)

            def gate_up(n, s, i=None):
                sg, su = unit(), unit()
                wg, wu, hg, hu = [v.rearrange("p (k n) -> p k n", k=KC)
                                  for v in (ring_r[:, sg, :], ring_r[:, su, :], hi_gate(s), hi_up(s))]
                split(n, gate_unit(s), i)
                for c in range(2):
                    q = 2 * (NSLAB * n + s) + c
                    if q >= 4:
                        pe.wait_ge(ff_h, q - 3 if i is None else i * 4 + (q - 3))
                    for w, hi, o in ((wg, hg, 0), (wu, hu, SEQ)):
                        if w is wu and c == 0:
                            split(n, gate_unit(s) + 1, i)
                        for k in range(KC):
                            if s == 0 and c == 0 and w is wg and k == 4:
                                pe.wait_ge(xs_lo, 2 * SPLIT_NO[f"ffn{n}"] + 2)
                            sig = None
                            if k == KC - 1:
                                sig = ff_gu if w is wu else w_free if c else None
                            t = slice(c * P, (c + 1) * P)
                            three(bank[4 + q % 4][:, o:o + SEQ], hi[:, k, t], w[:, k, t], xt_r[:, k, :], x_lo(k),
                                  k == 0, k == KC - 1, sig)
                owed[0] += 1

            def down(n, s, i=None):
                u = unit()
                w, hi = [v.rearrange("p (c n) -> p c n", c=2) for v in (ring_r[:, u, :], hi_down(s))]
                q0, last = 2 * (NSLAB * n + s), s == NSLAB - 1
                split(n, down_unit(s), i)

                def add(h, e, c, stop, signal):
                    q, t, d = (q0 + c) % 4, slice(h * P, (h + 1) * P), slice(e * BANK, (e + 1) * BANK)
                    o, first = bank[2 * h + e][:, :], s == 0 and c == 0
                    mm(o, ff_h_t[q][:, t], hi[:, c, d], first, False)
                    mm(o, ff_h_t[q][:, t], w[:, c, d], False, False)
                    mm(o, ff_lo_t[q][:, t], hi[:, c, d], False, stop, signal=signal)

                if last:
                    pe.wait_ge(ff_h, q0 + 2)
                    for h in range(TB):
                        for e in range(2):
                            for c in range(2):
                                add(h, e, c, c == 1, ff_down if c else None)
                    owed[0] += 1
                    return
                for c in range(2):
                    pe.wait_ge(ff_h, q0 + c + 1 if i is None else i * 4 + (q0 + c + 1))
                    for h in range(TB):
                        for e in range(2):
                            add(h, e, c, False, w_free if c and h and e else None)

            def ffn(n):
                transposes(f"ffn{n}")
                transposed(f"ffn{n}")
                pe.wait_ge(xs_lo, 2 * SPLIT_NO[f"ffn{n}"] + 1 + n % 2)
                gate_up(n, 0)
                for s in range(2):
                    gate_up(n, s + 1)
                    down(n, s)
                with cur.loop(pe, (NSLAB - 3) // 2, 6) as i:
                    for s in range(2, 4):
                        gate_up(n, s + 1, i)
                        down(n, s, i)
                down(n, NSLAB - 1)

            def attention(n, Q_, K_, V_, bias=False):
                g = H * n
                for i in range(H + 3):
                    if i < H:
                        h = i
                        p0, pr = HD * (h % 2), h // 2
                        if g + h >= 4:
                            pe.wait_ge(at_sm, g + h - 3)
                        if bias:
                            pe.wait_ge(fx_aug, h + 1)
                        for t in range(TB):
                            n_s = P * (t + 1)
                            o = bank[h % 4][:, SEQ * t:SEQ * t + n_s]
                            mm(o, Q_[p0:p0 + HD, pr, t * P:(t + 1) * P], K_[p0:p0 + HD, pr, 0:n_s],
                               True, not bias, signal=at_s if t and not bias else None)
                            if bias:
                                mm(o, aug_l(h)[p0:p0 + 48, t * P:(t + 1) * P], aug_r[p0:p0 + 48, 0:n_s],
                                   False, True, signal=at_s if t else None)
                    if 2 <= i < H + 2:
                        h = i - 2
                        pe.wait_ge(at_p, g + h + 1)
                        if g + h >= 2:
                            pe.wait_ge(at_pt, g + h - 1)
                        for j, (t, s) in enumerate(((0, 0), (1, 0), (1, 1))):
                            mm(bank[4 + h % 2][:, j * P:(j + 1) * P], PR[h % 3][:, t * SEQ + s * P:t * SEQ + s * P + P],
                               ident, transpose=True, signal=at_t if j == 2 else None)
                    if i >= 3:
                        h = i - 3
                        pe.wait_ge(at_pt, g + h + 1)
                        if (g + h) // 2 >= 2 and h % 2 == 0:
                            pe.wait_ge(at_o, (g + h) // 2 - 1)
                        o = bank[6 + (h // 2) % 2][HD * (h % 2):HD * (h % 2) + HD, 0:SEQ]
                        mm(o, V_[:, 0, h * HD:(h + 1) * HD], PT[h % 2][:, 0:SEQ], True, False)
                        mm(o[:, P:SEQ], V_[:, 1, h * HD:(h + 1) * HD], PT[h % 2][:, SEQ:SEQ + P], False, True,
                           signal=at_pv)

            def attended(n):
                pe.wait_ge(at_o, H // 2 * (n + 1))

            def gather(n, i, half):
                for k in range(4 * half, 4 * half + 4):
                    for t in range(TB):
                        mm(bank[4 + half][:, (k % 4) * P:(k % 4 + 1) * P], Xn[:, t, k * P:(k + 1) * P], m_pack[:, t, :],
                           t == 0, t == TB - 1, signal=mo_x if k % 4 == 3 and t else None)

            def scatter():
                for t in range(TB):
                    for e in range(2):
                        mm(bank[4 + 2 * t + e][:, :], m_gT[:, t * P:(t + 1) * P], ye[:, e * BANK:(e + 1) * BANK],
                           signal=mo_s)

            def pair(n, i=None, first=False, last=False):
                def at(per, c):
                    return per * n + c if i is None else i * per + (per * n + c)

                pe.wait_ge(mo_xa, at(1, 1))
                pe.wait_ge(mo_xd, at(1, 1))
                for x in range(2):
                    for half in range(2):
                        s = [unit(), unit()]
                        for k in range(4):
                            for e in range(2):
                                w = ring[:, s[e], :].rearrange("p (k n) -> p k n", k=4)
                                kk = 4 * half + k
                                sig = None
                                if k == 3:
                                    sig = mo_gu if half and e else w_free
                                mm(bank[x][64 * e:64 * e + 64, :], XeT[:, kk, 64 * e:64 * e + 64], w[:, k, :],
                                   kk == 0, kk == KC - 1, signal=sig)
                    owed[0] += 1
                if not first:
                    pe.wait_ge(mo_ye, at(2, 0))
                    pe.wait_ge(mo_gte, at(1, 0))
                    scatter()
                if not last:
                    if not first:
                        pe.wait_ge(mo_acc, at(4, -3))
                    pe.wait_ge(mo_sel, at(1, 2))
                    gather(n, i, 0)
                if not first:
                    pe.wait_ge(mo_acc, at(4, -1))
                pe.wait_ge(mo_h, at(1, 1))
                for c in range(4):
                    mm(bank[6][:, c * P:(c + 1) * P], m_h[:, c * P:(c + 1) * P], ident, transpose=True,
                       signal=mo_ht if c == 3 else None)
                if not last:
                    gather(n, i, 1)
                if not first:
                    pe.wait_ge(mo_acc, at(4, 0))
                pe.wait_ge(mo_g, at(1, 1))
                for t in range(TB):
                    mm(bank[7][:, t * P:(t + 1) * P], m_gate[:, t, :], ident, transpose=True,
                       signal=mo_gt if t else None)
                pe.wait_ge(mo_hte, at(1, 1))
                for half in range(2):
                    s = [unit(), unit()]
                    for c in range(2):
                        for j in range(2):
                            for e in range(2):
                                w = ring[:, s[e], :].rearrange("p (c n) -> p c n", c=2)
                                cc = 2 * half + c
                                sig = None
                                if c and j:
                                    sig = mo_y if half and e else w_free
                                mm(bank[2 + j][64 * e:64 * e + 64, :],
                                   m_hT[:, cc * P + 64 * e:cc * P + 64 * e + 64], w[:, c, j * BANK:(j + 1) * BANK],
                                   cc == 0, cc == 3, signal=sig)
                owed[0] += 1

            def unpacked(l, i):
                pe.wait_ge(ov_step[l], i + 1)
                pe.wait_ge(ov_landed[l], i * 96 + 96)
                for t in range(TB):
                    for x in range(2):
                        for kk in range(KC):
                            w = ring[:, 2 * x + kk // 4, :].rearrange("p (k n) -> p k n", k=4)
                            ins = pe.matmul(bank[2 * t + x][:, :], xt[:, kk, t * P:(t + 1) * P], w[:, kk % 4, :],
                                            start=kk == 0, stop=kk == KC - 1, skip_group_check=True)
                    ins.then_inc(ov_gu[l], 1)
                for t in range(TB):
                    pe.wait_ge(ov_act[l], i * 2 + (t + 1))
                    for c in range(4):
                        ins = pe.transpose(bank[4 + t][:, c * P:(c + 1) * P], ov_h[t][:, c * P:(c + 1) * P], ident)
                    ins.then_inc(ov_t[l], 1)
                for t in range(TB):
                    pe.wait_ge(ov_te[l], i * 2 + (t + 1))
                    if t:
                        pe.wait_ge(ov_acc[l], i * 2 + 1)
                    for j in range(2):
                        for c in range(4):
                            w = ring[:, 4 + c // 2, :].rearrange("p (c n) -> p c n", c=2)
                            ins = pe.matmul(bank[6 + j][:, :], ov_hT[t][:, c * P:(c + 1) * P],
                                            w[:, c % 2, j * BANK:(j + 1) * BANK], start=c == 0, stop=c == 3,
                                            skip_group_check=True)
                    ins.then_inc(ov_y[l], 1)

            def moe(l):
                transposes(f"moe{l}")
                transposed(f"moe{l}")
                wait_taken(pe, PROJ_AT[("wo_r", "wo_f")[l]] + 1)
                pe.wait_ge(rt_landed, 48 * (l + 1))
                for t in range(TB):
                    for k in range(KC):
                        mm(bank[t][:, 0:N_RT], xt[:, k, t * P:(t + 1) * P], rt_w[:, k, :], k == 0, k == KC - 1,
                           signal=rt_pe if t and k == KC - 1 else None)
                pe.wait_ge(rt_dve, 3 * l + 3)
                up = cst("upto", TB, SEQ)
                mm(bank[2][:, 0:N_EXP], up[:, 0, 0:P], rt_sel[:, 0, :])
                mm(bank[2][:, N_EXP:2 * N_EXP], up[:, 0, P:SEQ], rt_sel[:, 0, :], True, False)
                mm(bank[2][:, N_EXP:2 * N_EXP], up[:, 1, P:SEQ], rt_sel[:, 1, :], False, True)
                mm(bank[2][0:1, 2 * N_EXP:3 * N_EXP], up[:, 0, SEQ - 1:SEQ], rt_sel[:, 0, :], True, False)
                mm(bank[2][0:1, 2 * N_EXP:3 * N_EXP], up[:, 1, SEQ - 1:SEQ], rt_sel[:, 1, :], False, True, signal=rt_pe)
                n = PAIRS * l
                pe.wait_ge(mo_sel, n + 1)
                gather(n, None, 0)
                gather(n, None, 1)
                pair(n, first=True)
                with cur.loop(pe, PAIRS - 2, 12) as i:
                    pair(n + 1, i)
                pair(n + PAIRS - 1, last=True)
                pe.wait_ge(mo_ye, 2 * (n + PAIRS))
                pe.wait_ge(mo_gte, n + PAIRS)
                scatter()
                with overflowed(pe, l):
                    with pe.Fori(0, N_EXP) as i:
                        unpacked(l, i)

            def low_rank():
                s1, landed, _ = cur.take(3)
                pe.wait_ge(w_landed[s1], landed)
                sg1, landed, _ = cur.take()
                pe.wait_ge(w_landed[sg1], landed)
                s3, landed, _ = cur.take(2)
                pe.wait_ge(w_landed[s3], landed)
                s4 = unit()
                w1 = ring[:, s1, 0:512].rearrange("p (k n) -> p k n", k=KC)
                a1 = ring[:, s1, 512:1024].rearrange("p (k n) -> p k n", k=KC)
                g1 = ring[:, sg1, 0:1280].rearrange("p (k n) -> p k n", k=KC)

                def hidden(n, o, w):
                    for k in range(KC):
                        mm(o, w(k), xi[n % 2][:, k, :], k == 0, k == KC - 1, signal=lo_pe if k == KC - 1 else None)

                def expand(name, parts):
                    for j in range(2):
                        b = PROJ_AT[name] + j
                        wait_taken(pe, b - 2)
                        for h in range(TB):
                            for n, (x, w) in enumerate(parts):
                                mm(bank[2 * (b % 2) + h][:, :], x[:, h * P:(h + 1) * P],
                                   w[:, j * BANK:(j + 1) * BANK], n == 0, n == len(parts) - 1,
                                   signal=pj_pe if n == len(parts) - 1 else None)

                pe.wait_ge(xi_set, 4)
                hidden(3, bank[4][0:64, 0:SEQ], lambda k: w1[:, k, :])
                pe.wait_ge(xi_set, 5)
                hidden(4, bank[5][0:64, 0:SEQ], lambda k: a1[:, k, :])
                pe.wait_ge(lo_act, 1)
                expand("lora_w", [(lo[0:64, 0:SEQ], ring[0:64, s1, 1024:2048])])
                owed[0] += 1
                pe.wait_ge(xi_set, 6)
                hidden(5, bank[6][:, 0:SEQ], lambda k: g1[:, k, 0:P])
                hidden(5, bank[7][0:32, 0:SEQ], lambda k: g1[:, k, P:P + 32])
                owed[0] += 1
                pe.wait_ge(lo_act, 2)
                expand("lora_a", [(lo[0:64, SEQ:2 * SEQ], ring[0:64, s3, 0:1024])])
                return s3, s4

            def rk_transposes(t):
                pe.wait_ge(rk_in, t + 1)
                if t:
                    for g in (2, 3):
                        rk_wait(pe, "dve", g, "yb")
                        rk_wait(pe, "act", g, "u0")
                for x, (s0, s1) in enumerate(((rKK, rR), (rA, rK))):
                    if t == 0:
                        pe.wait_ge(lg_act, 4)
                    for b in range(4):
                        for r in (2 * b, 2 * b + 1):
                            for y, src in enumerate((s0, s1)):
                                c = (r % 2) * SEQ + y * P
                                mm(bank[4 * x + b][:, c:c + P], src[:, t, r * P:(r + 1) * P], ident, transpose=True,
                                   signal=wt_pe if r % 2 and y else None)
                pe.wait_ge(wt_act, 4 * t + 4)
                pe.wait_ge(wt_dve, 4 * t + 4)

            def rk_bank(g, x):
                return bank[4 * (g % 2) + x]

            def four(g, x, lhs, rhs, sig):
                for i in range(4):
                    c = slice(i * P, (i + 1) * P)
                    mm(rk_bank(g, x)[:, c], rk_t[g % 2][lhs][:, c], rk_t[g % 2][rhs][:, c],
                       signal=rk_pe[g % 2] if i == 3 else None)

            def tall(o, c, c0, lhs, i, rhs, signal):
                mm(o[HD * c:HD * c + HD, c0:c0 + HD], lhs[:, i * P + HD * c:i * P + HD * c + HD], rhs, signal=signal)

            def need(g, dve=None, act=None):
                if dve:
                    rk_wait(pe, "dve", g, dve)
                if act:
                    rk_wait(pe, "act", g, act)

            def s_ab(g):
                if g >= 2 and g != 4 and g != 5:
                    need(g - 2, "yb", "u0")
                for i, par, pp, r, h in rk_heads(g):
                    q = slice(HD * par, HD * par + HD)
                    mm(rk_bank(g, par)[:, pp * P:(pp + 1) * P], AR[q, r, 0, :], BK[q, r, 0, :],
                       signal=rk_pe[g % 2] if i == 3 else None)
                for i, par, pp, r, h in rk_heads(g):
                    q = slice(HD * par, HD * par + HD)
                    mm(rk_bank(g, 2 + par)[:, pp * SEQ:(pp + 1) * SEQ], BK[q, r, 0, :],
                       AR[q, r, :, :].rearrange("p x t -> p (x t)"), signal=rk_pe[g % 2] if i == 3 else None)

            def s_k(g):
                need(g, dve="de")
                for i, par, pp, r, h in rk_heads(g):
                    q = slice(HD * par, HD * par + HD)
                    mm(rk_bank(g, par)[:, pp * SEQ:(pp + 1) * SEQ], BK[q, r, 1, :],
                       AR[q, r, :, :].rearrange("p x t -> p (x t)"), signal=rk_pe[g % 2] if i == 3 else None)

            def s_ny(g):
                need(g, dve="mk")
                for c in range(2):
                    for x, tile in enumerate((5, 6)):
                        for i, par, pp, r, h in rk_heads(g):
                            tall(rk_bank(g, 2), c, x * SEQ + i * HD, rk_t[g % 2][tile], i,
                                 rV[:, g // 4, h * HD:(h + 1) * HD], rk_pe[g % 2] if c and x and i == 3 else None)

            def s_d2(g):
                four(g, 0, 1, 0, True)
                four(g, 1, 0, 1, True)

            def s_d4(g):
                need(g, "d2", "d2t")
                four(g, 0, 4, 3, True)
                four(g, 1, 3, 4, True)

            def s_d8(g):
                need(g, "d4t", "d4")
                four(g, 3, 6, 5, True)

            def s_at(g):
                need(g, "d2i", "ny")
                four(g, 0, 3, 1, True)
                need(g, "d4ti")
                four(g, 1, 6, 7, True)

            def s_t16(g):
                need(g, "at", "b")
                four(g, 2, 4, 0, True)
                four(g, 3, 0, 4, True)

            def s_f(g):
                need(g, "t16t", "t16")
                four(g, 0, 5, 2, True)
                four(g, 1, 2, 5, True)

            def s_f2(g):
                need(g, "f", "ft")
                four(g, 2, 3, 1, True)

            def s_gt(g):
                need(g, "fti")
                four(g, 0, 0, 3, True)

            def s_tt(g):
                need(g, act="gt")
                four(g, 1, 7, 4, True)

            def s_uw(g):
                need(g, "tt", "ny")
                tt = rk_t[g % 2][2]
                for c in range(2):
                    for i in range(4):
                        tall(rk_bank(g, 2), c, i * HD, tt, i, rk_n[g % 2][:, i * HD:(i + 1) * HD],
                             rk_pe[g % 2] if c and i == 3 else None)
                for i, par, pp, r, h in rk_heads(g):
                    mm(rk_bank(g, 3)[HD * par:HD * par + HD, pp * P:(pp + 1) * P],
                       rKK[:, g // 4, h * HD:(h + 1) * HD], tt[:, i * P:(i + 1) * P],
                       signal=rk_pe[g % 2] if i == 3 else None)

            def s_u(c):
                def step(g):
                    need(g, "z_0" if c else "w1", "u0")
                    if g >= 4 and c == 0:
                        need(g - 4, "z_1")
                    t = slice(CH * c, CH * c + CH)
                    for par in range(2):
                        for x in range(2):
                            for pp in range(2):
                                r, q = 2 * (g % 4) + pp, slice(HD * par, HD * par + HD)
                                lhs = AR[q, r, 1, t] if x else rk_t[g % 2][6][q, SEQ + pp * P + CH * c:SEQ + pp * P + CH * c + CH]
                                mm(rk_bank(g, par)[t, x * P + pp * HD:x * P + (pp + 1) * HD], lhs, Z[q, r, :],
                                   signal=rk_pe[g % 2] if par and x and pp else None)
                return step

            def s_z(c):
                def step(g):
                    need(g, f"u_{c}")
                    t = slice(CH * c, CH * c + CH)
                    for i, par, pp, r, h in rk_heads(g):
                        o = rk_bank(g, 2)[HD * par:HD * par + HD, pp * HD:(pp + 1) * HD]
                        hc = slice(h * HD, (h + 1) * HD)
                        mm(o, rA[t, g // 4, hc], rk_t[g % 2][5][t, i * HD:(i + 1) * HD], True, False)
                        mm(o, rK[t, g // 4, hc], rV[t, g // 4, hc], False, True,
                           signal=rk_pe[g % 2] if i == 3 else None)
                return step

            def s_yb(g):
                for c in range(2):
                    for i in range(4):
                        tall(rk_bank(g, 3), c, i * HD, rk_t[g % 2][8], i, rk_t[g % 2][5][:, i * HD:(i + 1) * HD],
                             rk_pe[g % 2] if c and i == 3 else None)

            rk_steps = [s_ab, s_k, s_ny, s_d2, s_d4, s_d8, s_at, s_t16, s_f, s_f2, s_gt, s_tt, s_uw,
                        s_u(0), s_z(0), s_u(1), s_z(1), s_yb]

            pe.wait_ge(in_landed, 48)
            ffn(0)
            pe.wait_ge(const_landed, 16)
            transposes("mix_a")
            transposed("mix_a")
            project_split("qkv_a")
            transposes("q_a")
            transposes("k_a")
            transposed("k_a")
            wait_taken(pe, PROJ_AT["qkv_a"] + 5)
            attention(0, QT, KT, V)
            attended(0)
            project("wo_a", tokens_of(OT))
            ffn(1)
            transposes("kv")
            transposed("kv")
            project_split("kv_b")
            transposes("k_b")
            ffn(2)
            transposes("mix_b")
            transposed("mix_b")
            project_split("q_b")
            transposes("q_b")
            transposed("q_b")
            attention(1, QT, KT, V)
            attended(1)
            project("wo_b", tokens_of(OT))
            ffn(3)
            transposes("mix_r")
            transposed("mix_r")
            for n, name in enumerate(("rwkv_r", "rwkv_k", "rwkv_v")):
                pe.wait_ge(xi_set, n + 1)
                project(name, tokens_of(xi[n % 2]))
            s3, s4 = low_rank()
            pe.wait_ge(rk_f, 1)
            wait_taken(pe, PROJ_AT["lora_a"] + 1)
            for h in range(TB):
                for j in range(2):
                    mm(bank[2 * h + j][:, :], cst("decay_upto"), rS[:, h, j * BANK:(j + 1) * BANK],
                       signal=rk_c if h and j else None)
            for h in range(TB):
                for k in range(KC):
                    mm(bank[4][:, 4 * k + 2 * h:4 * k + 2 * h + 2], rS[:, h, k * P:(k + 1) * P], cst("decay_of"),
                       signal=rk_c if h and k == KC - 1 else None)
            pe.wait_ge(lo_act, 4)
            for n, (j, h) in enumerate(((0, 0), (0, 1), (1, 0), (1, 1))):
                if n == 3:
                    pe.wait_ge(rk_f, 4)
                o, t = bank[(5, 6, 7, 4)[n]][:, :], slice(h * P, h * P + P)
                mm(o, lo[:, 2 * SEQ:3 * SEQ][:, t], ring[:, s3, 1024 + j * BANK:1024 + (j + 1) * BANK], True, False)
                mm(o, lo[0:32, 3 * SEQ:4 * SEQ][:, t], ring[0:32, s4, j * BANK:(j + 1) * BANK], False, True,
                   signal=lg_pe)
            owed[0] += 2
            for duo in range(4):
                if duo % 2 == 0:
                    rk_transposes(duo // 2)
                for step in rk_steps:
                    for g in (2 * duo, 2 * duo + 1):
                        step(g)
            for g in (6, 7):
                rk_wait(pe, "dve", g, "yb")
            transposes("y_r")
            transposed("y_r")
            project("wo_r", tokens_of(xt))
            moe(0)
            pe.wait_ge(mo_acc, 4 * PAIRS)
            transposes("kv_f")
            transposed("kv_f")
            project_split("kv_f")
            b = PROJ_AT["forget"]
            wait_taken(pe, b - 2)
            pe.wait_ge(fx_landed, 64)
            for h in range(TB):
                for k in range(KC):
                    t = slice(h * P, (h + 1) * P)
                    mm(bank[2 * (b % 2) + h][:, 0:H], f32(xt_r[:, k, t]), fx_w[:, k, :], k == 0, False)
                    mm(bank[2 * (b % 2) + h][:, 0:H], f32(x_lo(k)[:, t]), fx_w[:, k, :], False, k == KC - 1,
                       signal=pj_pe if k == KC - 1 else None)
            transposes("mix_f")
            transposed("mix_f")
            project_split("qg_f")
            transposes("k_f")
            pe.wait_ge(fx_z1, 2)
            wait_taken(pe, PROJ_AT["qg_f"] + 3)
            mm(bank[2][0:112, 0:SEQ], fx_ls[:, 0, :], cst("upto", TB, SEQ)[:, 0, :], True, False)
            mm(bank[2][0:112, 0:SEQ], fx_ls[:, 1, :], cst("upto", TB, SEQ)[:, 1, :], False, True, signal=fx_pe)
            pe.wait_ge(fx_z1, 3)
            transposes("q_f")
            transposes("g_f")
            transposed("g_f")
            attention(2, QT, KT, fV, bias=True)
            attended(2)
            project("wo_f", tokens_of(OT))
            moe(1)

        @block.scalar
        def _(act):
            def transposes(name, dst, gain_name=None):
                n = TRANS_AT[name]
                for b in range(2):
                    act.wait_ge(tr_pe, 4 * n + b + 1)
                    if gain_name:
                        for k in (2 * b, 2 * b + 1):
                            ins = act.activation(dst[:, k, :], bank[4 + b][:, (k % 2) * SEQ:(k % 2 + 1) * SEQ],
                                                 ACT.Copy, scale=gain(gain_name, k))
                    else:
                        ins = act.activation(dst[:, 2 * b:2 * b + 2, :], pair_of(bank[4 + b]), ACT.Copy)
                    ins.then_inc(tr_act, 1)

            def mod_row(r):
                for b in range(4):
                    act.wait_ge(mod_pe, 4 * r + b + 1)
                    if b == 0:
                        act.wait_ge(mod_pe, 4 * r + 4)
                    act.activation(mod_acc[r % 2][0:1, b * BANK:(b + 1) * BANK], bank[4 + b][0:1, :], ACT.Copy)\
                       .then_inc(mod_take, 1)
                act.wait_ge(mod_take, 4 * r + 4)
                act.dma_start(mods[r:r + 1, :], mod_acc[r % 2][0:1, :]).then_inc(mod_out[r % 2], 16)

            def root(n):
                act.wait_ge(rms_ms, n + 1)
                act.activation(rms_r[n % 2], rms_m[n % 2], ACT.Sqrt).then_inc(rms_root, 1)
                if n < len(NORMED):
                    act.wait_ge(nm_inv, n + 1)
                    act.activation(Xn[:, 1, :], X[:, 1, :], ACT.Copy, scale=rms_i[n % 2][:, 1:2]).then_inc(nm_act, 1)

            def take(name, dst, blocks=None):
                first = PROJ_AT[name]
                for j in blocks or range(PROJ_N[name]):
                    for h in range(TB):
                        act.wait_ge(pj_pe, PROJ_DONE[first + j] + h + 1)
                        act.activation(dst(j, h), bank[2 * ((first + j) % 2) + h][:, :], ACT.Copy).then_inc(pj_act, 1)

            def columns(*bufs):
                return lambda j, h: bufs[j // 2][:, h, (j % 2) * BANK:(j % 2 + 1) * BANK]

            cur = Cursor()

            def skip(n):
                for _ in range(n):
                    cur.take()

            def split(hi, back=None):
                slot, landed, pos = cur.take()
                act.wait_ge(w_landed[slot], landed)
                if back:
                    act.wait_ge(w_free, pos - back + R)
                act.activation(hi, ring[:, slot, :], ACT.Copy).then_inc(sp_hi, 1)

            def silu(n, i):
                act.wait_ge(ff_gu, n + 1 if i is None else i * 4 + (n + 1))
                if n >= 2:
                    act.wait_ge(ff_h, n - 1 if i is None else i * 4 + (n - 1))
                act.activation(ff_silu_t[n % 2], bank[4 + n % 4][:, 0:SEQ], ACT.Silu).then_inc(ff_silu, 1)

            def slab(n, s, i=None):
                q = 2 * (NSLAB * n + s)
                if s:
                    split(hi_down(s - 1), 3)
                if s + 1 < NSLAB:
                    split(hi_gate(s + 1))
                silu(q, i)
                if s + 1 < NSLAB:
                    split(hi_up(s + 1))
                silu(q + 1, i)

            def take_split(name, dst):
                n = PROJ_N[name]
                for j in range(n):
                    if j == 0:
                        split(hi_proj(1), 2)
                    if j + 1 < n:
                        split(hi_proj(0), 2)
                    take(name, dst, blocks=(j,))
                    if j + 1 < n:
                        split(hi_proj(1), 2)

            def ffn_first():
                split(hi_gate(0))
                split(hi_up(0))

            def ffn(n):
                act.wait_ge(tr_pe, 4 * TRANS_AT[f"ffn{n}"] + 4)
                slab(n, 0)
                with cur.loop(act, (NSLAB - 3) // 2, 6) as i:
                    slab(n, 1, i)
                    slab(n, 2, i)
                slab(n, NSLAB - 2)
                slab(n, NSLAB - 1)
                split(hi_down(NSLAB - 1))

            def attention(n, take_out=True):
                g = H * n
                for i in range(H + 4):
                    if i < H:
                        h = i
                        act.wait_ge(at_nb, g + h + 1)
                        for t in range(TB):
                            v = PR[h % 3][:, t * SEQ:t * SEQ + P * (t + 1)]
                            act.activation(v, v, ACT.Exp, bias=at_bias[h % 3][:, t:t + 1], scale=HD ** -0.5,
                                           accum_out=at_sum[h % 3][:, t:t + 1]).then_inc(at_e, 1)
                    if 2 <= i < H + 2:
                        h = i - 2
                        act.wait_ge(at_t, g + h + 1)
                        if h >= 2:
                            act.wait_ge(at_pv, g + h - 1)
                        act.activation(PT[h % 2], bank[4 + h % 2][:, 0:3 * P], ACT.Copy).then_inc(at_pt, 1)
                    if take_out and i >= 4 and i % 2 == 1:
                        r = (i - 4) // 2
                        act.wait_ge(at_pv, g + 2 * r + 2)
                        act.activation(OT[:, r, :], bank[6 + r % 2][:, 0:SEQ], ACT.Copy).then_inc(at_o, 1)

            def moe(l):
                transposes(f"moe{l}", xt)
                for n in range(2):
                    act.wait_ge(rt_dve, 3 * l + n + 1)
                    for t in range(TB):
                        if n == 0:
                            ins = act.activation(rt_ex[:, t, :], rt_l[:, t, 0:N_GRP], ACT.Exp, bias=rt_nm[:, t:t + 1],
                                                 accum_out=rt_sum[:, t:t + 1])
                        else:
                            ins = act.activation(rt_e2[:, t:t + 1], rt_em[:, t, 1:2], ACT.Exp,
                                                 bias=rt_nm[:, 2 + t:3 + t])
                    ins.then_inc(rt_act, 1)

                def pair(n, i=None, last=False):
                    def at(per, c):
                        return per * n + c if i is None else i * per + (per * n + c)

                    act.wait_ge(mo_gu, at(2, 1))
                    act.activation(m_sg, bank[0][:, :], ACT.Silu).then_inc(mo_silu, 1)
                    if not last:
                        act.wait_ge(mo_x, at(2, 3))
                        act.activation(XeT[:, 0:4, :].rearrange("p k s -> p (k s)"), bank[4][:, :], ACT.Copy)\
                           .then_inc(mo_xa, 1)
                    act.wait_ge(mo_ht, at(1, 1))
                    act.activation(m_hT, bank[6][:, :], ACT.Copy).then_inc(mo_hte, 1)
                    act.wait_ge(mo_gt, at(1, 1))
                    act.activation(m_gT, bank[7][:, 0:SEQ], ACT.Copy).then_inc(mo_gte, 1)
                    act.wait_ge(mo_y, at(1, 1))
                    for j in range(2):
                        act.activation(ye[:, j * BANK:(j + 1) * BANK], bank[2 + j][:, :], ACT.Copy).then_inc(mo_ye, 1)

                n = PAIRS * l
                act.wait_ge(mo_x, 2 * n + 1)
                act.activation(XeT[:, 0:4, :].rearrange("p k s -> p (k s)"), bank[4][:, :], ACT.Copy).then_inc(mo_xa, 1)
                pair(n)
                with act.Fori(0, PAIRS - 2) as i:
                    pair(n + 1, i)
                pair(n + PAIRS - 1, last=True)
                with overflowed(act, l):
                    act.wait_ge(ov_step[l], 1)
                    with act.Fori(0, N_EXP) as i:
                        for t in range(TB):
                            act.wait_ge(ov_gu[l], i * 2 + (t + 1))
                            act.activation(ov_h[t], bank[2 * t][:, :], ACT.Silu).then_inc(ov_silu[l], 1)
                        for t in range(TB):
                            act.wait_ge(ov_t[l], i * 2 + (t + 1))
                            act.activation(ov_hT[t], bank[4 + t][:, :], ACT.Copy).then_inc(ov_te[l], 1)

            act.wait_ge(in_landed, 48)
            act.activation(cs, cs, ACT.Silu).then_inc(cs_set, 1)
            root(0)
            transposes("ffn0", xt_r, "ffn1_0")
            ffn_first()
            ffn(0)
            split(hi_proj(0), 2)
            mod_row(0)
            root(1)
            transposes("mix_a", xt_r, "mix_0")
            take_split("qkv_a", columns(Q, K, V))
            mod_row(1)
            transposes("q_a", QT)
            transposes("k_a", KT)
            attention(0)
            skip(4)
            ffn_first()
            mod_row(2)
            root(2)
            transposes("ffn1", xt_r, "ffn2_0")
            ffn(1)
            split(hi_proj(0), 2)
            mod_row(3)
            root(3)
            transposes("kv", xt_r, "kv")
            take_split("kv_b", columns(K, V))
            transposes("k_b", KT)
            root(4)
            act.wait_ge(tr_pe, 4 * TRANS_AT["k_b"] + 4)
            ffn_first()
            transposes("ffn2", xt_r, "ffn1_1")
            ffn(2)
            split(hi_proj(0), 2)
            mod_row(4)
            root(5)
            transposes("mix_b", xt_r, "mix_1")
            take_split("q_b", columns(Q))
            transposes("q_b", QT)
            attention(1)
            skip(4)
            ffn_first()
            mod_row(5)
            root(6)
            transposes("ffn3", xt_r, "ffn2_1")
            ffn(3)
            mod_row(6)
            root(7)
            transposes("mix_r", xt)
            take("rwkv_r", columns(rR))
            take("rwkv_k", columns(rK))
            take("rwkv_v", columns(rV))
            for n, (o, i, f) in enumerate(((lo[0:64, 0:SEQ], bank[4][0:64, 0:SEQ], ACT.Tanh),
                                           (lo[0:64, SEQ:2 * SEQ], bank[5][0:64, 0:SEQ], ACT.Copy),
                                           (lo[:, 2 * SEQ:3 * SEQ], bank[6][:, 0:SEQ], ACT.Sigmoid),
                                           (lo[0:32, 3 * SEQ:4 * SEQ], bank[7][0:32, 0:SEQ], ACT.Sigmoid))):
                act.wait_ge(lo_pe, n + 1)
                act.activation(o, i, f).then_inc(lo_act, 1)
            act.wait_ge(rk_z, 1)
            act.activation(rS[:], rS[:], ACT.Sigmoid).then_inc(rk_f, 1)
            act.wait_ge(rk_z, 2)
            act.activation(rA[:], rA[:], ACT.Sigmoid).then_inc(rk_f, 1)
            act.wait_ge(rk_z, 3)
            act.activation(hs_root, hs_sum, ACT.Sqrt).then_inc(rk_f, 1)
            act.wait_ge(rk_c, 2)
            act.activation(pct[:].rearrange("p k c -> p (k c)"), bank[4][:, 0:32], ACT.Exp).then_inc(rk_f, 1)
            for h in range(TB):
                for n, sc in enumerate((1.0, -1.0)):
                    for j in range(2):
                        act.activation(rE[n][:, h, j * BANK:(j + 1) * BANK], bank[2 * h + j][:, :], ACT.Exp,
                                       scale=sc).then_inc(rk_f, 1)
            for h in range(TB):
                act.wait_ge(rk_z, 4 + h)
                act.activation(rE[2][:, h, :], rE[2][:, h, :], ACT.Exp).then_inc(rk_f, 1)
            for n, (j, h) in enumerate(((0, 0), (0, 1), (1, 0), (1, 1))):
                act.wait_ge(lg_pe, n + 1)
                act.activation(rG[:, h, j * BANK:(j + 1) * BANK], bank[(5, 6, 7, 4)[n]][:, :], ACT.Copy)\
                    .then_inc(lg_act, 1)

            def rk_copy(g, name, dst, x, cols=slice(0, BANK), on=None):
                rk_wait(act, "pe", g, on or name)
                return act.activation(dst, bank[4 * (g % 2) + x][:, cols], ACT.Copy)

            def rk_step(name, tile, x):
                def step(g):
                    rk_copy(g, name, rk_t[g % 2][tile], x).then_inc(rk_act[g % 2], 1)
                return step

            def rk_ny(g):
                rk_wait(act, "pe", g, "ny")
                act.activation(rk_n[g % 2], bank[4 * (g % 2) + 2][:, 0:SEQ], ACT.Copy)
                for par in range(2):
                    v = bank[4 * (g % 2) + 2][:, SEQ + 2 * HD * par:SEQ + 2 * HD * (par + 1)]
                    ins = act.activation(rk_cols(rR, g, par), v.rearrange("p (a d) -> p a d", a=2), ACT.Copy)
                ins.then_inc(rk_act[g % 2], 1)

            def rk_u0(g):
                rk_wait(act, "pe", g, "u0")
                act.activation(rk_t[g % 2][6][:, 0:SEQ], bank[4 * (g % 2) + 2][:, 0:SEQ], ACT.Copy)\
                   .then_inc(rk_act[g % 2], 1)

            for duo in range(4):
                if duo % 2 == 0:
                    for b in range(4):
                        act.wait_ge(wt_pe, 8 * (duo // 2) + b + 1)
                        act.activation(AR[:, 2 * b:2 * b + 2, :, :].rearrange("p r x t -> p (r x t)"), bank[b][:, :],
                                       ACT.Copy).then_inc(wt_act, 1)
                for step in (rk_ny, rk_step("d2t", 4, 1), rk_step("d4", 5, 0), rk_step("b", 4, 1),
                             rk_step("t16", 7, 3), rk_step("ft", 3, 1), rk_step("gt", 4, 0), rk_u0):
                    for g in (2 * duo, 2 * duo + 1):
                        step(g)
            act.wait_ge(gn_var, 1)
            n = quarter(3)[2]
            act.activation(hs_root[:, n:n + 8], hs_sum[:, n:n + 8], ACT.Sqrt).then_inc(gn_root, 1)
            transposes("y_r", xt)
            root(8)
            moe(0)
            root(9)
            cur.skip_second_trunk()
            split(hi_proj(0))
            transposes("kv_f", xt_r)
            take_split("kv_f", columns(fK, fV))
            transposes("mix_f", xt_r)
            split(hi_proj(0))
            split(hi_proj(1))
            act.wait_ge(fx_z1, 1)
            act.activation(fx_z[1], fx_z[1], ACT.Exp, scale=-1.0).then_inc(fx_act, 1)
            act.wait_ge(fx_act, 1)
            act.activation(fx_z[1], fx_z[1], ACT.Ln, bias=1.0).then_inc(fx_act, 1)
            act.wait_ge(rk_z, 6)
            act.activation(hs_root, hs_sum, ACT.Sqrt).then_inc(rk_f, 1)
            split(hi_proj(0), 2)
            take("qg_f", columns(fQ), blocks=(0,))
            split(hi_proj(1), 2)
            split(hi_proj(0), 2)
            take("qg_f", columns(fQ), blocks=(1,))
            split(hi_proj(1), 2)
            act.wait_ge(rk_z, 7)
            act.activation(hs_root, hs_sum, ACT.Sqrt).then_inc(rk_f, 1)
            split(hi_proj(0), 2)
            take("qg_f", columns(fQ, fG), blocks=(2,))
            split(hi_proj(1), 2)
            take("qg_f", columns(fQ, fG), blocks=(3,))
            act.wait_ge(pj_act, PROJ_TAKES[PROJ_AT["qg_f"] + 3][1])
            act.activation(fG[:], fG[:], ACT.Sigmoid).then_inc(fx_act, 1)
            transposes("k_f", KT)
            transposes("q_f", QT)
            transposes("g_f", fGT)
            attention(2, take_out=False)
            root(10)
            moe(1)
            root(11)

        @block.vector
        def _(dve):
            ch = Chain(dve, dve_chain)
            link = ch.link

            def row(name):
                n = ROWS.index(name)
                dve.wait_ge(row_landed[n % NROW], 16 * (n // NROW + 1))
                return bc[n % NROW]

            def row_done(ins, name):
                n = ROWS.index(name)
                ins.then_inc(row_free[n % NROW], 1)
                dve.wait_ge(row_free[n % NROW], n // NROW + 1)

            def modulate(tag):
                sc = row("sc_" + tag)
                for h in range(TB):
                    ins = dve.scalar_tensor_tensor(out=Xn[:, h, :], in0=sc, scalar=1.0, in1=X[:, h, :],
                                                   op0=ALU.add, op1=ALU.mult)
                row_done(ins, "sc_" + tag)
                sh = row("sh_" + tag)
                for h in range(TB):
                    ins = dve.tensor_tensor(Xn[:, h, :], Xn[:, h, :], sh, ALU.add)
                row_done(ins, "sh_" + tag)
                dve.engine_nop().then_inc(tr_src, 1)

            def layer_norm(n, tag, Y_, proj=None, mod=None, trans=None):
                gt = row("gt_" + tag)
                st = tiny(64, 24).rearrange("p (h j s) -> p h j s", h=TB, j=2)
                mv = tiny(88, 4).rearrange("p (h s) -> p h s", h=TB)
                for j in range(2):
                    c = slice(j * BANK, (j + 1) * BANK)
                    for h in range(TB):
                        if proj:
                            b = PROJ_AT[proj] + j
                            dve.wait_ge(pj_pe, PROJ_DONE[b] + h + 1)
                            dve.scalar_tensor_tensor(out=Y_[:, h, c], in0=gt[:, c], scalar=1.0,
                                                     in1=bank[2 * (b % 2) + h][:, :], op0=ALU.add, op1=ALU.mult)\
                                .then_inc(pj_dve, 1)
                            dve.wait_ge(pj_dve, PROJ_TAKES[b][1] - TB + h + 1)
                        else:
                            link(dve.scalar_tensor_tensor(out=Y_[:, h, c], in0=gt[:, c], scalar=1.0, in1=Y_[:, h, c],
                                                          op0=ALU.add, op1=ALU.mult))
                        link(dve.scalar_tensor_tensor(out=X[:, h, c], in0=X[:, h, c], scalar=ALPHA, in1=Y_[:, h, c],
                                                      op0=ALU.mult, op1=ALU.add))
                        ins = dve.bn_stats(st[:, h, j, :], X[:, h, c])
                row_done(ins, "gt_" + tag)
                for h in range(TB):
                    ins = dve.bn_aggr(mv[:, h, :], st[:, h, :, :].rearrange("p j s -> p (j s)"))
                link(ins)
                k = 8 + n
                dve.tensor_scalar(rms_m[k % 2], mv[:, :, 1], LN_EPS, None, ALU.add).then_inc(rms_ms, 1)
                dve.wait_ge(rms_root, k + 1)
                link(dve.reciprocal(rms_i[k % 2], rms_r[k % 2]))
                for h in range(TB):
                    ins = dve.tensor_scalar(X[:, h, :], X[:, h, :], mv[:, h, 0:1], rms_i[k % 2][:, h:h + 1],
                                            ALU.subtract, ALU.mult)
                link(ins)
                if mod:
                    dve.wait_ge(row_mixed, n + 1)
                    sc, sh = row("sc_" + mod), row("sh_" + mod)
                    for h in range(TB):
                        ins = dve.tensor_tensor(Xn[:, h, :], X[:, h, :], sc, ALU.mult)
                    row_done(ins, "sc_" + mod)
                    for h in range(TB):
                        ins = dve.tensor_tensor(Xn[:, h, :], Xn[:, h, :], sh, ALU.add)
                    ins.then_inc(tr_src, 1)
                    dve.wait_ge(tr_src, TRANS_AT[trans] + 1)
                    dve.sem_inc(row_free[ROWS.index("sh_" + mod) % NROW], 1)

            def norm_gain(n):
                g = row(f"ln_g{n}")
                for h in range(TB):
                    ins = dve.tensor_tensor(X[:, h, :], X[:, h, :], g, ALU.mult)
                row_done(ins, f"ln_g{n}")

            def norm_bias(n):
                b = row(f"ln_b{n}")
                for h in range(TB):
                    ins = dve.tensor_tensor(X[:, h, :], X[:, h, :], b, ALU.add)
                row_done(ins, f"ln_b{n}")

            sq = tiny(92, 4).rearrange("p (h e) -> p h e", h=TB)

            def squares(h, e):
                c = slice(e * BANK, (e + 1) * BANK)
                link(dve.tensor_tensor_reduce(Xn[:, h, c], X[:, h, c], X[:, h, c], 1.0, 0.0, ALU.mult, ALU.add,
                                              sq[:, h, e:e + 1]))

            def mean_square(n):
                link(dve.tensor_tensor(rms_m[n % 2], sq[:, :, 0], sq[:, :, 1], ALU.add))
                dve.tensor_scalar(rms_m[n % 2], rms_m[n % 2], 1.0 / D, RMS_EPS, ALU.mult, ALU.add).then_inc(rms_ms, 1)
                dve.wait_ge(rms_root, n + 1)

            def normalise(n, name):
                mean_square(n)
                dve.reciprocal(rms_i[n % 2], rms_r[n % 2]).then_inc(nm_inv, 1)
                dve.wait_ge(nm_inv, n + 1)
                dve.tensor_scalar(Xn[:, 0, :], X[:, 0, :], rms_i[n % 2][:, 0:1], None, ALU.mult).then_inc(tr_src, 1)

            def transposes(name, dst, gain_name=None):
                n = TRANS_AT[name]
                for b in (2, 3):
                    dve.wait_ge(tr_pe, 4 * n + b + 1)
                    if gain_name:
                        for k in (2 * b, 2 * b + 1):
                            ins = dve.tensor_scalar(dst[:, k, :], bank[4 + b][:, (k % 2) * SEQ:(k % 2 + 1) * SEQ],
                                                    gain(gain_name, k), None, ALU.mult)
                    else:
                        ins = dve.tensor_copy(dst[:, 2 * b:2 * b + 2, :], pair_of(bank[4 + b]))
                    ins.then_inc(tr_dve, 1)

            cur = Cursor()

            def skip(n):
                for _ in range(n):
                    cur.take()

            def split(n, x, hi, i=None):
                slot, _, _ = cur.take()
                x += SPLIT_AT[n if isinstance(n, str) else f"ffn{n}"] + 1
                dve.wait_ge(sp_hi, x if i is None else i * 6 + x)
                dve.tensor_tensor(ring_r[:, slot, :], ring[:, slot, :], f32(hi), ALU.subtract).then_inc(sp_lo, 1)

            def split_units(name, hi_units):
                for x in range(1, PROJ_N[name] * 2):
                    split(name, x, hi_units(x % 2))

            def operand_lo(name, g=None):
                dve.wait_ge(tr_act, 2 * TRANS_AT[name] + 2)
                dve.wait_ge(tr_dve, 2 * TRANS_AT[name] + 2)
                for k in range(KC):
                    ins = dve.scalar_tensor_tensor(out=x_lo(k), in0=bank[4 + k // 2][:, k % 2 * SEQ:(k % 2 + 1) * SEQ],
                                                   scalar=gain(g, k) if g else 1.0, in1=f32(xt_r[:, k, :]), op0=ALU.mult, op1=ALU.subtract)
                    if k % 4 == 3:
                        ins.then_inc(xs_lo, 1)

            def hidden(n, i):
                def v(c):
                    return c if i is None else i * 4 + c

                t = ff_silu_t[n % 2]
                dve.wait_ge(ff_silu, v(n + 1))
                dve.tensor_tensor(t, t, bank[4 + n % 4][:, SEQ:2 * SEQ], ALU.mult).then_inc(ff_m, 1)
                dve.wait_ge(ff_m, v(n + 1))
                dve.tensor_copy(ff_h_t[n % 4], t).then_inc(ff_hi, 1)
                dve.wait_ge(ff_hi, v(n + 1))
                dve.tensor_tensor(ff_lo_t[n % 4], t, f32(ff_h_t[n % 4]), ALU.subtract).then_inc(ff_h, 1)

            def slab(n, s, i=None):
                q = 2 * (NSLAB * n + s)
                if s:
                    split(n, down_unit(s - 1), hi_down(s - 1), i)
                if s + 1 < NSLAB:
                    split(n, gate_unit(s + 1), hi_gate(s + 1), i)
                hidden(q, i)
                if s + 1 < NSLAB:
                    split(n, gate_unit(s + 1) + 1, hi_up(s + 1), i)
                hidden(q + 1, i)

            def ffn_first(n):
                split(n, 0, hi_gate(0))
                split(n, 1, hi_up(0))

            def ffn(n):
                slab(n, 0)
                with cur.loop(dve, (NSLAB - 3) // 2, 6) as i:
                    slab(n, 1, i)
                    slab(n, 2, i)
                slab(n, NSLAB - 2)
                slab(n, NSLAB - 1)
                split(n, down_unit(NSLAB - 1), hi_down(NSLAB - 1))
                for h in range(TB):
                    for e in range(2):
                        dve.wait_ge(ff_down, 4 * n + 2 * h + e + 1)
                        x = X[:, h, e * BANK:(e + 1) * BANK]
                        dve.scalar_tensor_tensor(out=x, in0=bank[2 * h + e][:, :], scalar=0.5, in1=x,
                                                 op0=ALU.mult, op1=ALU.add).then_inc(ff_out, 1)
                        dve.wait_ge(ff_out, 4 * n + 2 * h + e + 1)
                        squares(h, e)

            def add_projection(name):
                first = PROJ_AT[name]
                for j in range(2):
                    for h in range(TB):
                        dve.wait_ge(pj_pe, PROJ_DONE[first + j] + h + 1)
                        x = X[:, h, j * BANK:(j + 1) * BANK]
                        dve.tensor_tensor(x, bank[2 * ((first + j) % 2) + h][:, :], x, ALU.add).then_inc(pj_dve, 1)
                        dve.wait_ge(pj_dve, PROJ_TAKES[first + j][1] - TB + h + 1)
                        squares(h, j)

            def rotate(buf, name):
                v = buf[:].rearrange("p t (h d) -> p t h d", d=HD)
                for h in range(TB):
                    x1, x2 = v[:, h, :, 0:HALF], v[:, h, :, HALF:ROT]
                    c = cst("cos", TB, HALF)[:, h, :].unsqueeze(1).to_broadcast([P, H, HALF])
                    s = cst("sin", TB, HALF)[:, h, :].unsqueeze(1).to_broadcast([P, H, HALF])
                    t = [small[:, 128 * j:128 * (j + 1)].rearrange("p (h d) -> p h d", h=H) for j in range(4)]
                    dve.tensor_tensor(t[0], x1, c, ALU.mult)
                    dve.tensor_tensor(t[1], x2, s, ALU.mult)
                    dve.tensor_tensor(t[2], x1, s, ALU.mult)
                    link(dve.tensor_tensor(t[3], x2, c, ALU.mult))
                    dve.tensor_tensor(x1, t[0], t[1], ALU.subtract)
                    ins = dve.tensor_tensor(x2, t[2], t[3], ALU.add)
                    if h == 0:
                        link(ins)
                ins.then_inc(tr_src, 1)
                dve.wait_ge(tr_src, TRANS_AT[name] + 1)

            def attention(n, mask, count=None, bias=False):
                g = H * n

                def gate_terms(h):
                    dve.tensor_scalar(aug_l(h)[0:112], aug_f[0:112], cst("aug_sel")[0:112, h:h + 1], None, ALU.mult)\
                       .then_inc(fx_aug, 1)

                if bias:
                    gate_terms(0)
                    gate_terms(1)
                for i in range(H + (4 if bias else 1)):
                    if i < H:
                        h = i
                        dve.wait_ge(at_s, g + h + 1)
                        if bias and h + 2 < H:
                            gate_terms(h + 2)
                        if h >= 3:
                            dve.wait_ge(at_t, g + h - 2)
                        for t in range(TB):
                            w = P * (t + 1)
                            ins = dve.tensor_tensor_reduce(PR[h % 3][:, t * SEQ:t * SEQ + w],
                                                           bank[h % 4][:, t * SEQ:t * SEQ + w],
                                                           mask[:, t, 0:w], 1.0, NEG, ALU.add, ALU.max,
                                                           at_max[h % 3][:, t:t + 1])
                        ins.then_inc(at_sm, 1)
                        dve.wait_ge(at_sm, g + h + 1)
                        dve.tensor_scalar(at_bias[h % 3], at_max[h % 3], -HD ** -0.5, None, ALU.mult).then_inc(at_nb, 1)
                    if 1 <= i <= H:
                        h = i - 1
                        dve.wait_ge(at_e, 2 * (g + h) + 2)
                        if count is not None:
                            for t in range(TB):
                                v = PR[h % 3][:, t * SEQ:t * SEQ + P * (t + 1)]
                                ins = dve.tensor_tensor_reduce(v, v, count[:, t, 0:P * (t + 1)], 1.0, 0.0, ALU.mult,
                                                               ALU.add, at_sum[h % 3][:, t:t + 1])
                            link(ins)
                        link(dve.reciprocal(at_inv[h % 3], at_sum[h % 3]))
                        for t in range(TB):
                            v = PR[h % 3][:, t * SEQ:t * SEQ + P * (t + 1)]
                            ins = dve.tensor_scalar(v, v, at_inv[h % 3][:, t:t + 1], None, ALU.mult)
                        ins.then_inc(at_p, 1)
                    if bias and i >= 4 and i % 2 == 1:
                        r = (i - 4) // 2
                        dve.wait_ge(at_pv, g + 2 * r + 2)
                        dve.tensor_tensor(OT[:, r, :], bank[6 + r % 2][:, 0:SEQ], fGT[:, r, :], ALU.mult)\
                           .then_inc(at_o, 1)

            def heads(buf, h):
                return buf[:, h, :].rearrange("p (h d) -> p h d", d=HD)

            def head_sums(src, h):
                return dve.tensor_reduce(hs_sum[:, h * H:(h + 1) * H], heads(src, h), AX.X, ALU.add)

            def per_head(t, h):
                return t[:, h * H:(h + 1) * H].unsqueeze(2).to_broadcast([P, H, HD])

            def head_norm(buf, g, n):
                for h in range(TB):
                    ins = dve.tensor_tensor(B[9][:, h, :], buf[:, h, :], buf[:, h, :], ALU.mult)
                link(ins)
                head_sums(B[9], 0)
                link(head_sums(B[9], 1))
                dve.tensor_scalar(hs_sum, hs_sum, 1.0 / HD, QK_EPS, ALU.mult, ALU.add).then_inc(rk_z, 1)
                dve.wait_ge(rk_f, n)
                link(dve.reciprocal(hs_inv, hs_root))
                for h in range(TB):
                    ins = dve.tensor_tensor(heads(buf, h), heads(buf, h), per_head(hs_inv, h), ALU.mult)
                link(ins)
                for h in range(TB):
                    ins = dve.tensor_tensor(heads(buf, h), heads(buf, h),
                                            g.unsqueeze(1).to_broadcast([P, H, HD]), ALU.mult)
                ins.then_inc(tr_src, 1)

            def route(l):
                def both(f):
                    f(0)
                    link(f(1))

                dve.wait_ge(rt_landed, 48 * (l + 1))
                dve.wait_ge(rt_pe, 2 * l + 1)
                dve.memset(rt_g8, NEG)
                both(lambda t: dve.tensor_tensor(rt_l[:, t, :], bank[t][:, 0:N_RT], rt_b, ALU.add))
                link(dve.tensor_copy(rt_g8[:, :, 0:N_GRP], rt_l[:, :, 0:N_GRP]))
                both(lambda t: dve.max(rt_gm[:, t, :], rt_g8[:, t, :]))
                dve.tensor_scalar(rt_nm[:, 0:2], rt_gm[:, :, 0], -1.0, None, ALU.mult).then_inc(rt_dve, 1)
                both(lambda t: dve.max_index(rt_idx[:, t, :], rt_gm[:, t, :], rt_g8[:, t, :]))
                link(dve.tensor_copy(rt_if, rt_idx))
                both(lambda t: dve.tensor_scalar(rt_ohg[:, t, :], cst("eight"), rt_if[:, t, 0:1], None, ALU.is_equal))
                both(lambda t: dve.tensor_scalar(rt_es[:, t, :], rt_l[:, t, N_GRP:N_GRP + N_PER], rt_ohg[:, t, 0:1],
                                                 None, ALU.mult))
                for g in range(1, N_GRP):
                    a = N_GRP + N_PER * g
                    both(lambda t: dve.scalar_tensor_tensor(out=rt_es[:, t, :], in0=rt_l[:, t, a:a + N_PER],
                                                            scalar=rt_ohg[:, t, g:g + 1], in1=rt_es[:, t, :],
                                                            op0=ALU.mult, op1=ALU.add))
                both(lambda t: dve.max(rt_em[:, t, :], rt_es[:, t, :]))
                dve.tensor_scalar(rt_nm[:, 2:4], rt_em[:, :, 0], -1.0, None, ALU.mult).then_inc(rt_dve, 1)
                both(lambda t: dve.max_index(rt_idx[:, t, :], rt_em[:, t, :], rt_es[:, t, :]))
                link(dve.tensor_copy(rt_if, rt_idx))
                both(lambda t: dve.tensor_scalar(rt_se[:, t, :], cst("eight"), rt_if[:, t, 0:1], None, ALU.is_equal))
                both(lambda t: dve.tensor_scalar(rt_t[:, t, :], cst("eight"), rt_if[:, t, 1:2], None, ALU.is_equal))
                link(dve.tensor_tensor(rt_se, rt_se, rt_t, ALU.add))
                for t in range(TB):
                    ins = dve.tensor_tensor(rt_sel[:, t, :].rearrange("p (g e) -> p g e", g=N_GRP),
                                            rt_ohg[:, t, 0:N_GRP].unsqueeze(2).to_broadcast([P, N_GRP, N_PER]),
                                            rt_se[:, t, :].unsqueeze(1).to_broadcast([P, N_GRP, N_PER]), ALU.mult)
                ins.then_inc(rt_dve, 1)
                dve.wait_ge(rt_act, 2 * l + 2)
                link(dve.tensor_scalar(rt_w1[:, 0:2], rt_e2[:, 0:2], 1.0, None, ALU.add))
                link(dve.tensor_tensor(rt_w1[:, 0:2], rt_w1[:, 0:2], rt_sum[:, 0:2], ALU.mult))
                link(dve.reciprocal(rt_w1[:, 0:2], rt_w1[:, 0:2]))
                link(dve.tensor_tensor(rt_w1[:, 2:4], rt_w1[:, 0:2], rt_e2[:, 0:2], ALU.mult))
                both(lambda t: dve.tensor_scalar(rt_ge[:, t, :], cst("eight"), rt_if[:, t, 0:1], rt_w1[:, t:t + 1],
                                                 ALU.is_equal, ALU.mult))
                both(lambda t: dve.tensor_scalar(rt_t[:, t, :], cst("eight"), rt_if[:, t, 1:2], rt_w1[:, 2 + t:3 + t],
                                                 ALU.is_equal, ALU.mult))
                link(dve.tensor_tensor(rt_ge, rt_ge, rt_t, ALU.add))
                both(lambda t: dve.tensor_tensor(rt_gate[:, t, :].rearrange("p (g e) -> p g e", g=N_GRP),
                                                 rt_ohg[:, t, 0:N_GRP].unsqueeze(2).to_broadcast([P, N_GRP, N_PER]),
                                                 rt_ge[:, t, :].unsqueeze(1).to_broadcast([P, N_GRP, N_PER]), ALU.mult))
                dve.wait_ge(rt_pe, 2 * l + 2)
                both(lambda t: dve.tensor_tensor(rt_rank[:, t, :], bank[2][:, t * N_EXP:(t + 1) * N_EXP],
                                                 rt_sel[:, t, :], ALU.mult))
                dve.tensor_reduce(rt_cnt[0:1, 0:1], bank[2][0:1, 2 * N_EXP:3 * N_EXP], AX.X, ALU.max)
                link(dve.tensor_scalar(rt_rank, rt_rank, -1.0, None, ALU.add))
                dve.tensor_scalar(ov_flag[l][0:1, :], rt_cnt[0:1, 0:1], CAP + 0.5, None, ALU.is_gt).then_inc(ov_known, 1)

            def moe(l):
                norm_gain(2 * l)
                transposes(f"moe{l}", xt)
                norm_bias(2 * l)
                route(l)
                link(dve.memset(Yacc[:], 0.0))

                def matrix(dst, t, e, first, gates):
                    r = rt_rank[:, t, bass.ds(first + e, 1)]
                    g = rt_gate[:, t, bass.ds(first + e, 1)] if gates else None
                    return dve.tensor_scalar(dst[:, t, 64 * e:64 * e + 64], cst("slots"), r, g, ALU.is_equal,
                                             ALU.mult if gates else ALU.bypass)

                def pack(p):
                    for t in range(TB):
                        for e in range(2):
                            ins = matrix(m_pack, t, e, p * 2, False)
                    ins.then_inc(mo_sel, 1)

                def take_packed(v):
                    dve.wait_ge(mo_x, v)
                    dve.tensor_copy(XeT[:, 4:8, :].rearrange("p k s -> p (k s)"), bank[5][:, :]).then_inc(mo_xd, 1)

                def add_blocks(wait):
                    for t in range(TB):
                        for e in range(2):
                            dve.wait_ge(mo_s, wait(2 * t + e + 1))
                            y = Yacc[:, t, e * BANK:(e + 1) * BANK]
                            dve.tensor_tensor(y, bank[4 + 2 * t + e][:, :], y, ALU.add).then_inc(mo_acc, 1)

                def pair(n, p, i=None, first=False, last=False):
                    def at(per, c):
                        return per * n + c if i is None else i * per + (per * n + c)

                    if not last:
                        dve.wait_ge(mo_x, at(2, 2))
                        pack(p + 1)
                    if not first:
                        dve.wait_ge(mo_gt, at(1, 0))
                    for t in range(TB):
                        for e in range(2):
                            ins = matrix(m_gate, t, e, p * 2, True)
                    ins.then_inc(mo_g, 1)
                    dve.wait_ge(mo_silu, at(1, 1))
                    dve.wait_ge(mo_gu, at(2, 2))
                    dve.tensor_tensor(m_h, m_sg, bank[1][:, :], ALU.mult).then_inc(mo_h, 1)
                    if not first:
                        if i is not None or n % PAIRS > 1:
                            dve.wait_ge(mo_acc, at(4, -4))
                        add_blocks(lambda c: at(4, c - 4))
                    if not last:
                        take_packed(at(2, 4))

                n = PAIRS * l
                pack(0)
                take_packed(2 * n + 2)
                pair(n, 0, first=True)
                with dve.Fori(0, PAIRS - 2) as i:
                    pair(n + 1, i + 1, i)
                pair(n + PAIRS - 1, PAIRS - 1, last=True)
                dve.wait_ge(mo_acc, 4 * (n + PAIRS - 1))
                add_blocks(lambda c: 4 * (n + PAIRS - 1) + c)
                dve.wait_ge(mo_acc, 4 * (n + PAIRS))
                with overflowed(dve, l):
                    dve.scalar_tensor_tensor(out=rt_gate, in0=rt_rank, scalar=CAP - 0.5, in1=rt_gate,
                                             op0=ALU.is_gt, op1=ALU.mult).then_inc(ov_step[l], 1)
                    dve.wait_ge(ov_step[l], 1)
                    with dve.Fori(0, N_EXP) as i:
                        for t in range(TB):
                            dve.wait_ge(ov_silu[l], i * 2 + (t + 1))
                            dve.tensor_tensor(ov_h[t], ov_h[t], bank[2 * t + 1][:, :], ALU.mult).then_inc(ov_act[l], 1)
                        for t in range(TB):
                            dve.wait_ge(ov_y[l], i * 2 + (t + 1))
                            for j in range(2):
                                y = Yacc[:, t, j * BANK:(j + 1) * BANK]
                                ins = dve.scalar_tensor_tensor(out=y, in0=bank[6 + j][:, :],
                                                               scalar=rt_gate[:, t, bass.ds(i, 1)], in1=y,
                                                               op0=ALU.mult, op1=ALU.add)
                            ins.then_inc(ov_acc[l], 1)
                            dve.wait_ge(ov_acc[l], i * 2 + (t + 1))
                        dve.sem_inc(ov_step[l], 1)
                    dve.wait_ge(ov_step[l], N_EXP + 1)

            for h in range(TB):
                dve.wait_ge(x_landed[h], 16)
                for e in range(2):
                    squares(h, e)
            normalise(0, "ffn0")
            dve.wait_ge(in_landed, 48)
            transposes("ffn0", xt_r, "ffn1_0")
            operand_lo("ffn0", "ffn1_0")
            ffn_first(0)
            ffn(0)
            dve.wait_ge(const_landed, 16)
            normalise(1, "mix_a")
            split("qkv_a", 0, hi_proj(0))
            transposes("mix_a", xt_r, "mix_0")
            operand_lo("mix_a", "mix_0")
            split_units("qkv_a", hi_proj)
            wait_taken(dve, PROJ_AT["qkv_a"] + 1)
            rotate(Q, "q_a")
            wait_taken(dve, PROJ_AT["qkv_a"] + 3)
            rotate(K, "k_a")
            transposes("q_a", QT)
            transposes("k_a", KT)
            attention(0, cst("mask_dilated", TB, SEQ), cst("count_dilated", TB, SEQ))
            skip(4)
            ffn_first(1)
            add_projection("wo_a")
            normalise(2, "ffn1")
            transposes("ffn1", xt_r, "ffn2_0")
            operand_lo("ffn1", "ffn2_0")
            ffn(1)
            normalise(3, "kv")
            split("kv_b", 0, hi_proj(0))
            transposes("kv", xt_r, "kv")
            operand_lo("kv", "kv")
            split_units("kv_b", hi_proj)
            wait_taken(dve, PROJ_AT["kv_b"] + 1)
            rotate(K, "k_b")
            transposes("k_b", KT)
            normalise(4, "ffn2")
            ffn_first(2)
            transposes("ffn2", xt_r, "ffn1_1")
            operand_lo("ffn2", "ffn1_1")
            ffn(2)
            normalise(5, "mix_b")
            split("q_b", 0, hi_proj(0))
            transposes("mix_b", xt_r, "mix_1")
            operand_lo("mix_b", "mix_1")
            split_units("q_b", hi_proj)
            wait_taken(dve, PROJ_AT["q_b"] + 1)
            rotate(Q, "q_b")
            transposes("q_b", QT)
            attention(1, cst("mask_causal", TB, SEQ))
            skip(4)
            ffn_first(3)
            add_projection("wo_b")
            normalise(6, "ffn3")
            transposes("ffn3", xt_r, "ffn2_1")
            operand_lo("ffn3", "ffn2_1")
            ffn(3)
            mean_square(7)
            link(dve.reciprocal(rms_i[1], rms_r[1]))
            dve.wait_ge(m0_mixed, 2)
            sc, sh = row("sc_m0"), row("sh_m0")
            for h in range(TB):
                ins = dve.scalar_tensor_tensor(out=Xn[:, h, :], in0=X[:, h, :], scalar=rms_i[1][:, h:h + 1],
                                               in1=sc, op0=ALU.mult, op1=ALU.mult)
            row_done(ins, "sc_m0")
            for h in range(TB):
                ins = dve.tensor_tensor(Xn[:, h, :], Xn[:, h, :], sh, ALU.add)
            ins.then_inc(tr_src, 1)
            dve.wait_ge(tr_src, TRANS_AT["mix_r"] + 1)
            dve.sem_inc(row_free[ROWS.index("sh_m0") % NROW], 1)
            g = row("final_norm")
            for h in range(TB):
                ins = dve.scalar_tensor_tensor(out=X[:, h, :], in0=X[:, h, :], scalar=rms_i[1][:, h:h + 1],
                                               in1=g, op0=ALU.mult, op1=ALU.mult)
            row_done(ins, "final_norm")
            transposes("mix_r", xt)
            dve.wait_ge(tr_act, 2 * TRANS_AT["mix_r"] + 2)
            dve.wait_ge(tr_dve, 2 * TRANS_AT["mix_r"] + 2)
            dve.tensor_tensor(xxT[:, :, 1:SEQ], xt[:, :, 0:SEQ - 1], xt[:, :, 1:SEQ], ALU.subtract)
            link(dve.tensor_scalar(xxT[:, :, 0:1], xt[:, :, 0:1], -1.0, None, ALU.mult))
            dve.wait_ge(mod_out[0], 16 * (len(MODS) // 2 + 1))
            for n, m in enumerate((0, 2, 3, 1, 4, 5)):
                if 2 <= n < 5:
                    dve.wait_ge(pj_pe, PROJ_DONE[PROJ_AT[("rwkv_k", "rwkv_v", "lora_w")[n - 2]]])
                if n == 5:
                    dve.wait_ge(lo_pe, 1)
                for k in range(KC):
                    ins = dve.scalar_tensor_tensor(out=xi[n % 2][:, k, :], in0=xxT[:, k, :], scalar=gain(f"mu{m}", k),
                                                   in1=xt[:, k, :], op0=ALU.mult, op1=ALU.add)
                ins.then_inc(xi_set, 1)

            def add_row(proj, dst, name):
                w = row(name)
                for j in range(2):
                    b = PROJ_AT[proj] + j
                    for h in range(TB):
                        dve.wait_ge(pj_pe, PROJ_DONE[b] + h + 1)
                        c = slice(j * BANK, (j + 1) * BANK)
                        ins = dve.tensor_tensor(dst[:, h, c], bank[2 * (b % 2) + h][:, :], w[:, c], ALU.add)
                        ins.then_inc(pj_dve, 1)
                wait_taken(dve, PROJ_AT[proj] + 1)

            add_row("lora_w", rS, "w0")
            dve.engine_nop().then_inc(row_free[ROWS.index("w0") % NROW], 1)
            dve.engine_nop().then_inc(rk_z, 1)
            add_row("lora_a", rA, "a0")
            dve.engine_nop().then_inc(row_free[ROWS.index("a0") % NROW], 1)
            dve.engine_nop().then_inc(rk_z, 1)

            wait_taken(dve, PROJ_AT["rwkv_v"] + 1)
            w = row("k_k")
            for h in range(TB):
                ins = dve.tensor_tensor(rKK[:, h, :], rK[:, h, :], w, ALU.mult)
            row_done(ins, "k_k")
            for h in range(TB):
                if h == 0:
                    dve.wait_ge(lo_pe, 4)
                ins = dve.tensor_tensor(B[9][:, h, :], rKK[:, h, :], rKK[:, h, :], ALU.mult)
            link(ins)
            head_sums(B[9], 0)
            head_sums(B[9], 1).then_inc(rk_z, 1)
            dve.wait_ge(rk_f, 3)
            link(dve.tensor_scalar(hs_root, hs_root, 1e-12, None, ALU.max))
            link(dve.reciprocal(hs_inv, hs_root))
            for h in range(TB):
                ins = dve.tensor_tensor(heads(rKK, h), heads(rKK, h), per_head(hs_inv, h), ALU.mult)
            link(ins)
            w = row("k_a")
            for h in range(TB):
                ins = dve.scalar_tensor_tensor(out=B[9][:, h, :], in0=rA[:, h, :], scalar=-1.0, in1=w,
                                               op0=ALU.add, op1=ALU.mult)
            row_done(ins, "k_a")
            for h in range(TB):
                ins = dve.scalar_tensor_tensor(out=rK[:, h, :], in0=B[9][:, h, :], scalar=1.0, in1=rK[:, h, :],
                                               op0=ALU.add, op1=ALU.mult)
            link(ins)
            for h in range(TB):
                ins = dve.tensor_tensor(B[9][:, h, :], rR[:, h, :], rK[:, h, :], ALU.mult)
            link(ins)
            w = row("r_k")
            for h in range(TB):
                ins = dve.tensor_tensor(B[9][:, h, :], B[9][:, h, :], w, ALU.mult)
            row_done(ins, "r_k")
            for h in range(TB):
                ins = dve.tensor_reduce(bonus[:, h * H:(h + 1) * H], heads(B[9], h), AX.X, ALU.add)
            link(ins)
            for h in range(TB):
                ins = dve.tensor_tensor(rA[:, h, :], rA[:, h, :], rKK[:, h, :], ALU.mult)
            link(ins)
            dve.memset(Z[:], 0.0)
            for h in range(TB):
                dve.wait_ge(rk_f, 8 + 4 * h)
                for j in range(2):
                    c = slice(j * BANK, (j + 1) * BANK)
                    ins = dve.scalar_tensor_tensor(out=B[9][:, h, c], in0=rS[:, h, c], scalar=DECAY,
                                                   in1=bank[2 * h + j][:, :], op0=ALU.mult, op1=ALU.add)
                ins.then_inc(rk_z, 1)
            for h in range(TB):
                dve.tensor_tensor(rR[:, h, :], rR[:, h, :], rE[0][:, h, :], ALU.mult)
                dve.tensor_tensor(rK[:, h, :], rK[:, h, :], rE[1][:, h, :], ALU.mult)
                dve.tensor_tensor(rA[:, h, :], rA[:, h, :], rE[1][:, h, :], ALU.mult)
                dve.wait_ge(rk_f, 13 + h)
                dve.scalar_tensor_tensor(out=rKK[:, h, :], in0=rKK[:, h, :], scalar=-1.0, in1=rE[2][:, h, :],
                                         op0=ALU.mult, op1=ALU.mult).then_inc(rk_in, 1)

            def rkb(g, x):
                return bank[4 * (g % 2) + x]

            def sig(ins, g):
                ins.then_inc(rk_dve[g % 2], 1)

            def masked(g, tile, src, mask, x0):
                for par in range(2):
                    v = src(rkb(g, x0 + par))
                    ins = dve.tensor_tensor(rk_t[g % 2][tile][:, par * SEQ:(par + 1) * SEQ]
                                            .rearrange("p (a s) -> p a s", a=2), v,
                                            cst(mask).unsqueeze(1).to_broadcast([P, 2, P]), ALU.mult)
                return ins

            def low(b):
                return b[:, 0:SEQ].rearrange("p (a s) -> p a s", a=2)

            def side(x):
                return lambda b: b[:, :].rearrange("p (a x s) -> p a x s", a=2, x=2)[:, :, x, :]

            def v_de(g):
                rk_wait(dve, "pe", g, "ab")
                masked(g, 0, low, "sub_lower", 0)
                sig(masked(g, 2, low, "off_lower", 0), g)

            def v_dtm(g):
                rk_wait(dve, "pe", g, "abt")
                masked(g, 1, side(0), "sub_upper", 2)
                sig(masked(g, 8, side(1), "chunk_upto", 2), g)

            def v_mk(g):
                rk_wait(dve, "pe", g, "k")
                masked(g, 5, side(0), "chunk_upper", 0)
                sig(masked(g, 6, side(1), "chunk_upto", 0), g)

            def v_copy(name, tile, x):
                def step(g):
                    rk_wait(dve, "pe", g, name)
                    sig(dve.tensor_copy(rk_t[g % 2][tile], rkb(g, x)[:, :]), g)
                return step

            def plus_one(g, dst, src):
                sig(dve.tensor_tensor(dst.rearrange("p (a s) -> p a s", a=4), src.rearrange("p (a s) -> p a s", a=4),
                                      ident.unsqueeze(1).to_broadcast([P, 4, P]), ALU.add), g)

            def v_one(tile, pe_name, own):
                def step(g):
                    rk_wait(dve, "pe", g, pe_name)
                    if own:
                        rk_wait(dve, "dve", g, own)
                    else:
                        rk_wait(dve, "act", g, "ft")
                    plus_one(g, rk_t[g % 2][tile], rk_t[g % 2][tile])
                return step

            def v_from(name, tile, x):
                def step(g):
                    rk_wait(dve, "pe", g, name)
                    plus_one(g, rk_t[g % 2][tile], rkb(g, x)[:, :])
                return step

            def v_w1(g):
                rk_wait(dve, "pe", g, "w1")
                sig(dve.tensor_copy(rk_t[g % 2][6][:, SEQ:2 * SEQ], rkb(g, 3)[:, 0:SEQ]), g)

            def v_u(c):
                def step(g):
                    rk_wait(dve, "pe", g, f"u_{c}")
                    rk_wait(dve, "act", g, "u0")
                    t = slice(CH * c, CH * c + CH)
                    for par in range(2):
                        cc = slice(2 * HD * par, 2 * HD * (par + 1))
                        dve.tensor_tensor(rk_t[g % 2][5][t, cc], rkb(g, par)[t, 0:P], rk_t[g % 2][6][t, cc], ALU.add)
                        y = rk_cols(rR, g, par)[t]
                        ins = dve.tensor_tensor(y, rkb(g, par)[t, P:2 * P].rearrange("p (a d) -> p a d", a=2), y, ALU.add)
                    sig(ins, g)
                return step

            def v_z(c):
                def step(g):
                    rk_wait(dve, "pe", g, f"z_{c}")
                    r = slice(2 * (g % 4), 2 * (g % 4) + 2)
                    z = Z[:, r, :]
                    link(dve.tensor_tensor(z, rkb(g, 2)[:, 0:P].rearrange("p (a d) -> p a d", a=2), z, ALU.add))
                    n = 2 * (g // 4) + c
                    sig(dve.tensor_tensor(z, z, pct[:, r, n:n + 1].to_broadcast([P, 2, HD]), ALU.mult), g)
                return step

            def v_yb(g):
                rk_wait(dve, "pe", g, "yb")
                rk_wait(dve, "dve", g, "u_1")
                for par in range(2):
                    y = rk_cols(rR, g, par)
                    v = rkb(g, 3)[:, 2 * HD * par:2 * HD * (par + 1)].rearrange("p (a d) -> p a d", a=2)
                    ins = dve.tensor_tensor(y, v, y, ALU.add)
                sig(ins, g)

            for duo in range(4):
                if duo % 2 == 0:
                    dve.wait_ge(rk_in, TB)
                    for b in range(4):
                        dve.wait_ge(wt_pe, 8 * (duo // 2) + 4 + b + 1)
                        dve.tensor_copy(BK[:, 2 * b:2 * b + 2, :, :].rearrange("p r x t -> p (r x t)"),
                                        bank[4 + b][:, :]).then_inc(wt_dve, 1)
                for step in (v_de, v_dtm, v_mk, v_copy("d2", 3, 0), v_one(1, "d2t", "dtm"), v_copy("d4t", 6, 1),
                             v_one(3, "d4t", "d2"), v_from("d8", 7, 3), v_one(6, "d8", "d4t"), v_copy("at", 0, 0),
                             v_copy("t16t", 5, 2), v_copy("f", 1, 0), v_from("f2", 0, 2), v_one(3, "f2", None),
                             v_copy("tt", 2, 1), v_w1, v_u(0), v_z(0), v_u(1), v_z(1), v_yb):
                    for g in (2 * duo, 2 * duo + 1):
                        step(g)
            h, c, n = quarter(3)
            y, hs = rR[:, h, c], slice(n, n + 8)
            for g in (6, 7):
                rk_wait(dve, "dve", g, "yb")
            dve.wait_ge(gn_done, 1)
            link(dve.tensor_reduce(hs_sum[:, hs], eight(y), AX.X, ALU.add))
            link(dve.scalar_tensor_tensor(out=eight(y), in0=spread(hs_sum, n), scalar=-1.0 / HD, in1=eight(y),
                                          op0=ALU.mult, op1=ALU.add))
            link(dve.tensor_tensor(gn_t[0], y, y, ALU.mult))
            link(dve.tensor_reduce(hs_sum[:, hs], eight(gn_t[0]), AX.X, ALU.add))
            dve.tensor_scalar(hs_sum[:, hs], hs_sum[:, hs], 1.0 / HD, GN_EPS, ALU.mult, ALU.add).then_inc(gn_var, 1)
            dve.wait_ge(gn_root, 1)
            link(dve.reciprocal(hs_inv[:, hs], hs_root[:, hs]))
            link(dve.tensor_tensor(eight(y), eight(y), spread(hs_inv, n), ALU.mult))
            link(dve.tensor_tensor(y, y, rG[:, h, c], ALU.mult))
            dve.tensor_tensor(y, y, gn_t[1], ALU.add).then_inc(tr_src, 1)
            transposes("y_r", xt)

            layer_norm(0, "m0", B[1], proj="wo_r", mod="f0", trans="moe0")
            moe(0)
            layer_norm(1, "f0", Yacc, mod="kv", trans="kv_f")
            norm_gain(1)
            cur.skip_second_trunk()
            split("kv_f", 0, hi_proj(0))
            transposes("kv_f", xt_r)
            operand_lo("kv_f")
            split_units("kv_f", hi_proj)
            norm_bias(1)
            modulate("m1")
            dve.wait_ge(fx_landed, 64)
            b = PROJ_AT["forget"]
            for h in range(TB):
                dve.wait_ge(pj_pe, PROJ_DONE[b] + h + 1)
                dve.tensor_tensor(fx_z[0][:, h, :], bank[2 * (b % 2) + h][:, 0:H], fx_b, ALU.add).then_inc(pj_dve, 1)
            wait_taken(dve, b)
            link(dve.tensor_scalar(fx_z[1], fx_z[0], -1.0, None, ALU.mult))
            dve.tensor_tensor(fx_z[1], fx_z[0], fx_z[1], ALU.max).then_inc(fx_z1, 1)
            transposes("mix_f", xt_r)
            operand_lo("mix_f")
            split("qg_f", 0, hi_proj(0))
            split("qg_f", 1, hi_proj(1))
            link(dve.memset(fx_ls, 0.0))
            dve.wait_ge(fx_act, 2)
            for x in range(4):
                n = 16 if x == 3 else 32
                ins = dve.scalar_tensor_tensor(out=fx_ls[:, :, 32 * x:32 * x + 16], in0=fx_z[0], scalar=0.0, in1=fx_z[1],
                                               op0=ALU.min, op1=ALU.subtract)
            ins.then_inc(fx_z1, 1)
            wait_taken(dve, PROJ_AT["kv_f"] + 1)
            head_norm(fK, fx_kn, 15)
            for x in range(2, 6):
                split("qg_f", x, hi_proj(x % 2))
            wait_taken(dve, PROJ_AT["qg_f"] + 1)
            head_norm(fQ, fx_qn, 16)
            for x in range(6, 8):
                split("qg_f", x, hi_proj(x % 2))
            dve.wait_ge(fx_act, 3)
            dve.engine_nop().then_inc(tr_src, 1)
            transposes("k_f", KT)
            dve.wait_ge(fx_pe, 1)
            f = bank[2][0:112, 0:SEQ]
            dve.tensor_scalar(aug_f[0:112], f, cst("aug_val")[0:112], cst("aug_one")[0:112], ALU.mult, ALU.add)
            link(dve.tensor_scalar(aug_r[0:112], f, cst("aug_one")[0:112], -1.0, ALU.mult, ALU.mult))
            dve.tensor_scalar(aug_r[0:112], aug_r[0:112], cst("aug_val")[0:112], None, ALU.add).then_inc(fx_z1, 1)
            transposes("q_f", QT)
            transposes("g_f", fGT)
            dve.wait_ge(fx_z1, 3)
            attention(2, cst("mask_causal", TB, SEQ), bias=True)
            layer_norm(2, "m1", B[1], proj="wo_f", mod="f1", trans="moe1")
            moe(1)
            layer_norm(3, "f1", Yacc)
            norm_gain(3)
            norm_bias(3)
            dve.engine_nop().then_inc(x_final, 1)

        @block.gpsimd
        def _(pool):
            def mod_columns(r):
                w, b = [(A["ada_w_2"][0], A["ada_b_2"][0]), (A["kv_ada_w_2"], A["kv_ada_b_2"]),
                        (A["ada_w_2"][1], A["ada_b_2"][1])][(0, 0, 0, 1, 2, 2, 2)[r]]
                c0 = MODW * (0, 1, 2, 0, 0, 1, 2)[r]
                v = w[:, c0:c0 + MODW].rearrange("(k p) (j n) -> j p k n", p=P, n=BANK)
                tile = mod_acc[r % 2]
                if r > 1:
                    pool.wait_ge(mod_out[r % 2], 16 * (r // 2))
                pool.memset(tile, 0.0).then_inc(mod_chain, 1)
                pool.wait_ge(mod_chain, 41 * r + 1)
                pool.dma_start(tile[0:1, :], b[c0:c0 + MODW].unsqueeze(0)).then_inc(mod_b, 16)
                pool.wait_ge(mod_b, 16 * (r + 1))

                def until(s, value):
                    pool.wait_ge(s, value)
                    pool.sem_inc(mod_seen, 1)

                with pool.Fori(0, MODW // BANK) as j:
                    for t in range(4):
                        pool.dma_start(mod_w[t].rearrange("p (k n) -> p k n", k=2), v[j, :, 2 * t:2 * t + 2])\
                            .then_inc(mod_landed[t], 16)
                    for t in range(4):
                        until(mod_landed[t], j * 16 + (64 * r + 16))
                        w = mod_w[t].rearrange("p (k n) -> p k n", k=2)
                        pool.tensor_tensor(w, w, cs[:, 2 * t:2 * t + 2].unsqueeze(2).to_broadcast([P, 2, BANK]),
                                           ALU.mult).then_inc(mod_chain, 1)
                        if t % 2:
                            until(mod_chain, j * 10 + (41 * r + (3 if t == 1 else 6)))
                            pool.tensor_tensor(mod_w[t - 1], mod_w[t - 1], mod_w[t], ALU.add).then_inc(mod_chain, 1)
                    until(mod_chain, j * 10 + (41 * r + 7))
                    pool.tensor_tensor(mod_w[0], mod_w[0], mod_w[2], ALU.add).then_inc(mod_chain, 1)
                    until(mod_chain, j * 10 + (41 * r + 8))
                    pool.tensor_tensor(mod_sum, mod_w[0][:, 0:BANK], mod_w[0][:, BANK:D], ALU.add).then_inc(mod_chain, 1)
                    pool.tensor_copy(mod_bias, tile[:, bass.ds(j * BANK, BANK)]).then_inc(mod_chain, 1)
                    until(mod_chain, j * 10 + (41 * r + 10))
                    acc = tile[:, bass.ds(j * BANK, BANK)]
                    pool.tensor_tensor(acc, mod_sum, mod_bias, ALU.add).then_inc(mod_chain, 1)
                    until(mod_chain, j * 10 + (41 * r + 11))
                pool.sem_inc(mod_done, 1)

            def group_norms():
                ch = Chain(pool, gn_chain)
                gn_g, gn_b = ROWS.index("gn_g"), ROWS.index("gn_b")
                tree = eight(gn_t[0])

                def sums(v, hs):
                    w = HD // 2
                    while w > 1:
                        ch.link(pool.tensor_tensor(tree[:, :, 0:w], v[:, :, 0:w], v[:, :, w:2 * w], ALU.add))
                        v, w = tree, w // 2
                    ch.link(pool.tensor_tensor(hs_sum[:, hs].unsqueeze(2), v[:, :, 0:1], v[:, :, 1:2], ALU.add))

                for i in (gn_g, gn_b):
                    pool.wait_ge(row_landed[i % NROW], 16 * (i // NROW + 1))
                pool.wait_ge(rk_in, TB)
                pool.wait_ge(lg_act, 4)
                for q in range(4):
                    h, c, n = quarter(q)
                    ch.link(pool.tensor_tensor(eight(gn_t[1]), eight(rV[:, h, c]), spread(bonus, n), ALU.mult))
                    ch.link(pool.tensor_tensor(gn_t[1], gn_t[1], bc[gn_b % NROW][:, c], ALU.add))
                    ch.link(pool.tensor_tensor(gn_t[1], gn_t[1], rG[:, h, c], ALU.mult))
                    ch.link(pool.tensor_tensor(rG[:, h, c], rG[:, h, c], bc[gn_g % NROW][:, c], ALU.mult))
                    if q == 3:
                        break
                    y, hs = rR[:, h, c], slice(n, n + 8)
                    for g in (2 * q, 2 * q + 1):
                        rk_wait(pool, "dve", g, "yb")
                    sums(eight(y), hs)
                    ch.link(pool.tensor_scalar(hs_sum[:, hs], hs_sum[:, hs], 1.0 / HD, None, ALU.mult))
                    ch.link(pool.tensor_tensor(eight(y), eight(y), spread(hs_sum, n), ALU.subtract))
                    ch.link(pool.tensor_tensor(gn_t[0], y, y, ALU.mult))
                    sums(eight(gn_t[0]), hs)
                    ch.link(pool.tensor_scalar(hs_sum[:, hs], hs_sum[:, hs], 1.0 / HD, GN_EPS, ALU.mult, ALU.add))
                    ch.link(pool.tensor_tensor(hs_inv[:, hs], hs_sum[:, hs],
                                               cst("minus_half").to_broadcast([P, 8]), ALU.pow))
                    ch.link(pool.tensor_tensor(eight(y), eight(y), spread(hs_inv, n), ALU.mult))
                    ch.link(pool.tensor_tensor(y, y, rG[:, h, c], ALU.mult))
                    ch.link(pool.tensor_tensor(y, y, gn_t[1], ALU.add))
                pool.sem_inc(gn_done, 1)
                pool.sem_inc(row_free[gn_g % NROW], 1)
                pool.sem_inc(row_free[gn_b % NROW], 1)

            def mix_rows(n, mod):
                names = f"ln_g{n}", f"ln_b{n}", "sc_" + mod, "sh_" + mod
                for x in names:
                    pool.wait_ge(row_landed[ROWS.index(x) % NROW], 16 * (ROWS.index(x) // NROW + 1))
                g, b, sc, sh = [bc[ROWS.index(x) % NROW] for x in names]
                ch = Chain(pool, mix_chain)
                ch.n = 4 * n
                ch.link(pool.tensor_scalar(sc, sc, 1.0, None, ALU.add))
                ch.link(pool.tensor_tensor(mix_t[:], sc, b, ALU.mult))
                ch.link(pool.tensor_tensor(sh, sh, mix_t[:], ALU.add))
                ch.link(pool.tensor_tensor(sc, sc, g, ALU.mult))
                pool.sem_inc(row_mixed, 1)

            for n, name in enumerate(ROWS):
                if n == 1:
                    pool.wait_ge(in_landed, 48)
                    pool.wait_ge(const_landed, 16)
                    pool.wait_ge(cs_set, 1)
                    for r in range(len(MODS) - 1):
                        mod_columns(r)
                if n == 4:
                    pool.wait_ge(mod_out[1], 16 * (len(MODS) // 2))
                if n == 6:
                    mod_columns(len(MODS) - 1)
                if name == "sc_f0":
                    group_norms()
                if name in MOD_ROWS:
                    r = MOD_ROWS[name] // MODW
                    pool.wait_ge(mod_out[r % 2], 16 * (r // 2 + 1))
                if n >= NROW:
                    pool.wait_ge(row_free[n % NROW], n // NROW)
                pool.dma_start(bc[n % NROW], row_source(name).partition_broadcast(P)).then_inc(row_landed[n % NROW], 16)
                if name == "sc_m0":
                    i = ROWS.index("final_norm")
                    pool.wait_ge(row_landed[i], 16)
                    pool.wait_ge(row_landed[n], 16)
                    pool.tensor_scalar(bc[n], bc[n], 1.0, None, ALU.add).then_inc(m0_mixed, 1)
                    pool.wait_ge(m0_mixed, 1)
                    pool.tensor_tensor(bc[n], bc[n], bc[i], ALU.mult).then_inc(m0_mixed, 1)
                if name in ("sc_f0", "sc_f1"):
                    l = int(name[4])
                    if l == 0:
                        pool.wait_ge(tr_src, TRANS_AT["y_r"] + 1)
                    mix_rows(2 * l, name[3:])
                    if l:
                        pool.wait_ge(at_o, H // 2 * 3)
                    pool.dma_start(rt_w[:, :, 0:N_GRP], A["moe_wgrp_2"][l].rearrange("(k p) n -> p k n", p=P))\
                        .then_inc(rt_landed, 16)
                    pool.dma_start(rt_w[:, :, N_GRP:N_RT], A["moe_wexp_2"][l].rearrange("(k p) n -> p k n", p=P))\
                        .then_inc(rt_landed, 16)
                    pool.dma_start(rt_b, A["rt_bias"][l].partition_broadcast(P)).then_inc(rt_landed, 16)
                if name == "sc_kv":
                    mix_rows(1, "kv")
                if name == "sc_f0":
                    pool.dma_start(fx_w, A["kv_w_2"][:, 2 * D:2 * D + H].rearrange("(k p) n -> p k n", p=P))\
                        .then_inc(fx_landed, 16)
                    for dst, src in ((fx_b, A["kv_fb_2"]), (fx_kn, A["kv_knorm_2"]), (fx_qn, A["fx_qnorm_2"][0])):
                        pool.dma_start(dst, src.partition_broadcast(P)).then_inc(fx_landed, 16)


_BIG = ["x", "ffn1_w_gate", "ffn1_w_up", "ffn1_w_down", "ffn2_w_gate", "ffn2_w_up", "ffn2_w_down", "a_w_qkv",
        "a_w_o", "kv_w", "b_w_q", "b_w_o", "final_norm"]


_BIG2 = ["ada_w_2", "ada_b_2", "ln_g_2", "ln_b_2", "rw_rkv_2", "rw_w0_2", "rw_w1_2", "rw_w2_2", "rw_a0_2", "rw_a1_2",
         "rw_a2_2", "rw_g1_2", "rw_g2_2", "rw_kk_2", "rw_ka_2", "rw_rk_2", "rw_gn_g_2", "rw_gn_b_2", "rw_wo_2",
         "kv_ada_w_2", "kv_ada_b_2", "kv_w_2", "kv_fb_2", "kv_knorm_2", "fx_wqg_2", "fx_qnorm_2", "fx_wo_2",
         "moe_wgrp_2", "moe_wexp_2", "moe_wgate_2", "moe_wup_2", "moe_wdown_2"]


def kernel(**inputs):
    from concourse import bacc
    from concourse.bass_utils import run_bass_kernel_spmd

    arrays = {n: np.ascontiguousarray(inputs[n]) for n in _BIG}
    arrays["x"] = arrays["x"].reshape(SEQ, D)
    for n in _BIG2:
        arrays[n] = np.ascontiguousarray(inputs[n])
    arrays["rt_bias"] = np.ascontiguousarray(
        np.concatenate([inputs["moe_bgrp_2"], inputs["moe_bexp_2"]], axis=1))
    arrays["c"] = np.ascontiguousarray(inputs["c_2"].reshape(KC, P).T)
    arrays["const"] = np.concatenate(list(CONST.values()), axis=1)

    def columns(v):
        return np.asarray(v).reshape(KC, P).T

    arrays["gains"] = np.ascontiguousarray(np.concatenate(
        [columns(inputs["ffn1_norm"][0]), columns(inputs["ffn1_norm"][1]), columns(inputs["mix_norm"][0]),
         columns(inputs["mix_norm"][1]), columns(inputs["ffn2_norm"][0]), columns(inputs["ffn2_norm"][1]),
         columns(inputs["kv_norm"])] + [columns(inputs["rw_mu_2"][0, i]) for i in range(6)], axis=1))
    nc = bacc.Bacc("TRN2", target_bir_lowering=False, num_devices=1)
    aps = {n: nc.dram_tensor(f"in_{n}", a.shape, F32, kind="ExternalInput").ap() for n, a in arrays.items()}
    out = nc.dram_tensor("out", (SEQ, D), F32, kind="ExternalOutput").ap()
    build(nc, aps, out)
    r = run_bass_kernel_spmd(nc, [{f"in_{n}": a for n, a in arrays.items()}], core_ids=[0])
    return r.results[0]["out"].reshape(1, SEQ, D)
```
